# Optimizing a Trainium2 kernel written in Bass

```python
import jax
import jax.numpy as jnp
from jax import lax
import numpy as np

D_MODEL = 1024
BATCH = 1
SEQ = 512
DEPTH = 2

CTX_LEN = 256
GRID_W = 64
EPS = 1e-6
ROPE_THETA = 10000.0
Q_BLOCK = 128
N_ATTN_LAYERS = (DEPTH + 1) // 2
N_FC_LAYERS = DEPTH // 2

MLA_HEADS = 4
MLA_Q_RANK = D_MODEL // 2
MLA_KV_RANK = D_MODEL // 4
MLA_NOPE = 128
MLA_ROPE = 64
MLA_V = 128
MLA_SCALE = (MLA_NOPE + MLA_ROPE) ** -0.5

GQA_HEADS = 4
GQA_KV_HEADS = 2
GQA_GROUP = GQA_HEADS // GQA_KV_HEADS
GQA_HEAD_DIM = 128
GQA_SCALE = GQA_HEAD_DIM ** -0.5

FNET_GROUPS = 4
FNET_GROUP_W = 128
FNET_W = FNET_GROUPS * FNET_GROUP_W
CONV_CH = 512
CONV_K = 31

D_FF = 4 * D_MODEL
N_MOD = 6

ATTN_Q_W = MLA_Q_RANK + GQA_HEADS * GQA_HEAD_DIM
ATTN_KV_W = MLA_KV_RANK + MLA_ROPE + 2 * GQA_KV_HEADS * GQA_HEAD_DIM
ATTN_IN_W = ATTN_Q_W + ATTN_KV_W
ATTN_MIX_W = MLA_HEADS * MLA_V + GQA_HEADS * GQA_HEAD_DIM
FC_IN_W = FNET_W + 2 * CONV_CH
FC_MIX_W = FNET_W + CONV_CH

kernel_name = 'hybrid_mla_gqa_fnet_conformer_dit_block'

def rms_norm(x, g):
    xf = x.astype(jnp.float32)
    y = xf * lax.rsqrt(jnp.mean(xf * xf, axis=-1, keepdims=True) + EPS)
    return (y * g.astype(jnp.float32)).astype(x.dtype)

def layer_norm(x, g, b):
    xf = x.astype(jnp.float32)
    mu = jnp.mean(xf, axis=-1, keepdims=True)
    var = jnp.mean(jnp.square(xf - mu), axis=-1, keepdims=True)
    y = (xf - mu) * lax.rsqrt(var + EPS)
    return (y * g.astype(jnp.float32) + b.astype(jnp.float32)).astype(x.dtype)

def adaln_params(cond, w, b):
    m = jax.nn.silu(cond) @ w + b
    return jnp.split(m[:, None, :], N_MOD, axis=-1)

def modulate(h, shift, scale):
    return h * (1 + scale) + shift

def rope_1d(x, pos):
    half = x.shape[-1] // 2
    freqs = ROPE_THETA ** (-jnp.arange(half, dtype=jnp.float32) / half)
    ang = pos.astype(jnp.float32)[:, None] * freqs[None, :]
    cos = jnp.cos(ang)[None, :, None, :]
    sin = jnp.sin(ang)[None, :, None, :]
    xf = x.astype(jnp.float32)
    x1, x2 = xf[..., :half], xf[..., half:]
    return jnp.concatenate([x1 * cos - x2 * sin, x1 * sin + x2 * cos], axis=-1).astype(x.dtype)

def rope_2d(x, pos):
    if pos is None:
        return x
    row, col = pos
    half = x.shape[-1] // 2
    return jnp.concatenate([rope_1d(x[..., :half], row), rope_1d(x[..., half:], col)], axis=-1)

def attention(q, k, v, scale):
    b, s, hkv, g, dk = q.shape
    nb = s // Q_BLOCK
    qb = jnp.moveaxis(q.reshape(b, nb, Q_BLOCK, hkv, g, dk), 1, 0)

    def block(qblk):
        sc = jnp.einsum('bqhgd,bthd->bhgqt', qblk, k).astype(jnp.float32) * scale
        p = jax.nn.softmax(sc, axis=-1).astype(v.dtype)
        return jnp.einsum('bhgqt,bthe->bqhge', p, v)

    o = lax.map(block, qb)
    return jnp.moveaxis(o, 0, 1).reshape(b, s, hkv * g * v.shape[-1])

def attn_queries(pq, q_norm_g, w_uq, qk_norm_g, pos):
    b, t, _ = pq.shape
    cq = rms_norm(pq[..., :MLA_Q_RANK], q_norm_g)
    q = (cq @ w_uq).reshape(b, t, MLA_HEADS, MLA_NOPE + MLA_ROPE)
    q_mla = jnp.concatenate([q[..., :MLA_NOPE], rope_2d(q[..., MLA_NOPE:], pos)], axis=-1)
    q_gqa = rope_2d(rms_norm(pq[..., MLA_Q_RANK:].reshape(b, t, GQA_HEADS, GQA_HEAD_DIM), qk_norm_g), pos)
    return (q_mla.reshape(b, t, MLA_HEADS, 1, MLA_NOPE + MLA_ROPE),
            q_gqa.reshape(b, t, GQA_KV_HEADS, GQA_GROUP, GQA_HEAD_DIM))

def attn_keys_values(pkv, kv_norm_g, w_ukv, k_norm_g, pos):
    b, t, _ = pkv.shape
    o1 = MLA_KV_RANK
    o2 = o1 + MLA_ROPE
    o3 = o2 + GQA_KV_HEADS * GQA_HEAD_DIM
    ckv = rms_norm(pkv[..., :o1], kv_norm_g)
    kv = (ckv @ w_ukv).reshape(b, t, MLA_HEADS, MLA_NOPE + MLA_V)
    k_rope = rope_2d(pkv[..., o1:o2].reshape(b, t, 1, MLA_ROPE), pos)
    k_mla = jnp.concatenate([kv[..., :MLA_NOPE], jnp.broadcast_to(k_rope, (b, t, MLA_HEADS, MLA_ROPE))], axis=-1)
    v_mla = kv[..., MLA_NOPE:]
    k_gqa = rope_2d(rms_norm(pkv[..., o2:o3].reshape(b, t, GQA_KV_HEADS, GQA_HEAD_DIM), k_norm_g), pos)
    v_gqa = pkv[..., o3:].reshape(b, t, GQA_KV_HEADS, GQA_HEAD_DIM)
    return (k_mla, v_mla, k_gqa, v_gqa)

def attn_mix(q, kv, w_out):
    q_mla, q_gqa = q
    k_mla, v_mla, k_gqa, v_gqa = kv
    o_mla = attention(q_mla, k_mla, v_mla, MLA_SCALE)
    o_gqa = attention(q_gqa, k_gqa, v_gqa, GQA_SCALE)
    return jnp.concatenate([o_mla, o_gqa], axis=-1) @ w_out

def fourier_conv_mix(h, w_in, conv_w, conv_b, ln_g, ln_b, w_out):
    b, t, _ = h.shape
    p = h @ w_in
    f = p[..., :FNET_W].reshape(b, t, FNET_GROUPS, FNET_GROUP_W).astype(jnp.float32)
    f = jnp.fft.fft2(f, axes=(1, 3), norm='ortho').real.astype(h.dtype).reshape(b, t, FNET_W)
    a, gate = jnp.split(p[..., FNET_W:], 2, axis=-1)
    u = a * jax.nn.sigmoid(gate)
    u = lax.conv_general_dilated(u, conv_w[:, None, :].astype(u.dtype), (1,), [(CONV_K // 2, CONV_K // 2)],
                                 dimension_numbers=('NWC', 'WIO', 'NWC'), feature_group_count=CONV_CH) + conv_b
    u = jax.nn.silu(layer_norm(u, ln_g, ln_b))
    return jnp.concatenate([f, u], axis=-1) @ w_out

def sq_relu_mlp(h, w1, w2):
    return jnp.square(jax.nn.relu(h @ w1)) @ w2

def setup_inputs(seed: int = 0) -> dict:
    key = jax.random.key(seed)
    ks = jax.random.split(key, 25)
    f32 = jnp.float32
    d = D_MODEL
    na, nf = N_ATTN_LAYERS, N_FC_LAYERS

    def nrm(k, shape, scale):
        return jax.random.normal(k, shape, f32) * scale

    def gain(k, shape):
        return 1.0 + 0.05 * jax.random.normal(k, shape, f32)

    return {
        'x': nrm(ks[0], (BATCH, SEQ, d), 1.0),
        'c': nrm(ks[1], (BATCH, d), 1.0),
        'ctx': nrm(ks[2], (BATCH, CTX_LEN, d), 1.0),
        'c_ctx': nrm(ks[3], (d,), 1.0),
        'mod_w': nrm(ks[4], (DEPTH, d, N_MOD * d), 0.5 * d ** -0.5),
        'mod_b': nrm(ks[5], (DEPTH, N_MOD * d), 0.02),
        'norm1_g': gain(ks[6], (DEPTH, d)),
        'norm2_g': gain(ks[7], (DEPTH, d)),
        'attn_w_in': nrm(ks[8], (na, d, ATTN_IN_W), d ** -0.5),
        'mla_q_norm_g': gain(ks[9], (na, MLA_Q_RANK)),
        'mla_w_uq': nrm(ks[10], (na, MLA_Q_RANK, MLA_HEADS * (MLA_NOPE + MLA_ROPE)), MLA_Q_RANK ** -0.5),
        'mla_kv_norm_g': gain(ks[11], (na, MLA_KV_RANK)),
        'mla_w_ukv': nrm(ks[12], (na, MLA_KV_RANK, MLA_HEADS * (MLA_NOPE + MLA_V)), MLA_KV_RANK ** -0.5),
        'gqa_q_norm_g': gain(ks[13], (na, GQA_HEAD_DIM)),
        'gqa_k_norm_g': gain(ks[14], (na, GQA_HEAD_DIM)),
        'attn_w_out': nrm(ks[15], (na, ATTN_MIX_W, d), ATTN_MIX_W ** -0.5),
        'fc_w_in': nrm(ks[16], (nf, d, FC_IN_W), d ** -0.5),
        'conv_w': nrm(ks[17], (nf, CONV_K, CONV_CH), CONV_K ** -0.5),
        'conv_b': nrm(ks[18], (nf, CONV_CH), 0.02),
        'conv_ln_g': gain(ks[19], (nf, CONV_CH)),
        'conv_ln_b': nrm(ks[20], (nf, CONV_CH), 0.02),
        'fc_w_out': nrm(ks[21], (nf, FC_MIX_W, d), FC_MIX_W ** -0.5),
        'mlp_w1': nrm(ks[22], (DEPTH, d, D_FF), d ** -0.5),
        'mlp_w2': nrm(ks[23], (DEPTH, D_FF, d), D_FF ** -0.5),
        'final_g': gain(ks[24], (d,)),
    }

def reference(x, c, ctx, c_ctx, mod_w, mod_b, norm1_g, norm2_g, attn_w_in, mla_q_norm_g, mla_w_uq,
              mla_kv_norm_g, mla_w_ukv, gqa_q_norm_g, gqa_k_norm_g, attn_w_out, fc_w_in, conv_w, conv_b,
              conv_ln_g, conv_ln_b, fc_w_out, mlp_w1, mlp_w2, final_g):
    s = x.shape[1]
    rows = s // GRID_W
    row = jnp.repeat(jnp.arange(rows, dtype=jnp.int32), GRID_W)
    col = jnp.tile(jnp.arange(GRID_W, dtype=jnp.int32), rows)
    pos = (row, col)
    last_attn = ((DEPTH - 1) // 2) * 2

    for i in range(DEPTH):
        ctx_mode = 'full' if i < last_attn else ('kv' if i == last_attn else 'none')
        j = i // 2
        sh1, sc1, g1, sh2, sc2, g2 = adaln_params(c, mod_w[i], mod_b[i])
        h = modulate(rms_norm(x, norm1_g[i]), sh1, sc1)
        if ctx_mode != 'none':
            csh1, csc1, cg1, csh2, csc2, cg2 = adaln_params(c_ctx[None, :], mod_w[i], mod_b[i])
            hc = modulate(rms_norm(ctx, norm1_g[i]), csh1, csc1)

        if i % 2 == 0:
            q_p = (mla_q_norm_g[j], mla_w_uq[j], gqa_q_norm_g[j])
            kv_p = (mla_kv_norm_g[j], mla_w_ukv[j], gqa_k_norm_g[j])
            w_in = attn_w_in[j]
            if ctx_mode == 'full':
                pc = hc @ w_in
                pqc, pkvc = pc[..., :ATTN_Q_W], pc[..., ATTN_Q_W:]
            else:
                pkvc = hc @ w_in[:, ATTN_Q_W:]
            kvc = attn_keys_values(pkvc, *kv_p, None)
            px = h @ w_in
            qx = attn_queries(px[..., :ATTN_Q_W], *q_p, pos)
            kvx = attn_keys_values(px[..., ATTN_Q_W:], *kv_p, pos)
            kv_all = tuple(jnp.concatenate([a, bb], axis=1) for a, bb in zip(kvc, kvx))
            x = x + g1 * attn_mix(qx, kv_all, attn_w_out[j])
            if ctx_mode == 'full':
                qc = attn_queries(pqc, *q_p, None)
                ctx = ctx + cg1 * attn_mix(qc, kvc, attn_w_out[j])
        else:
            fc_p = (fc_w_in[j], conv_w[j], conv_b[j], conv_ln_g[j], conv_ln_b[j], fc_w_out[j])
            x = x + g1 * fourier_conv_mix(h, *fc_p)
            if ctx_mode == 'full':
                ctx = ctx + cg1 * fourier_conv_mix(hc, *fc_p)

        x = x + g2 * sq_relu_mlp(modulate(rms_norm(x, norm2_g[i]), sh2, sc2), mlp_w1[i], mlp_w2[i])
        if ctx_mode == 'full':
            ctx = ctx + cg2 * sq_relu_mlp(modulate(rms_norm(ctx, norm2_g[i]), csh2, csc2), mlp_w1[i], mlp_w2[i])

    return rms_norm(x, final_g)


_drawn_inputs = setup_inputs


def setup_inputs(seed=0):
    import zlib

    import numpy as np

    out = dict(_drawn_inputs(seed))
    spreads = {}
    factors = {'ctx': 4.966,
     'norm1_g': 5.932,
     'mla_q_norm_g': 8.0,
     'mla_w_uq': 3.089,
     'mla_kv_norm_g': 8.0,
     'gqa_q_norm_g': 8.0,
     'gqa_k_norm_g': 8.0,
     'conv_b': 27.994,
     'conv_ln_g': 22.253,
     'conv_ln_b': 55.411,
     'norm2_g': 3.959}
    for name, (base, spread) in spreads.items():
        noise = np.random.default_rng([zlib.crc32(name.encode()), seed]).standard_normal(out[name].shape)
        drawn = base * np.exp(spread * noise) if base else spread * noise
        out[name] = jnp.asarray(drawn.astype(out[name].dtype))
    for name, factor in factors.items():
        out[name] = (out[name] * factor).astype(out[name].dtype)
    return out
```

```python
from contextlib import ExitStack

import numpy as np

import concourse.bass as bass
from concourse import mybir

ACT = mybir.ActivationFunctionType
ALU = mybir.AluOpType
AX = mybir.AxisListType
F32 = mybir.dt.float32
F32R = mybir.dt.float32r

P = 128
D = 1024
KD = D // P
SEQ, CTX = 512, 256
KEYS = CTX + SEQ
TX, TC = SEQ // P, CTX // P
TK = TX + TC
FF = 4 * D
GRID_W = 64
EPS = 1e-6
MLA_HEADS, NOPE, ROPE = 4, 128, 64
GQA_HEADS, GQA_KV, HD = 4, 2, 128
Q_RANK, KV_RANK = D // 2, D // 4
KQ, KKV = Q_RANK // P, KV_RANK // P
MLA_SCALE = float(NOPE + ROPE) ** -0.5
GQA_SCALE = float(HD) ** -0.5
HEADS = MLA_HEADS + GQA_HEADS
GROUPS, CH, TAPS = 4, 512, 31
KCH = CH // P
GATE_AT = 2 * CH
PAD = TAPS // 2

CHUNK = 1024
BLOCK = 512
FFG = 4
STAGES = 4
SLOTS = 2

VEC = {}
_at = 0
for _name, _n in (("n1", 2 * KD), ("n2", 2 * KD), ("nf", KD), ("modb", 2 * 6 * KD), ("qg", KQ), ("kvg", KKV),
                  ("gqg", 1), ("gkg", 1), ("convb", KCH), ("lng", KCH), ("lnb", KCH), ("convw", KCH * TAPS)):
    VEC[_name] = _at
    _at += _n
NVEC = _at
TAB = {"cosg": 0, "sing": 512, "cosm": 1024, "sinm": 1536, "ident": 2048, "rotg": 2176, "rotm": 2304}
NTAB = 2432

PROJ = ["ckv0", "ckv1", "kr", "kg0", "kg1", "v0", "v1", "cq0", "cq1", "cq2", "cq3", "gq0", "gq1", "gq2", "gq3"]
NPROJ = len(PROJ)
BOTH = 7
UQ0, UQ1, UQR, UKK, UKV = range(NPROJ, NPROJ + 5)
NW_IN = NPROJ + 5
NM0 = 32
N_IN, N_WOUT = 0, NW_IN + NM0
N_MLP0 = N_WOUT + KD
MLP_W, MLP_M = 16, 12
N_FC = N_MLP0 + FFG * (MLP_W + MLP_M)
NFI = 12
N_FCOUT = N_FC + NFI
N_MLP1 = N_FCOUT + KD
W_WOUT, W_MLP0 = NW_IN, NW_IN + KD
W_FC = W_MLP0 + FFG * MLP_W
W_FCOUT = W_FC + NFI
W_MLP1 = W_FCOUT + KD

FI = ["g0", "a0", "g1", "a1", "g2", "a2", "g3", "a3", "f0", "f1", "f2", "f3"]
ROTS = ["kr", "kg0", "kg1", "gq0", "gq1", "gq2", "gq3", "qr0", "qr1"]
EVENTS = [("x0", KD, TX, D, "x"), ("ctx0", KD, TC, D, "c"), ("ckv", KKV, TK, KV_RANK, "xc"),
          ("kg0", 1, TK, HD, "xc"), ("kg1", 1, TK, HD, "xc"), ("cq", KQ, TX, Q_RANK, ""),
          ("gq0", 1, TX, HD, ""), ("gq1", 1, TX, HD, ""), ("gq2", 1, TX, HD, ""), ("gq3", 1, TX, HD, ""),
          ("x1", KD, TX, D, "x"), ("x2", KD, TX, D, "x"), ("ln", KCH, TX, CH, "x"), ("x3", KD, TX, D, "x"),
          ("x4", KD, TX, D, "x")]
EV = {e[0]: i for i, e in enumerate(EVENTS)}
SQ0 = [sum(e[1] for e in EVENTS[:i]) for i in range(len(EVENTS) + 1)]
BC = [sum(bool(e[4]) for e in EVENTS[:i]) for i in range(len(EVENTS) + 1)]


def event_tiles(e):
    if EVENTS[e][4] == "x" or EVENTS[e][2] == TX:
        return [(5, t * P) for t in range(TX)]
    if EVENTS[e][4] == "c":
        return [(6, t * P) for t in range(TC)]
    return [(6, t * P) for t in range(TC)] + [(5, t * P) for t in range(TX)]


class Ledger:

    def __init__(self):
        self.uses, self.at = [0] * 8, {}

    def use(self, key, bank):
        self.uses[bank] += 1
        self.at[key] = (bank, self.uses[bank])


def plan_banks():
    led = Ledger()
    for b in range(4):
        led.use(("row", b), b)
    led.use("mod columns x", 4)
    for t in range(NPROJ):
        led.use(("px", t), t % 2)
        if t < BOTH:
            led.use(("pc", t), 2 + t % 2)
    for n, (a, b) in enumerate(((2, 3), (0, 1), (2, 3))):
        led.use(("uq", n, 0), a)
        led.use(("uq", n, 1), b)
    for n, (a, b, c) in enumerate(((0, 1, 5), (2, 3, 6))):
        led.use(("kx", 2 * n), a)
        led.use(("kx", 2 * n + 1), b)
        led.use(("kc", n), c)
    for t, b in enumerate((0, 1, 2, 3, 5, 6)):
        led.use(("v", t), b)
    for h in range(HEADS):
        led.use(("pv", h), 6)
    for b in range(8):
        led.use(("mc0", b), 7)
    for j in range(KD):
        led.use(("wo", j), j % 4)
    per = {}

    def mlp(l):
        base = list(led.uses)
        for s in range(MLP_W):
            led.use(("mlp", l, s), s % 4)
        if l == 0:
            for b in range(3):
                led.use(("mc1", b), 6)
        per[l] = [a - b for a, b in zip(led.uses, base)]
        led.uses = [b + FFG * p for b, p in zip(base, per[l])]

    mlp(0)
    for c in range(NFI):
        led.use(("fi", c), c % 4)
    for g in range(GROUPS):
        led.use(("f1", g, 0), 4)
        led.use(("f1", g, 1), 5)
    for g in range(GROUPS):
        led.use(("f2", g), 6)
    led.use("mean", 4)
    for j in range(KD):
        led.use(("fo", j), j % 4)
    mlp(1)
    return led.at, per


def dit_block_kernel(nc, c_cols, vectors, tables, dft, dft_small, x_t, ctx_t, mod0_head, mod0, mod1, w_mix0, w_mlp0,
                     w_fc, w_mlp1, out):
    AT, PER = plan_banks()
    with ExitStack() as life:
        def sb(name, shape, dt=F32, on=life):
            return on.enter_context(nc.sbuf_tensor(name, [P, *shape], dt))

        def sem(name):
            return life.enter_context(nc.semaphore(name))

        ps = life.enter_context(nc.psum_tensor("ps", [P, 8, 512], F32))

        vec = sb("vec", [NVEC])
        tab = sb("tab", [NTAB])
        x = sb("x", [KD, SEQ])
        stage = sb("stage", [STAGES, CHUNK])
        w_hi = sb("w_hi", [SLOTS, CHUNK], F32R)
        w_lo = sb("w_lo", [SLOTS, CHUNK], F32R)
        h_hi = sb("h_hi", [KD, SEQ], F32R)
        h_lo = sb("h_lo", [KD, SEQ], F32R)
        ones = sb("ones", [P])
        meanw = sb("meanw", [P])
        minus_half = sb("minus_half", [TK])
        c_in = sb("c_in", [KD * 2])
        c_act = sb("c_act", [KD * 2])
        modA = sb("modA", [2, 2 * KD])
        modG = sb("modG", [2, KD])
        modc0 = sb("modc0", [4 * KD])
        modc1 = sb("modc1", [6 * KD])
        gains = sb("gains", [3, KD])
        var = sb("var", [len(EVENTS), TK])
        rstd = sb("rstd", [len(EVENTS), TK])
        row_scale = sb("row_scale", [1 + GQA_HEADS, TX])
        top = sb("top", [32])
        minus_top = sb("minus_top", [32])
        psum_row = sb("psum_row", [32])
        inv_row = sb("inv_row", [32])
        ident = tab[:, TAB["ident"]:TAB["ident"] + P]

        mix0 = ExitStack()
        with ExitStack() as a:
            mod_head = sb("mod_head", [16, CHUNK], on=a)
        gq = sb("gq", [GQA_HEADS, SEQ], on=mix0)
        kg = sb("kg", [GQA_KV, KEYS], on=mix0)
        kr_even = sb("kr_even", [KEYS], on=mix0)
        kr_odd = sb("kr_odd", [KEYS], on=mix0)
        vg = sb("vg", [TK, GQA_KV * HD], on=mix0)
        with ExitStack() as a:
            cq_hi = sb("cq_hi", [KQ, SEQ], F32R, a)
            cq_lo = sb("cq_lo", [KQ, SEQ], F32R, a)
            ckv_hi = sb("ckv_hi", [KKV, KEYS], F32R, a)
            ckv_lo = sb("ckv_lo", [KKV, KEYS], F32R, a)
        probs_t = sb("probs_t", [2, TK, SEQ], on=mix0)
        sb("gap_a", [1024], on=mix0)
        with ExitStack() as a:
            hc_hi = sb("hc_hi", [KD, CTX], F32R, a)
            hc_lo = sb("hc_lo", [KD, CTX], F32R, a)
            with ExitStack() as b:
                ctx_x = sb("ctx_x", [KD, CTX], on=b)
            ckv_raw = sb("ckv_raw", [KKV, KEYS], on=a)
        qn = sb("qn", [MLA_HEADS, SEQ], on=mix0)
        qr = sb("qr", [2, SEQ], on=mix0)
        kn = sb("kn", [MLA_HEADS, KEYS], on=mix0)
        with ExitStack() as a:
            sq = [sb(f"sq{i}", [KEYS], on=a) for i in range(2)]
            kr_raw = sb("kr_raw", [KEYS], on=a)
            kg_raw = sb("kg_raw", [GQA_KV, KEYS], on=a)
        vm = sb("vm", [TK, MLA_HEADS * P], on=mix0)
        sb("gap_b", [768], on=mix0)
        with ExitStack() as a:
            knx = sb("knx", [SEQ], on=a)
            q_raw = sb("q_raw", [2, SEQ], on=a)
            diag = sb("diag", [TK, P], on=a)
        probs = sb("probs", [3, KEYS], on=mix0)
        with ExitStack() as a:
            tmp = sb("tmp", [3, SEQ], on=a)
        mod_acc0 = sb("mod_acc0", [2, 2, BLOCK], on=mix0)
        mix0.close()

        cs = sb("cs", [2, TX, SEQ])
        cs_small = sb("cs_small", [2 * P])
        sq_b = [sb(f"sq_b{i}", [SEQ]) for i in range(2)]
        tmp_b = sb("tmp_b", [3, SEQ])
        diag_b = sb("diag_b", [TK, P])
        mod_acc1 = sb("mod_acc1", [3, 2, BLOCK])
        with ExitStack() as a:
            hid_hi = sb("hid_hi", [KD, SEQ], F32R, a)
            hid_lo = sb("hid_lo", [KD, SEQ], F32R, a)
            relu = sb("relu", [2, SEQ], on=a)
            relu2 = sb("relu2", [2, SEQ], on=a)
        f_t = sb("f_t", [GROUPS, SEQ])
        f_mid = sb("f_mid", [TX, GROUPS, 2 * P])
        gate = sb("gate", [2, SEQ])
        u = sb("u", [KCH, SEQ + 2 * PAD])
        conv = sb("conv", [KCH, SEQ])
        cent = sb("cent", [KCH, SEQ])

        c_landed, vec_landed, tab_landed = sem("c_landed"), sem("vec_landed"), sem("tab_landed")
        x_landed, ctx_landed, dft_landed = sem("x_landed"), sem("ctx_landed"), sem("dft_landed")
        head_landed = [sem(f"head_landed{b}") for b in range(4)]
        staged = [sem(f"staged{s}") for s in range(STAGES)]
        out_written = sem("out_written")
        consts_set, pads_set = sem("consts_set"), sem("pads_set")
        chunk_done = sem("chunk_done")
        w_high = sem("w_high")
        filled = [sem(f"filled{b}") for b in range(8)]
        drained = [sem(f"drained{b}") for b in range(8)]
        silu_done = sem("silu_done")
        sq_ready, sq_summed = sem("sq_ready"), sem("sq_summed")
        var_ready, rstd_ready = sem("var_ready"), sem("rstd_ready")
        diag_ready, scale_spread = sem("diag_ready"), sem("scale_spread")
        t_ready, hh_ready, h_ready = sem("t_ready"), sem("hh_ready"), sem("h_ready")
        knx_ready, rotated, rot_used = sem("knx_ready"), sem("rotated"), sem("rot_used")
        cq_ready, ckv_scaled, ckvh_ready, ckv_ready = (sem("cq_ready"), sem("ckv_scaled"), sem("ckvh_ready"),
                                                       sem("ckv_ready"))
        scored, top_ready, exp_done, probs_ready = sem("scored"), sem("top_ready"), sem("exp_done"), sem("probs_ready")
        turned, turned_copied, oh_ready = sem("turned"), sem("turned_copied"), sem("oh_ready")
        hidh_ready, hid_ready = sem("hidh_ready"), sem("hid_ready")
        fh_ready, conv_step, cent_ready, y_ready, s_ready, sh_ready, mix_ready = (
            sem("fh_ready"), sem("conv_step"), sem("cent_ready"), sem("y_ready"), sem("s_ready"), sem("sh_ready"),
            sem("mix_ready"))
        y_tile = sem("y_tile")
        dve_step = sem("dve_step")

        block = life.enter_context(nc.Block())

        def v(name, n=0, w=1):
            return vec[:, VEC[name] + n:VEC[name] + n + w]

        def bank_of(key):
            return ps[:, AT[key][0], :]

        def staged_value(n, at=0):
            return 16 * (n // STAGES + 1) + at * 16

        def mlp_offsets(l):
            if l:
                return list(range(MLP_W)), []
            return [0, *(2 * s - 1 for s in range(1, 13)), 25, 26, 27], [2 * q + 2 for q in range(MLP_M)]

        @block.sync
        def _(sp):
            sp.dma_start(c_in[:], c_cols).then_inc(c_landed, 16)
            sp.dma_start(x[:], x_t.rearrange("k p t -> p k t")).then_inc(x_landed, 16)
            sp.dma_start(vec[:], vectors).then_inc(vec_landed, 16)
            for b in range(4):
                sp.dma_start(mod_head[:, 4 * b:4 * b + 4, :],
                             mod0_head[4 * b:4 * b + 4].rearrange("c p n -> p c n")).then_inc(head_landed[b], 16)
                if b == 0:
                    sp.dma_start(ctx_x[:], ctx_t.rearrange("k p t -> p k t")).then_inc(ctx_landed, 16)
                    sp.dma_start(tab[:], tables).then_inc(tab_landed, 16)

            def load(n, src, later=0):
                if n >= STAGES:
                    sp.wait_ge(chunk_done, n - STAGES + 1 + later)
                sp.dma_start(stage[:, n % STAGES, :], src).then_inc(staged[n % STAGES], 16)

            for w in range(NW_IN):
                load(w, w_mix0[w])
            for m in range(NM0):
                load(NW_IN + m, mod0[m])
            for j in range(KD):
                load(N_WOUT + j, w_mix0[NW_IN + j])
            bank, use = AT[("wo", 0)]
            sp.wait_ge(drained[bank], use)
            sp.dma_start(cs[:], dft).then_inc(dft_landed, 16)
            sp.dma_start(cs_small[:], dft_small).then_inc(dft_landed, 16)
            for l, (n0, weights) in enumerate(((N_MLP0, w_mlp0), (N_MLP1, w_mlp1))):
                w_at, m_at = mlp_offsets(l)
                per = len(w_at) + len(m_at)
                with sp.Fori(0, FFG) as i:
                    for o in range(per):
                        src = (weights[bass.ds(i * MLP_W + w_at.index(o), 1)] if o in w_at
                               else mod1[bass.ds(i * MLP_M + m_at.index(o), 1)])
                        load(n0 + o, src.rearrange("a p n -> (a p) n"), i * per)
                if l == 0:
                    for c in range(NFI + KD):
                        load(N_FC + c, w_fc[c])
            for k in range(KD):
                sp.wait_ge(y_tile, k + 1)
                sp.dma_start(out[k], x[:, k, :]).then_inc(out_written, 16)
            sp.wait_ge(out_written, 16 * KD)

        @block.gpsimd
        def _(pool):
            pool.memset(ones[:], 1.0).then_inc(consts_set, 1)
            pool.memset(meanw[:], -1.0 / CH).then_inc(consts_set, 1)
            pool.memset(minus_half[:], -0.5).then_inc(consts_set, 1)
            pool.wait_ge(consts_set, 3)

            def inverse_root(e):
                n = EVENTS[e][2]
                pool.wait_ge(var_ready, e + 1)
                pool.tensor_tensor(rstd[:, e, 0:n], var[:, e, 0:n], minus_half[:, 0:n], ALU.pow).then_inc(rstd_ready, 1)

            inverse_root(EV["x0"])
            inverse_root(EV["ctx0"])
            pool.wait_ge(drained[3], 1)
            pool.memset(kr_even[ROPE:P, :], 0.0).then_inc(pads_set, 1)
            pool.memset(kr_odd[0:ROPE, :], 0.0).then_inc(pads_set, 1)
            pool.wait_ge(pads_set, 2)
            for e in range(EV["ckv"], EV["ln"]):
                inverse_root(e)
                if e == EV["x2"]:
                    pool.memset(u[:, :, 0:PAD], 0.0).then_inc(pads_set, 1)
                    pool.memset(u[:, :, PAD + SEQ:SEQ + 2 * PAD], 0.0).then_inc(pads_set, 1)
                    pool.wait_ge(pads_set, 4)
            for e in range(EV["ln"], len(EVENTS)):
                inverse_root(e)

        @block.scalar
        def _(act):
            def full(key, later=0):
                bank, use = AT[key]
                act.wait_ge(filled[bank], use + later)
                return ps[:, bank, :]

            def free(ins, key):
                ins.then_inc(drained[AT[key][0]], 1)

            def split_high(n, w, slot_key, staged_later=0, key_later=0):
                act.wait_ge(staged[n % STAGES], 16 * (n // STAGES + 1) + staged_later)
                if slot_key is not None:
                    full(slot_key, key_later)
                act.activation(w_hi[:, w % SLOTS, :], stage[:, n % STAGES, :], ACT.Copy).then_inc(w_high, 1)

            def square(q, in_ap):
                buf = (sq if q < SQ0[EV["x1"]] else sq_b)[q % 2]
                if q >= 2:
                    act.wait_ge(sq_summed, q - 1)
                return act.activation(buf[:, 0:in_ap.shape[1]], in_ap, ACT.Square)

            def modulated_high(a, shift, hi, width, t):
                for k in range(KD):
                    act.wait_ge(t_ready, a * KD + k + 1)
                    act.activation(hi[:, k, :], t[:, (a * KD + k) % 3, 0:width], ACT.Identity,
                                   bias=shift[:, k:k + 1]).then_inc(hh_ready, 1)

            def square_x(event, k, key):
                bank, use = AT[key]
                act.wait_ge(drained[bank], use)
                square(SQ0[EV[event]] + k, x[:, k, :]).then_inc(sq_ready, 1)

            act.wait_ge(c_landed, 16)
            act.activation(c_act[:], c_in[:], ACT.Silu).then_inc(silu_done, 1)
            act.wait_ge(x_landed, 16)
            for k in range(KD):
                square(SQ0[EV["x0"]] + k, x[:, k, :]).then_inc(sq_ready, 1)
            act.wait_ge(ctx_landed, 16)
            for k in range(KD):
                square(SQ0[EV["ctx0"]] + k, ctx_x[:, k, :]).then_inc(sq_ready, 1)
            split_high(0, 0, None)
            split_high(1, 1, None)
            for b in range(4):
                act.activation(mod_acc0[0:2, b // 2, b % 2, :], full(("row", b))[0:2, :],
                               ACT.Copy).then_inc(drained[b], 1)
            modulated_high(0, modA[:, 0, :], h_hi, SEQ, tmp)
            modulated_high(1, modA[:, 1, :], hc_hi, CTX, tmp)

            for t, name in enumerate(PROJ):
                if t >= 1:
                    split_high(t + 1, t + 1, ("px", t - 1))
                if t == 5:
                    for i in range(KKV):
                        act.wait_ge(ckv_scaled, i + 1)
                        act.activation(ckv_hi[:, i, :], ckv_raw[:, i, :], ACT.Copy).then_inc(ckvh_ready, 1)
                px = full(("px", t))
                if t < BOTH:
                    pc = full(("pc", t))[:, 0:CTX]
                if name in ("ckv0", "ckv1", "kg0", "kg1"):
                    i = int(name[-1])
                    raw = (ckv_raw if name[0] == "c" else kg_raw)[:, i, :]
                    q = SQ0[EV["ckv"]] + i if name[0] == "c" else SQ0[EV[name]]
                    act.activation(raw[:, CTX:KEYS], px, ACT.Copy)
                    act.wait_ge(sq_summed, q - 1)
                    free(act.activation(sq[q % 2][:, CTX:KEYS], px, ACT.Square), ("px", t))
                    free(act.activation(raw[:, 0:CTX], pc, ACT.Copy), ("pc", t))
                    act.wait_ge(drained[AT[("pc", t)][0]], AT[("pc", t)][1])
                    act.activation(sq[q % 2][:, 0:CTX], raw[:, 0:CTX], ACT.Square).then_inc(sq_ready, 1)
                elif name == "kr":
                    free(act.activation(kr_raw[:, CTX:KEYS], px, ACT.Copy), ("px", t))
                    free(act.activation(kr_raw[:, 0:CTX], pc, ACT.Copy), ("pc", t))
                elif name in ("v0", "v1"):
                    cols = slice(int(name[1]) * P, int(name[1]) * P + P)
                    free(act.activation(vg[:, TC:TK, cols], px.rearrange("p (t c) -> p t c", c=P), ACT.Copy), ("px", t))
                    free(act.activation(vg[:, 0:TC, cols], pc.rearrange("p (t c) -> p t c", c=P), ACT.Copy), ("pc", t))
                elif name[:2] == "cq":
                    i = int(name[2])
                    act.activation(cq_hi[:, i, :], px, ACT.Copy, scale=v("qg", i))
                    square(SQ0[EV["cq"]] + i, px).then_inc(sq_ready, 1)
                else:
                    i = int(name[2])
                    square(SQ0[EV[name]], px).then_inc(sq_ready, 1)
                    if i >= 2:
                        act.wait_ge(rot_used, ROTS.index(name) - 1)
                    free(act.activation(q_raw[:, i % 2, :], px, ACT.Copy, scale=v("gqg")), ("px", t))

            split_high(UQ0 + 1, UQ0 + 1, ("px", NPROJ - 1))
            for i in range(2):
                free(act.activation(qn[:, i, :], full(("uq", 0, i)), ACT.Copy), ("uq", 0, i))
            split_high(UQR, UQR, ("uq", 0, 1))
            for i in range(2):
                free(act.activation(qn[:, 2 + i, :], full(("uq", 1, i)), ACT.Copy), ("uq", 1, i))
            split_high(UKK, UKK, ("uq", 1, 1))
            for i in range(2):
                act.wait_ge(rot_used, ROTS.index(f"qr{i}") - 1)
                free(act.activation(q_raw[:, i, :], full(("uq", 2, i)), ACT.Copy), ("uq", 2, i))
            split_high(UKV, UKV, ("uq", 2, 1))
            for n in range(2):
                for h in (2 * n, 2 * n + 1):
                    free(act.activation(kn[:, h, CTX:KEYS], full(("kx", h)), ACT.Copy), ("kx", h))
                free(act.activation(kn[:, 2 * n:2 * n + 2, 0:CTX],
                                    full(("kc", n)).rearrange("p (h t) -> p h t", t=CTX), ACT.Copy), ("kc", n))
            for t in range(TK):
                free(act.activation(vm[:, t, :], full(("v", t)), ACT.Copy), ("v", t))

            for s in range(4 * HEADS + 4):
                if s >= 7 and s % 4 == 3:
                    h = (s - 7) // 4
                    act.activation(h_hi[:, h, :], full(("pv", h)), ACT.Copy).then_inc(oh_ready, 1)
                if 2 <= s < 4 * HEADS + 2:
                    n = s - 2
                    h, qt = n // 4, n % 4
                    act.wait_ge(turned, n + 1)
                    act.activation(probs_t[:, h % 2, :, qt * P:qt * P + P].rearrange("p (a b) c -> p a b c", a=2),
                                   ps[:, 4:6, 0:3 * P].rearrange("p a (b c) -> p a b c", c=P),
                                   ACT.Copy).then_inc(turned_copied, 1)
                if s < 4 * HEADS:
                    h, qt = s // 4, s % 4
                    pair = 2 * (s % 2)
                    act.wait_ge(top_ready, s + 1)
                    if s >= 3:
                        act.wait_ge(turned, s - 2)
                    head_scale = row_scale[:, max(h - MLA_HEADS + 1, 0), qt:qt + 1]
                    act.activation(probs[:, s % 3, :].rearrange("p (a b) -> p a b", a=2), ps[:, pair:pair + 2, 0:384],
                                   ACT.Exp, bias=minus_top[:, s:s + 1], scale=head_scale,
                                   accum_out=psum_row[:, s:s + 1]).then_inc(exp_done, 1)

            split_high(N_WOUT, W_WOUT, ("v", TK - 1))
            split_high(N_WOUT + 1, W_WOUT + 1, ("v", TK - 1))
            for j in range(KD):
                n, w = (N_WOUT + j + 2, W_WOUT + j + 2) if j < KD - 2 else (N_MLP0 + j - KD + 2, W_MLP0 + j - KD + 2)
                split_high(n, w, ("wo", j))
                if j >= 1:
                    square_x("x1", j - 1, ("wo", j - 1))
            square_x("x1", KD - 1, ("wo", KD - 1))
            modulated_high(2, modc0[:, KD:2 * KD], h_hi, SEQ, tmp_b)

            def mlp(l, i, last):
                n0, w0 = (N_MLP0, W_MLP0) if l == 0 else (N_MLP1, W_MLP1)
                w_at, m_at = mlp_offsets(l)
                per = len(w_at) + len(m_at)
                for s in range(MLP_W):
                    o = w_at[s + 2] if s + 2 < MLP_W else per + s + 2 - MLP_W
                    if not (last and l == 1 and s + 2 >= MLP_W):
                        split_high(n0 + o, w0 + s + 2, ("mlp", l, s), 16 * per // STAGES * i, PER[l][s % 4] * i)
                    if s < KD:
                        key = ("mlp", l, s)
                        p = full(key, PER[l][s % 4] * i)
                        if s >= 2:
                            act.wait_ge(hid_ready, l * FFG * KD + s - 1 + KD * i)
                        free(act.activation(relu[:, s % 2, :], p, ACT.Relu), key)
                        act.wait_ge(drained[AT[key][0]], AT[key][1] + PER[l][s % 4] * i)
                        act.activation(hid_hi[:, s, :], relu[:, s % 2, :], ACT.Square).then_inc(hidh_ready, 1)
                    elif last and s > KD:
                        bank, use = AT[("mlp", l, s - 1)]
                        act.wait_ge(drained[bank], use + PER[l][bank] * i)
                        square(SQ0[EV["x2" if l == 0 else "x4"]] + s - KD - 1, x[:, s - KD - 1, :]).then_inc(sq_ready, 1)
                if last:
                    bank, use = AT[("mlp", l, MLP_W - 1)]
                    act.wait_ge(drained[bank], use + PER[l][bank] * i)
                    square(SQ0[EV["x2" if l == 0 else "x4"]] + KD - 1, x[:, KD - 1, :]).then_inc(sq_ready, 1)

            with act.Fori(0, FFG - 1) as i:
                mlp(0, i, False)
            mlp(0, FFG - 1, True)

            modulated_high(3, modc1[:, 0:KD], h_hi, SEQ, tmp_b)
            for c, name in enumerate(FI):
                split_high(N_FC + c + 2, W_FC + c + 2, ("fi", c))
                key = ("fi", c)
                i = int(name[1])
                if name[0] == "g":
                    if i >= 2:
                        bank, use = AT[("fi", FI.index(f"a{i - 2}"))]
                        act.wait_ge(drained[bank], use)
                    free(act.activation(gate[:, i % 2, :], full(key), ACT.Sigmoid), key)
                elif name[0] == "f":
                    free(act.activation(f_t[:, i, :], full(key), ACT.Copy), key)
                    if i >= 1:
                        for b in range(2):
                            free(act.activation(f_mid[:, 2 * b:2 * b + 2, i - 1, :],
                                                full(("f1", i - 1, b)).rearrange("p (t c) -> p t c", t=2),
                                                ACT.Copy), ("f1", i - 1, b))
            for b in range(2):
                free(act.activation(f_mid[:, 2 * b:2 * b + 2, GROUPS - 1, :],
                                    full(("f1", GROUPS - 1, b)).rearrange("p (t c) -> p t c", t=2),
                                    ACT.Copy), ("f1", GROUPS - 1, b))
            for g in range(GROUPS):
                act.activation(h_hi[:, g, :], full(("f2", g)), ACT.Copy,
                               scale=float((SEQ * P) ** -0.5)).then_inc(fh_ready, 1)
            for i in range(KCH):
                act.wait_ge(cent_ready, i + 1)
                square(SQ0[EV["ln"]] + i, cent[:, i, :]).then_inc(sq_ready, 1)
            for i in range(KCH + 1):
                if i < KCH:
                    act.wait_ge(y_ready, i + 1)
                    act.activation(conv[:, i, :], cent[:, i, :], ACT.Silu, bias=v("lnb", i),
                                   scale=v("lng", i)).then_inc(s_ready, 1)
                if i >= 1:
                    act.wait_ge(s_ready, i)
                    act.activation(h_hi[:, KCH + i - 1, :], conv[:, i - 1, :], ACT.Copy).then_inc(sh_ready, 1)
            for j in range(KD):
                n, w = (N_FCOUT + j + 2, W_FCOUT + j + 2) if j < KD - 2 else (N_MLP1 + j - KD + 2, W_MLP1 + j - KD + 2)
                split_high(n, w, ("fo", j))
                if j >= 1:
                    square_x("x3", j - 1, ("fo", j - 1))
            square_x("x3", KD - 1, ("fo", KD - 1))
            modulated_high(4, modc1[:, 3 * KD:4 * KD], h_hi, SEQ, tmp_b)
            with act.Fori(0, FFG - 1) as i:
                mlp(1, i, False)
            mlp(1, FFG - 1, True)

        @block.vector
        def _(dve):
            own = [0]

            def tick(ins):
                ins.then_inc(dve_step, 1)
                own[0] += 1
                return own[0]

            def own_wait(count, later=0):
                dve.wait_ge(dve_step, count + later)

            def full(key, later=0):
                bank, use = AT[key]
                dve.wait_ge(filled[bank], use + later)
                return ps[:, bank, :]

            def free(ins, key):
                ins.then_inc(drained[AT[key][0]], 1)

            def split_low(n, w, w_later=0, n_later=0):
                dve.wait_ge(w_high, w + 1 + w_later)
                dve.tensor_tensor(w_lo[:, w % SLOTS, :], stage[:, n % STAGES, :],
                                  w_hi[:, w % SLOTS, :].bitcast(F32), ALU.subtract).then_inc(chunk_done, 1)

            def mod_chunk(n, block_acc, q, staged_later=0, n_before=None, n_later=0):
                dve.wait_ge(staged[n % STAGES], 16 * (n // STAGES + 1) + staged_later)
                if q:
                    dve.wait_ge(chunk_done, n_before + 1 + n_later)
                for k2 in range(2):
                    k = 2 * q + k2
                    src = stage[:, n % STAGES, k2 * BLOCK:(k2 + 1) * BLOCK]
                    acc = block_acc[:, k2, :]
                    if q == 0:
                        ins = dve.tensor_scalar(acc, src, c_act[:, 2 * k:2 * k + 1], None, ALU.mult)
                    else:
                        ins = dve.scalar_tensor_tensor(out=acc, in0=src, scalar=c_act[:, 2 * k:2 * k + 1], in1=acc,
                                                       op0=ALU.mult, op1=ALU.add)
                ins.then_inc(chunk_done, 1)

            def variance(e):
                n, width = EVENTS[e][2], EVENTS[e][3]
                dve.wait_ge(sq_summed, SQ0[e + 1])
                dve.tensor_scalar(var[:, e, 0:n], ps[:, 7, 0:n], 1.0 / width, EPS, ALU.mult, ALU.add) \
                    .then_inc(var_ready, 1)

            def diagonals(e):
                dve.wait_ge(rstd_ready, e + 1)
                if BC[e]:
                    dve.wait_ge(scale_spread, BC[e])
                dst = diag if e < EV["x1"] else diag_b
                for t in range(EVENTS[e][2]):
                    ins = dve.tensor_scalar(dst[:, t, :], ident, rstd[:, e, t:t + 1], None, ALU.mult)
                ins.then_inc(diag_ready, 1)

            def modulated(a, e, src, gain, shift, hi, lo, width, bank, t):
                dve.wait_ge(scale_spread, BC[e] + 1)
                for k in range(KD + 1):
                    if k < KD:
                        if a * KD + k - 2 > 0:
                            dve.wait_ge(h_ready, a * KD + k - 2)
                        ins = dve.scalar_tensor_tensor(out=t[:, (a * KD + k) % 3, 0:width], in0=src[:, k, :],
                                                       scalar=gain[:, k:k + 1], in1=ps[:, bank, 0:width],
                                                       op0=ALU.mult, op1=ALU.mult).then_inc(t_ready, 1)
                    if k >= 1:
                        dve.wait_ge(hh_ready, a * KD + k)
                        dve.scalar_tensor_tensor(out=lo[:, k - 1, :], in0=t[:, (a * KD + k - 1) % 3, 0:width],
                                                 scalar=shift[:, k - 1:k], in1=hi[:, k - 1, :].bitcast(F32),
                                                 op0=ALU.add, op1=ALU.subtract).then_inc(h_ready, 1)

            def add_product(key, k, g, later=0):
                p = full(key, later)
                free(dve.scalar_tensor_tensor(out=x[:, k, :], in0=p, scalar=g, in1=x[:, k, :], op0=ALU.mult,
                                              op1=ALU.add), key)

            def rope(name, src, x_ready, dsts):
                r = ROTS.index(name)
                c, s = ("cosm", "sinm") if name[1] == "r" else ("cosg", "sing")
                x_ready()
                if r:
                    dve.wait_ge(rot_used, r)
                else:
                    dve.wait_ge(h_ready, 2 * KD)
                dve.tensor_tensor(tmp[:, 0, :], src, tab[:, TAB[c]:TAB[c] + SEQ], ALU.mult)
                dve.wait_ge(rotated, r + 1)
                done = tick(dve.tensor_tensor(tmp[:, 1, :], ps[:, 4, :], tab[:, TAB[s]:TAB[s] + SEQ], ALU.mult))
                own_wait(done)
                for dst, lo_p, hi_p in dsts:
                    ins = dve.tensor_tensor(dst, tmp[lo_p:hi_p, 0, :], tmp[lo_p:hi_p, 1, :], ALU.add)
                ins.then_inc(rot_used, 1)

            def drained_key(key):
                bank, use = AT[key]
                return lambda: dve.wait_ge(drained[bank], use)

            dve.wait_ge(consts_set, 3)
            variance(EV["x0"])
            dve.wait_ge(tab_landed, 16)
            diagonals(EV["x0"])
            variance(EV["ctx0"])
            diagonals(EV["ctx0"])
            split_low(0, 0)
            split_low(1, 1)
            dve.wait_ge(vec_landed, 16)
            cols = full("mod columns x")[:, 0:4 * KD].rearrange("p (j s) -> p s j", s=2)
            for s in range(2):
                ins = dve.tensor_tensor(modA[:, s, :], cols[:, s, :], v("modb", 0, 2 * KD), ALU.add)
            free(ins, "mod columns x")
            drained_key("mod columns x")()
            for s in range(2):
                done = tick(dve.scalar_tensor_tensor(out=modG[:, s, :], in0=modA[:, s, KD:2 * KD], scalar=1.0,
                                                     in1=v("n1", 0, KD), op0=ALU.add, op1=ALU.mult))
            own_wait(done)
            modulated(0, EV["x0"], x, modG[:, 0, :], modA[:, 0, :], h_hi, h_lo, SEQ, 5, tmp)
            modulated(1, EV["ctx0"], ctx_x, modG[:, 1, :], modA[:, 1, :], hc_hi, hc_lo, CTX, 6, tmp)

            def kr_rope():
                dve.wait_ge(pads_set, 2)
                drained_key(("pc", 2))()
                dve.tensor_copy(kr_even[0:ROPE, 0:CTX], kr_raw[0:ROPE, 0:CTX])
                dve.tensor_copy(kr_odd[ROPE:P, 0:CTX], kr_raw[ROPE:P, 0:CTX])
                rope("kr", kr_raw[:, CTX:KEYS], drained_key(("pc", 2)),
                     [(kr_even[0:ROPE, CTX:KEYS], 0, ROPE), (kr_odd[ROPE:P, CTX:KEYS], ROPE, P)])

            def scale_ckv():
                dve.wait_ge(scale_spread, BC[EV["ckv"]] + 1)
                for i in range(KKV):
                    for bank, lo_t, hi_t in ((6, 0, CTX), (5, CTX, KEYS)):
                        ins = dve.scalar_tensor_tensor(out=ckv_raw[:, i, lo_t:hi_t], in0=ckv_raw[:, i, lo_t:hi_t],
                                                       scalar=v("kvg", i), in1=ps[:, bank, 0:hi_t - lo_t],
                                                       op0=ALU.mult, op1=ALU.mult)
                    ins.then_inc(ckv_scaled, 1)

            def low_ckv():
                for i in range(KKV):
                    dve.wait_ge(ckvh_ready, i + 1)
                    dve.tensor_tensor(ckv_lo[:, i, :], ckv_raw[:, i, :], ckv_hi[:, i, :].bitcast(F32),
                                      ALU.subtract).then_inc(ckv_ready, 1)

            def scale_kg(i):
                dve.wait_ge(scale_spread, BC[EV[f"kg{i}"]] + 1)
                dve.scalar_tensor_tensor(out=kg[:, i, 0:CTX], in0=kg_raw[:, i, 0:CTX], scalar=v("gkg"),
                                         in1=ps[:, 6, 0:CTX], op0=ALU.mult, op1=ALU.mult)
                dve.scalar_tensor_tensor(out=knx[:], in0=kg_raw[:, i, CTX:KEYS], scalar=v("gkg"), in1=ps[:, 5, :],
                                         op0=ALU.mult, op1=ALU.mult).then_inc(knx_ready, 1)

            def row_scales(e, r, scale):
                dve.wait_ge(rstd_ready, e + 1)
                tick(dve.tensor_scalar(row_scale[:, r, :], rstd[:, e, 0:TX], scale, None, ALU.mult))

            def gq_steps(i):
                variance(EV[f"gq{i}"])
                rope(f"gq{i}", q_raw[:, i % 2, :], drained_key(("px", PROJ.index(f"gq{i}"))), [(gq[:, i, :], 0, P)])
                row_scales(EV[f"gq{i}"], 1 + i, GQA_SCALE)

            for t, name in enumerate(PROJ):
                if t == 3:
                    variance(EV["ckv"])
                    diagonals(EV["ckv"])
                if t == 4:
                    scale_ckv()
                    kr_rope()
                if t == 5:
                    variance(EV["kg0"])
                    diagonals(EV["kg0"])
                    low_ckv()
                if t == 6:
                    scale_kg(0)
                    variance(EV["kg1"])
                    diagonals(EV["kg1"])
                if t == 7:
                    rope("kg0", knx[:], lambda: dve.wait_ge(knx_ready, 1), [(kg[:, 0, CTX:KEYS], 0, P)])
                    scale_kg(1)
                if t == 8:
                    rope("kg1", knx[:], lambda: dve.wait_ge(knx_ready, 2), [(kg[:, 1, CTX:KEYS], 0, P)])
                if t == 12:
                    variance(EV["cq"])
                    row_scales(EV["cq"], 0, MLA_SCALE)
                if t >= 13:
                    gq_steps(t - 13)
                if t >= 1:
                    split_low(t + 1, t + 1)
                if name[:2] == "cq":
                    i = int(name[2])
                    px = full(("px", t))
                    dve.wait_ge(sq_ready, SQ0[EV["cq"]] + i + 1)
                    free(dve.scalar_tensor_tensor(out=cq_lo[:, i, :], in0=px, scalar=v("qg", i),
                                                  in1=cq_hi[:, i, :].bitcast(F32), op0=ALU.mult, op1=ALU.subtract),
                         ("px", t))
            gq_steps(2)
            split_low(UQ0 + 1, UQ0 + 1)
            gq_steps(3)
            for w in (UQR, UKK, UKV):
                split_low(w, w)
            for i in range(2):
                rope(f"qr{i}", q_raw[:, i, :], drained_key(("uq", 2, i)), [(qr[:, i, :], 0, P)])

            for s in range(4 * HEADS + 4):
                if 1 <= s < 4 * HEADS + 1:
                    n = s - 1
                    dve.wait_ge(exp_done, n + 1)
                    done = tick(dve.reciprocal(inv_row[:, n:n + 1], psum_row[:, n:n + 1]))
                    own_wait(done)
                    dve.tensor_scalar(probs[:, n % 3, :], probs[:, n % 3, :], inv_row[:, n:n + 1], None,
                                      ALU.mult).then_inc(probs_ready, 1)
                if s < 4 * HEADS:
                    h, qt, pair = s // 4, s % 4, 2 * (s % 2)
                    dve.wait_ge(scored, s + 1)
                    done = tick(dve.tensor_reduce(top[:, s:s + 1], ps[:, pair:pair + 2, 0:384], AX.XY, ALU.max))
                    own_wait(done)
                    dve.tensor_scalar(minus_top[:, s:s + 1], top[:, s:s + 1],
                                      row_scale[:, max(h - MLA_HEADS + 1, 0), qt:qt + 1], -1.0, ALU.mult,
                                      ALU.mult).then_inc(top_ready, 1)
                    b, q = s // 4, s % 4
                    mod_chunk(NW_IN + s, mod_acc0[:, b % 2], q, n_before=NW_IN + s - 1)
                if s >= 6 and s % 4 == 2:
                    b = (s - 6) // 4
                    p = full(("mc0", b))
                    free(dve.tensor_tensor(modc0[:, 4 * b:4 * b + 4], p[:, 0:4], v("modb", 2 * KD + 4 * b, 4),
                                           ALU.add), ("mc0", b))
                if s >= 7 and s % 4 == 3:
                    h = (s - 7) // 4
                    dve.wait_ge(oh_ready, h + 1)
                    free(dve.tensor_tensor(h_lo[:, h, :], full(("pv", h)), h_hi[:, h, :].bitcast(F32), ALU.subtract),
                         ("pv", h))

            split_low(N_WOUT, W_WOUT)
            split_low(N_WOUT + 1, W_WOUT + 1)
            for j in range(KD):
                n, w = (N_WOUT + j + 2, W_WOUT + j + 2) if j < KD - 2 else (N_MLP0 + j - KD + 2, W_MLP0 + j - KD + 2)
                split_low(n, w)
                add_product(("wo", j), j, modc0[:, j:j + 1])

            def gain(r, scales, norm):
                return tick(dve.scalar_tensor_tensor(out=gains[:, r, :], in0=scales, scalar=1.0, in1=norm, op0=ALU.add,
                                                     op1=ALU.mult))

            def norm_x(r, event, scales, norm, shift):
                done = gain(r, scales, norm)
                variance(EV[event])
                own_wait(done)
                diagonals(EV[event])
                modulated(2 + r, EV[event], x, gains[:, r, :], shift, h_hi, h_lo, SEQ, 5, tmp_b)

            norm_x(0, "x1", modc0[:, 2 * KD:3 * KD], v("n2", 0, KD), modc0[:, KD:2 * KD])

            def mlp(l, i, last, gate2):
                n0, w0 = (N_MLP0, W_MLP0) if l == 0 else (N_MLP1, W_MLP1)
                w_at, m_at = mlp_offsets(l)
                per = len(w_at) + len(m_at)
                first = own[0]
                steps = KD * i
                for s in range(MLP_W):
                    if s < len(m_at):
                        b, q = s // 4, s % 4
                        mod_chunk(n0 + m_at[s], mod_acc1[:, b], q, 16 * per // STAGES * i, n0 + m_at[s - 1], per * i)
                    o = w_at[s + 2] if s + 2 < MLP_W else per + s + 2 - MLP_W
                    if not (last and l == 1 and s + 2 >= MLP_W):
                        split_low(n0 + o, w0 + s + 2, MLP_W * i)
                    if l == 0 and s in (6, 10, 14):
                        b = (s - 6) // 4
                        p = full(("mc1", b), PER[0][6] * i)
                        cols = bass.ds((3 * i + b) * 4, 4)
                        free(dve.tensor_tensor(modc1[:, cols], p[:, 0:4],
                                               vec[:, bass.ds(VEC["modb"] + 6 * KD + (3 * i + b) * 4, 4)],
                                               ALU.add), ("mc1", b))
                    key = ("mlp", l, s)
                    if s < KD:
                        bank, use = AT[key]
                        dve.wait_ge(drained[bank], use + PER[l][bank] * i)
                        own[0] += 1
                        dve.tensor_tensor(relu2[:, s % 2, :], relu[:, s % 2, :], relu[:, s % 2, :],
                                          ALU.mult).then_inc(dve_step, 1)
                        dve.wait_ge(hidh_ready, (l * FFG + 0) * KD + s + 1 + KD * i)
                        own_wait(first + s + 1, steps)
                        dve.tensor_tensor(hid_lo[:, s, :], relu2[:, s % 2, :], hid_hi[:, s, :].bitcast(F32),
                                          ALU.subtract).then_inc(hid_ready, 1)
                    else:
                        add_product(key, s - KD, gate2[:, s - KD:s - KD + 1], PER[l][s % 4] * i)
                own[0] = first

            with dve.Fori(0, FFG - 1) as i:
                mlp(0, i, False, modc0[:, 3 * KD:4 * KD])
            mlp(0, FFG - 1, True, modc0[:, 3 * KD:4 * KD])
            own[0] += FFG * KD

            norm_x(1, "x2", modc1[:, KD:2 * KD], v("n1", KD, KD), modc1[:, 0:KD])

            def convolve(first, last):
                for n in range(first, last):
                    pair, k, i = n // (2 * TAPS), n % (2 * TAPS) // 2, n // (2 * TAPS) * 2 + n % 2
                    w = v("convw", i * TAPS + k)
                    if k == 0:
                        bank, use = AT[("fi", FI.index(f"a{i}"))]
                        dve.wait_ge(drained[bank], use)
                        ins = dve.tensor_scalar(conv[:, i, :], u[:, i, 0:SEQ], w, v("convb", i), ALU.mult, ALU.add)
                    else:
                        dve.wait_ge(conv_step, n - 1)
                        ins = dve.scalar_tensor_tensor(out=conv[:, i, :], in0=u[:, i, k:k + SEQ], scalar=w,
                                                       in1=conv[:, i, :], op0=ALU.mult, op1=ALU.add)
                    ins.then_inc(conv_step, 1)

            dve.wait_ge(pads_set, 4)
            for c, name in enumerate(FI):
                split_low(N_FC + c + 2, W_FC + c + 2)
                i = int(name[1])
                if name[0] == "a":
                    p = full(("fi", c))
                    bank, use = AT[("fi", c - 1)]
                    dve.wait_ge(drained[bank], use)
                    free(dve.tensor_tensor(u[:, i, PAD:PAD + SEQ], p, gate[:, i % 2, :], ALU.mult), ("fi", c))
                if c >= 4:
                    convolve(8 * (c - 4), 8 * (c - 3))
            for g in range(GROUPS):
                convolve(64 + 12 * g, 76 + 12 * g)
                dve.wait_ge(fh_ready, g + 1)
                free(dve.scalar_tensor_tensor(out=h_lo[:, g, :], in0=full(("f2", g)), scalar=float((SEQ * P) ** -0.5),
                                              in1=h_hi[:, g, :].bitcast(F32), op0=ALU.mult, op1=ALU.subtract),
                     ("f2", g))
            convolve(112, KCH * TAPS)
            mean = full("mean")
            for i in range(KCH):
                dve.tensor_tensor(cent[:, i, :], conv[:, i, :], mean, ALU.add).then_inc(cent_ready, 1)
            variance(EV["ln"])
            diagonals(EV["ln"])
            dve.wait_ge(scale_spread, BC[EV["ln"]] + 1)
            for i in range(KCH):
                dve.tensor_tensor(cent[:, i, :], cent[:, i, :], ps[:, 5, :], ALU.mult).then_inc(y_ready, 1)
            for i in range(KCH):
                dve.wait_ge(sh_ready, i + 1)
                dve.tensor_tensor(h_lo[:, KCH + i, :], conv[:, i, :], h_hi[:, KCH + i, :].bitcast(F32),
                                  ALU.subtract).then_inc(mix_ready, 1)
            for j in range(KD):
                n, w = (N_FCOUT + j + 2, W_FCOUT + j + 2) if j < KD - 2 else (N_MLP1 + j - KD + 2, W_MLP1 + j - KD + 2)
                split_low(n, w)
                add_product(("fo", j), j, modc1[:, 2 * KD + j:2 * KD + j + 1])
            norm_x(2, "x3", modc1[:, 4 * KD:5 * KD], v("n2", KD, KD), modc1[:, 3 * KD:4 * KD])
            with dve.Fori(0, FFG - 1) as i:
                mlp(1, i, False, modc1[:, 5 * KD:6 * KD])
            mlp(1, FFG - 1, True, modc1[:, 5 * KD:6 * KD])

            variance(EV["x4"])
            diagonals(EV["x4"])
            dve.wait_ge(scale_spread, BC[EV["x4"]] + 1)
            for k in range(KD):
                dve.scalar_tensor_tensor(out=x[:, k, :], in0=x[:, k, :], scalar=v("nf", k), in1=ps[:, 5, :],
                                         op0=ALU.mult, op1=ALU.mult).then_inc(y_tile, 1)

        @block.tensor
        def _(pe):
            def acquire(key, later=0):
                bank, use = AT[key]
                if use > 1:
                    pe.wait_ge(drained[bank], use - 1 + later)
                return ps[:, bank, :]

            def fill(ins, key):
                ins.then_inc(filled[AT[key][0]], 1)

            def product(outp, left, right, first, last):
                (lh, ll), (rh, rl) = left, right
                pe.matmul(outp, lh, rh, start=first, stop=False)
                pe.matmul(outp, lh, rl, start=False, stop=False)
                return pe.matmul(outp, ll, rh, start=False, stop=last)

            def weights(w, lo_c, hi_c):
                return w_hi[:, w % SLOTS, lo_c:hi_c], w_lo[:, w % SLOTS, lo_c:hi_c]

            def tile_product(key, w, n, hi, lo, ready=None, later=0, n_later=0):
                outp = acquire(key, later)[:, 0:hi.shape[2]]
                pe.wait_ge(chunk_done, n + 1 + n_later)
                for k in range(KD):
                    if ready:
                        ready(k)
                    ins = product(outp, weights(w, k * P, k * P + P), (hi[:, k, :], lo[:, k, :]), k == 0, k == KD - 1)
                fill(ins, key)

            def sum_squares(e, j):
                q = SQ0[e] + j
                buf = (sq if e < EV["x1"] else sq_b)[q % 2]
                if j == 0 and e > 0:
                    pe.wait_ge(var_ready, e)
                pe.wait_ge(sq_ready, q + 1)
                for t in range(EVENTS[e][2]):
                    ins = pe.matmul(ps[:, 7, t:t + 1], buf[:, t * P:t * P + P], ones[:, 0:1],
                                    start=(j == 0 and t == 0), stop=(j == EVENTS[e][1] - 1), skip_group_check=True)
                ins.then_inc(sq_summed, 1)

            def spread(e):
                pe.wait_ge(diag_ready, BC[e] + 1)
                src = diag if e < EV["x1"] else diag_b
                for t, (bank, col) in enumerate(event_tiles(e)):
                    ins = pe.matmul(ps[:, bank, col:col + P], ones[:], src[:, t, :], start=True, stop=True)
                ins.then_inc(scale_spread, 1)

            def rotate(name, src):
                r = ROTS.index(name)
                if r:
                    pe.wait_ge(rot_used, r)
                m = TAB["rotm" if name[1] == "r" else "rotg"]
                pe.matmul(ps[:, 4, :], tab[:, m:m + P], src, start=True, stop=True).then_inc(rotated, 1)

            def mod_columns(key, acc, later=0):
                outp = acquire(key, later)
                for j in range(4):
                    for k2 in range(2):
                        ins = pe.matmul(outp[:, j:j + 1], acc[:, k2, j * P:j * P + P], ones[:, 0:1],
                                        start=(j == 0 and k2 == 0), stop=(k2 == 1), skip_group_check=True)
                fill(ins, key)

            pe.wait_ge(consts_set, 3)
            for j in range(KD):
                sum_squares(EV["x0"], j)
            spread(EV["x0"])
            for j in range(KD):
                sum_squares(EV["ctx0"], j)
            spread(EV["ctx0"])
            pe.wait_ge(silu_done, 1)
            for b in range(4):
                pe.wait_ge(head_landed[b], 16)
                for k in range(KD):
                    ins = pe.matmul(ps[0:2, b, :], c_act[:, 2 * k:2 * k + 2],
                                    mod_head[:, 4 * b + k // 2, (k % 2) * BLOCK:(k % 2 + 1) * BLOCK],
                                    start=(k == 0), stop=(k == KD - 1))
                fill(ins, ("row", b))
            for j in range(2 * KD):
                if j % 4 == 0:
                    pe.wait_ge(drained[j // 4], 1)
                ins = pe.transpose(ps[:, 4, 2 * j:2 * j + 2],
                                   mod_acc0[0:2, j // 8, j // 4 % 2, j % 4 * P:j % 4 * P + P], ident[0:2, 0:2])
            fill(ins, "mod columns x")

            def kept(key):
                bank, use = AT[key]
                pe.wait_ge(drained[bank], use)

            def between(t):
                if t in (1, 2):
                    sum_squares(EV["ckv"], t - 1)
                if t == 3:
                    spread_after(EV["ckv"], t_ready, 2 * KD)
                    kept(("pc", 2))
                    rotate("kr", kr_raw[:, CTX:KEYS])
                if t == 4:
                    sum_squares(EV["kg0"], 0)
                if t == 5:
                    spread_after(EV["kg0"], ckv_scaled, KKV)
                    sum_squares(EV["kg1"], 0)
                if t == 6:
                    pe.wait_ge(knx_ready, 1)
                    rotate("kg0", knx[:])
                    spread_after(EV["kg1"], knx_ready, 1)
                if t == 7:
                    pe.wait_ge(knx_ready, 2)
                    rotate("kg1", knx[:])
                if 8 <= t < 12:
                    sum_squares(EV["cq"], t - 8)
                if 12 <= t < 16:
                    i = t - 12
                    sum_squares(EV[f"gq{i}"], 0)
                    kept(("px", 11 + i))
                    rotate(f"gq{i}", q_raw[:, i % 2, :])

            def spread_after(e, used, count):
                pe.wait_ge(used, count)
                spread(e)

            for t, name in enumerate(PROJ):
                if name[0] == "v":
                    acquire(("px", t))
                    acquire(("pc", t))
                    pe.wait_ge(chunk_done, t + 1)
                    for key, hi, lo, tiles in ((("px", t), h_hi, h_lo, TX), (("pc", t), hc_hi, hc_lo, TC)):
                        for tt in range(tiles):
                            cols = slice(tt * P, tt * P + P)
                            for k in range(KD):
                                ins = product(bank_of(key)[:, cols], (hi[:, k, cols], lo[:, k, cols]),
                                              weights(t, k * P, k * P + P), k == 0, k == KD - 1)
                        fill(ins, key)
                else:
                    tile_product(("px", t), t, t, h_hi, h_lo, (lambda k: pe.wait_ge(h_ready, k + 1)) if t == 0 else None)
                    if t < BOTH:
                        tile_product(("pc", t), t, t, hc_hi, hc_lo,
                                     (lambda k: pe.wait_ge(h_ready, KD + k + 1)) if t == 0 else None)
                between(t)

            pe.wait_ge(drained[AT[("px", 10)][0]], AT[("px", 10)][1])
            for n in range(3):
                pe.wait_ge(chunk_done, UQ0 + n + 1)
                for i in range(2):
                    outp = acquire(("uq", n, i))
                    for k in range(KQ):
                        c = (i * KQ + k) * P
                        ins = product(outp, weights(UQ0 + n, c, c + P), (cq_hi[:, k, :], cq_lo[:, k, :]), k == 0,
                                      k == KQ - 1)
                    fill(ins, ("uq", n, i))
                if n == 0:
                    between(15)
            pe.wait_ge(ckv_ready, KKV)
            pe.wait_ge(knx_ready, 2)
            pe.wait_ge(chunk_done, UKK + 1)
            for n in range(2):
                ctx_bank = acquire(("kc", n))
                for h in (2 * n, 2 * n + 1):
                    outp = acquire(("kx", h))
                    for k in range(KKV):
                        c = (h * KKV + k) * P
                        ins = product(outp, weights(UKK, c, c + P), (ckv_hi[:, k, CTX:KEYS], ckv_lo[:, k, CTX:KEYS]),
                                      k == 0, k == KKV - 1)
                    fill(ins, ("kx", h))
                for h in (2 * n, 2 * n + 1):
                    for k in range(KKV):
                        c = (h * KKV + k) * P
                        ins = product(ctx_bank[:, h % 2 * CTX:h % 2 * CTX + CTX], weights(UKK, c, c + P),
                                      (ckv_hi[:, k, 0:CTX], ckv_lo[:, k, 0:CTX]), k == 0, k == KKV - 1)
                fill(ins, ("kc", n))
                kept(("uq", 2, n))
                rotate(f"qr{n}", q_raw[:, n, :])
            pe.wait_ge(chunk_done, UKV + 1)
            for t in range(TK):
                outp = acquire(("v", t))
                cols = slice(t * P, t * P + P)
                for k in range(KKV):
                    ins = product(outp, (ckv_hi[:, k, cols], ckv_lo[:, k, cols]),
                                  weights(UKV, k * BLOCK, (k + 1) * BLOCK), k == 0, k == KKV - 1)
                fill(ins, ("v", t))

            kept(("v", TK - 1))
            pe.wait_ge(rot_used, len(ROTS))
            for s in range(4 * HEADS + 3):
                if s < 4 * HEADS:
                    h, qt, pair = s // 4, s % 4, 2 * (s % 2)
                    q_cols = slice(qt * P, qt * P + P)
                    if s >= 2:
                        pe.wait_ge(exp_done, s - 1)
                    for half in range(2):
                        keys = slice(half * 384, half * 384 + 384)
                        outp = ps[:, pair + half, 0:384]
                        if h < MLA_HEADS:
                            pe.matmul(outp, qn[:, h, q_cols], kn[:, h, keys], start=True, stop=False)
                            ins = pe.matmul(outp, qr[:, h // 2, q_cols], (kr_odd if h % 2 else kr_even)[:, keys],
                                            start=False, stop=True)
                        else:
                            g = h - MLA_HEADS
                            ins = pe.matmul(outp, gq[:, g, q_cols], kg[:, g // 2, keys], start=True, stop=True)
                    ins.then_inc(scored, 1)
                if 2 <= s < 4 * HEADS + 2:
                    n = s - 2
                    pe.wait_ge(probs_ready, n + 1)
                    if n:
                        pe.wait_ge(turned_copied, n)
                    for kt in range(TK):
                        ins = pe.transpose(ps[:, 4 + kt // 3, kt % 3 * P:kt % 3 * P + P],
                                           probs[:, n % 3, kt * P:kt * P + P], ident)
                    ins.then_inc(turned, 1)
                if s >= 5 and s % 4 == 1:
                    b = (s - 5) // 4
                    pe.wait_ge(chunk_done, NW_IN + 4 * b + 4)
                    mod_columns(("mc0", b), mod_acc0[:, b % 2])
                if s >= 6 and s % 4 == 2:
                    h = (s - 6) // 4
                    outp = acquire(("pv", h))
                    pe.wait_ge(turned_copied, 4 * h + 4)
                    for kt in range(TK):
                        g = (h - MLA_HEADS) // 2
                        val = vm[:, kt, h * P:h * P + P] if h < MLA_HEADS else vg[:, kt, g * P:g * P + P]
                        ins = pe.matmul(outp, val, probs_t[:, h % 2, kt, :], start=(kt == 0), stop=(kt == TK - 1))
                    fill(ins, ("pv", h))

            pe.wait_ge(exp_done, 4 * HEADS)
            for j in range(KD):
                tile_product(("wo", j), W_WOUT + j, N_WOUT + j, h_hi, h_lo,
                             (lambda k: kept(("pv", k))) if j == 0 else None)
                if j == 2:
                    pe.wait_ge(drained[7], AT[("mc0", 7)][1])
                if j >= 2:
                    sum_squares(EV["x1"], j - 2)
            sum_squares(EV["x1"], KD - 2)
            sum_squares(EV["x1"], KD - 1)
            spread_after(EV["x1"], turned_copied, 4 * HEADS)

            def mlp(l, i, last):
                n0, w0 = (N_MLP0, W_MLP0) if l == 0 else (N_MLP1, W_MLP1)
                w_at, m_at = mlp_offsets(l)
                per = len(w_at) + len(m_at)
                e = EV["x2" if l == 0 else "x4"]
                normed = (2 if l == 0 else 4) * KD
                for s in range(MLP_W):
                    key = ("mlp", l, s)
                    ready = None
                    if s == 0:
                        def ready(k):
                            pe.wait_ge(h_ready, normed + k + 1)
                    if s == KD:
                        def ready(k):
                            pe.wait_ge(hid_ready, l * FFG * KD + k + 1 + KD * i)
                    hi, lo = (h_hi, h_lo) if s < KD else (hid_hi, hid_lo)
                    tile_product(key, w0 + s, n0 + w_at[s], hi, lo, ready, PER[l][s % 4] * i, per * i)
                    if l == 0 and s in (5, 9, 13):
                        b = (s - 5) // 4
                        pe.wait_ge(chunk_done, n0 + m_at[4 * b + 3] + 1 + per * i)
                        mod_columns(("mc1", b), mod_acc1[:, b], PER[0][6] * i)
                    if last and s >= KD + 2:
                        sum_squares(e, s - KD - 2)
                if last:
                    sum_squares(e, KD - 2)
                    sum_squares(e, KD - 1)

            with pe.Fori(0, FFG - 1) as i:
                mlp(0, i, False)
            mlp(0, FFG - 1, True)
            spread(EV["x2"])

            def channel_dft(g):
                kept(("fi", FI.index(f"f{g}")))
                for b in range(2):
                    outp = acquire(("f1", g, b))
                    for t in (2 * b, 2 * b + 1):
                        ins = pe.matmul(outp[:, t % 2 * 2 * P:(t % 2 + 1) * 2 * P], f_t[:, g, t * P:t * P + P],
                                        cs_small[:], start=True, stop=True)
                    fill(ins, ("f1", g, b))

            for c in range(NFI):
                tile_product(("fi", c), W_FC + c, N_FC + c, h_hi, h_lo,
                             (lambda k: pe.wait_ge(h_ready, 3 * KD + k + 1)) if c == 0 else None)
                if c == 8:
                    pe.wait_ge(dft_landed, 32)
                if c >= 9:
                    channel_dft(c - 9)
            channel_dft(GROUPS - 1)
            for g in range(GROUPS):
                outp = acquire(("f2", g))
                kept(("f1", g, 0))
                kept(("f1", g, 1))
                for part in range(2):
                    for t in range(TX):
                        ins = pe.matmul(outp, f_mid[:, t, g, part * P:part * P + P], cs[:, part, t, :],
                                        start=(part == 0 and t == 0), stop=(part == 1 and t == TX - 1))
                fill(ins, ("f2", g))
            outp = acquire("mean")
            pe.wait_ge(conv_step, KCH * TAPS)
            for i in range(KCH):
                ins = pe.matmul(outp, meanw[:], conv[:, i, :], start=(i == 0), stop=(i == KCH - 1))
            fill(ins, "mean")
            for i in range(KCH):
                sum_squares(EV["ln"], i)
            spread(EV["ln"])

            def mixed(k):
                if k < GROUPS:
                    kept(("f2", k))
                else:
                    pe.wait_ge(mix_ready, k - GROUPS + 1)

            for j in range(KD):
                tile_product(("fo", j), W_FCOUT + j, N_FCOUT + j, h_hi, h_lo, mixed if j == 0 else None)
                if j >= 2:
                    sum_squares(EV["x3"], j - 2)
            sum_squares(EV["x3"], KD - 2)
            sum_squares(EV["x3"], KD - 1)
            spread_after(EV["x3"], y_ready, KCH)
            with pe.Fori(0, FFG - 1) as i:
                mlp(1, i, False)
            mlp(1, FFG - 1, True)
            spread(EV["x4"])


def rope_tables():
    tok = np.arange(SEQ)
    pos = (tok // GRID_W, tok % GRID_W)
    made = []
    for block in (HD // 2, ROPE // 2):
        half = block // 2
        freqs = np.float32(10000.0) ** (-np.arange(half, dtype=np.float32) / np.float32(half))
        cos, sin, rot = np.zeros((P, SEQ), np.float32), np.zeros((P, SEQ), np.float32), np.zeros((P, P), np.float32)
        for d in range(P):
            angle = pos[d // block % 2].astype(np.float32) * freqs[d % half]
            cos[d], sin[d] = np.cos(angle), np.sin(angle)
            if d % block < half:
                rot[d + half, d] = -1.0
            else:
                rot[d - half, d] = 1.0
        made.append((cos, sin, rot))
    (cg, sg, rg), (cm, sm, rm) = made
    return np.concatenate([cg, sg, cm, sm, np.eye(P, dtype=np.float32), rg, rm], axis=1)


def dft_tables():
    def table(n, f):
        k = np.outer(np.arange(n), np.arange(n)) % n
        return f(2 * np.pi * k / n).astype(np.float32)
    big = np.stack([table(SEQ, np.cos), -table(SEQ, np.sin)]).reshape(2, TX, P, SEQ).transpose(2, 0, 1, 3)
    return np.ascontiguousarray(big), np.concatenate([table(P, np.cos), table(P, np.sin)], axis=1)


def columns(a):
    return a.reshape(-1, P).T


def tiles(w):
    k, m = w.shape[0] // P, w.shape[1] // P
    return w.reshape(k, P, m, P).transpose(2, 1, 0, 3).reshape(m, P, k * P)


def mod_blocks(w):
    b = w.shape[1] // BLOCK
    return w.reshape(4, 2, P, b, BLOCK).transpose(3, 0, 2, 1, 4).reshape(b * 4, P, CHUNK)


def lay_out(i):
    w_in, uq, ukv = i["attn_w_in"][0], i["mla_w_uq"][0], i["mla_w_ukv"][0]
    at = np.cumsum([0, Q_RANK, GQA_HEADS * HD, KV_RANK, ROPE, GQA_KV * HD, GQA_KV * HD])
    cq, gq, ckv, kr, kg, vg = (w_in[:, a:b] for a, b in zip(at[:-1], at[1:]))
    proj = np.concatenate([ckv, kr, kr, kg, vg, cq, gq], axis=1)
    uq = uq.reshape(Q_RANK, MLA_HEADS, NOPE + ROPE)
    uq = np.concatenate([uq[:, :, :NOPE].reshape(Q_RANK, -1), uq[:, :, NOPE:].reshape(Q_RANK, -1)], axis=1)
    ukv = ukv.reshape(KV_RANK, MLA_HEADS, 2 * P)
    uq_chunks = tiles(uq).reshape(3, 2, P, KQ * P).transpose(0, 2, 1, 3).reshape(3, P, CHUNK)
    k_chunk = tiles(ukv[:, :, :NOPE].reshape(KV_RANK, -1)).transpose(1, 0, 2).reshape(1, P, CHUNK)
    v_chunk = ukv[:, :, NOPE:].reshape(KKV, P, MLA_HEADS * P).transpose(1, 0, 2).reshape(1, P, CHUNK)
    fc = i["fc_w_in"][0]
    order = np.concatenate([np.concatenate([np.arange(P) + GATE_AT + g * P, np.arange(P) + CH + g * P])
                            for g in range(KCH)] + [np.arange(CH)])
    vectors = [columns(i["norm1_g"]), columns(i["norm2_g"]), columns(i["final_g"]), columns(i["mod_b"]),
               columns(i["mla_q_norm_g"]), columns(i["mla_kv_norm_g"]), columns(i["gqa_q_norm_g"]),
               columns(i["gqa_k_norm_g"]), columns(i["conv_b"]), columns(i["conv_ln_g"]), columns(i["conv_ln_b"]),
               i["conv_w"][0].reshape(TAPS, KCH, P).transpose(2, 1, 0).reshape(P, -1)]
    mod = [mod_blocks(w) for w in i["mod_w"]]

    def mlp_chunks(l):
        up = tiles(i["mlp_w1"][l])
        down = [tiles(i["mlp_w2"][l][g * D:(g + 1) * D]) for g in range(FFG)]
        return np.concatenate([part for g in range(FFG) for part in (up[g * KD:(g + 1) * KD], down[g])])

    dft, dft_small = dft_tables()
    return [
        np.stack([i["c"][0], i["c_ctx"]]).reshape(2, KD, P).transpose(2, 1, 0).reshape(P, 2 * KD),
        np.concatenate(vectors, axis=1), rope_tables(), dft, dft_small,
        i["x"][0].T.reshape(KD, P, SEQ), i["ctx"][0].T.reshape(KD, P, CTX),
        mod[0][:16], mod[0][16:], mod[1],
        np.concatenate([tiles(proj), uq_chunks, k_chunk, v_chunk, tiles(i["attn_w_out"][0])]),
        mlp_chunks(0), np.concatenate([tiles(fc[:, order]), tiles(i["fc_w_out"][0])]), mlp_chunks(1),
    ]


def kernel(**inputs):
    import concourse.bacc as bacc
    from concourse.bass_utils import run_bass_kernel_spmd

    nc = bacc.Bacc("TRN2", target_bir_lowering=False, num_devices=1)
    names = ["c_cols", "vectors", "tables", "dft", "dft_small", "x_t", "ctx_t", "mod0_head", "mod0", "mod1", "w_mix0",
             "w_mlp0", "w_fc", "w_mlp1"]
    arrays, args = {}, []
    for name, a in zip(names, lay_out({k: np.asarray(a) for k, a in inputs.items()})):
        arrays[name] = np.ascontiguousarray(a)
        args.append(nc.dram_tensor(name, arrays[name].shape, F32, kind="ExternalInput").ap())
    args.append(nc.dram_tensor("y_t", (KD, P, SEQ), F32, kind="ExternalOutput").ap())
    dit_block_kernel(nc, *args)
    r = run_bass_kernel_spmd(nc, [arrays], core_ids=[0])
    return np.ascontiguousarray(r.results[0]["y_t"].reshape(D, SEQ).T)[None]
```

```python
from contextlib import ExitStack

import numpy as np

import concourse.bass as bass
from concourse import mybir

ACT = mybir.ActivationFunctionType
ALU = mybir.AluOpType
AX = mybir.AxisListType
F32 = mybir.dt.float32
F32R = mybir.dt.float32r

P = 128
D = 1024
KD = D // P
SEQ, CTX = 512, 256
KEYS = CTX + SEQ
TX, TC = SEQ // P, CTX // P
TK = TX + TC
FF = 4 * D
GRID_W = 64
EPS = 1e-6
MLA_HEADS, NOPE, ROPE = 4, 128, 64
GQA_HEADS, GQA_KV, HD = 4, 2, 128
Q_RANK, KV_RANK = D // 2, D // 4
KQ, KKV = Q_RANK // P, KV_RANK // P
MLA_SCALE = float(NOPE + ROPE) ** -0.5
GQA_SCALE = float(HD) ** -0.5
HEADS = MLA_HEADS + GQA_HEADS
GROUPS, CH, TAPS = 4, 512, 31
KCH = CH // P
GATE_AT = 2 * CH
PAD = TAPS // 2
POOL_TAPS = (14, 14, 14, 12)
PRODUCTS = 4

CHUNK = 1024
BLOCK = 512
FFG = 4
STAGES = 4
SLOTS = 2

VEC = {}
_at = 0
for _name, _n in (("n1", 2 * KD), ("n2", 2 * KD), ("nf", KD), ("modb", 2 * 6 * KD), ("qg", KQ), ("kvg", KKV),
                  ("gqg", 1), ("gkg", 1), ("convb", KCH), ("lng", KCH), ("lnb", KCH), ("convw", KCH * TAPS)):
    VEC[_name] = _at
    _at += _n
NVEC = _at
TAB = {"cosg": 0, "sing": 512, "cosm": 1024, "sinm": 1536, "ident": 2048, "rotg": 2176, "rotm": 2304}
NTAB = 2432

PROJ = ["ckv0", "ckv1", "kr", "kg0", "kg1", "v0", "v1", "cq0", "cq1", "cq2", "cq3", "gq0", "gq1", "gq2", "gq3"]
NPROJ = len(PROJ)
BOTH = 7
VALUES = (5, 6)
VALUE_BANKS = (3, 0, 2)
UQ0, UQ1, UQR, UKK, UKV = range(NPROJ, NPROJ + 5)
NW_IN = NPROJ + 5
NM0 = 32
N_IN, N_WOUT = 0, NW_IN + NM0
N_MLP0 = N_WOUT + KD
MLP_W, MLP_M = 16, 12
N_FC = N_MLP0 + FFG * (MLP_W + MLP_M)
NFI = 12
N_FCOUT = N_FC + NFI
N_MLP1 = N_FCOUT + KD
W_WOUT, W_MLP0 = NW_IN, NW_IN + KD
W_FC = W_MLP0 + FFG * MLP_W
W_FCOUT = W_FC + NFI
W_MLP1 = W_FCOUT + KD

FI = ["g0", "a0", "g1", "a1", "g2", "a2", "g3", "a3", "f0", "f1", "f2", "f3"]
ROTS = ["kr", "kg0", "kg1", "gq0", "gq1", "gq2", "gq3", "qr0", "qr1"]
EVENTS = [("x0", KD, TX, D, "x"), ("ctx0", KD, TC, D, "c"), ("ckv", KKV, TK, KV_RANK, "xc"),
          ("kg0", 1, TK, HD, "xc"), ("kg1", 1, TK, HD, "xc"), ("cq", KQ, TX, Q_RANK, ""),
          ("gq0", 1, TX, HD, ""), ("gq1", 1, TX, HD, ""), ("gq2", 1, TX, HD, ""), ("gq3", 1, TX, HD, ""),
          ("x1", KD, TX, D, "x"), ("x2", KD, TX, D, "x"), ("ln", KCH, TX, CH, "x"), ("x3", KD, TX, D, "x"),
          ("x4", KD, TX, D, "x")]
EV = {e[0]: i for i, e in enumerate(EVENTS)}
SQ0 = [sum(e[1] for e in EVENTS[:i]) for i in range(len(EVENTS) + 1)]
BC = [sum(bool(e[4]) for e in EVENTS[:i]) for i in range(len(EVENTS) + 1)]


def event_tiles(e):
    if EVENTS[e][4] == "x" or EVENTS[e][2] == TX:
        return [(5, t * P) for t in range(TX)]
    if EVENTS[e][4] == "c":
        return [(6, t * P) for t in range(TC)]
    return [(6, t * P) for t in range(TC)] + [(5, t * P) for t in range(TX)]


class Ledger:

    def __init__(self):
        self.uses, self.at = [0] * 8, {}

    def use(self, key, bank):
        self.uses[bank] += 1
        self.at[key] = (bank, self.uses[bank])


def plan_taps(quota, rate):
    done, order, last = [0] * KCH, [], None
    for c in range(NFI + 1):
        here = []
        while sum(done) < sum(quota) and (len(here) < rate or c == NFI):
            open_tiles = [i for i in range(KCH) if c >= 2 * i + 2 and done[i] < quota[i]]
            if not open_tiles:
                break
            last = max(open_tiles, key=lambda i: (i != last, quota[i] - done[i]))
            here.append((last, done[last]))
            done[last] += 1
        order.append(here)
    return order


def plan_banks():
    led = Ledger()
    for b in range(4):
        led.use(("row", b), b)
    led.use("mod columns x", 4)
    for t in range(NPROJ):
        if t not in VALUES:
            led.use(("px", t), t % 2)
            if t < BOTH:
                led.use(("pc", t), 2 + t % 2)
        elif t == VALUES[0]:
            for n, b in enumerate(VALUE_BANKS):
                led.use(("vg", n), b)
    for n, (a, b) in enumerate(((2, 3), (0, 1), (2, 3))):
        led.use(("uq", n, 0), a)
        led.use(("uq", n, 1), b)
    for n, (a, b, c) in enumerate(((0, 1, 5), (2, 3, 6))):
        led.use(("kx", 2 * n), a)
        led.use(("kx", 2 * n + 1), b)
        led.use(("kc", n), c)
    for t, b in enumerate((0, 1, 2, 3, 5, 6)):
        led.use(("v", t), b)
    for h in range(HEADS):
        led.use(("pv", h), 6)
    for b in range(8):
        led.use(("mc0", b), 7)
    for j in range(KD):
        led.use(("wo", j), j % 4)
    per = {}

    def mlp(l):
        base = list(led.uses)
        for s in range(MLP_W):
            led.use(("mlp", l, s), s % 4)
        if l == 0:
            for b in range(3):
                led.use(("mc1", b), 6)
        per[l] = [a - b for a, b in zip(led.uses, base)]
        led.uses = [b + FFG * p for b, p in zip(base, per[l])]

    mlp(0)
    for c in range(NFI):
        led.use(("fi", c), c % 4)
    for g in range(GROUPS):
        led.use(("f1", g, 0), 4)
        led.use(("f1", g, 1), 5)
    for g in range(GROUPS):
        led.use(("f2", g), (6, 2, 3, 6)[g])
    led.use("mean", 4)
    for j in range(KD):
        led.use(("fo", j), j % 4)
    mlp(1)
    return led.at, per


def dit_block_kernel(nc, c_cols, vectors, tables, dft, dft_small, x_t, ctx_t, mod0_head, mod0, mod1, w_mix0, w_mlp0,
                     w_fc, w_mlp1, out):
    AT, PER = plan_banks()
    with ExitStack() as life:
        def sb(name, shape, dt=F32, on=life):
            return on.enter_context(nc.sbuf_tensor(name, [P, *shape], dt))

        def sem(name):
            return life.enter_context(nc.semaphore(name))

        ps = life.enter_context(nc.psum_tensor("ps", [P, 8, 512], F32))

        vec = sb("vec", [NVEC])
        tab = sb("tab", [NTAB])
        x = sb("x", [KD, SEQ])
        stage = sb("stage", [STAGES, CHUNK])
        w_hi = sb("w_hi", [SLOTS, CHUNK], F32R)
        w_lo = sb("w_lo", [SLOTS, CHUNK], F32R)
        h_hi = sb("h_hi", [KD, SEQ], F32R)
        h_lo = sb("h_lo", [KD, SEQ], F32R)
        ones = sb("ones", [P])
        meanw = sb("meanw", [P])
        minus_half = sb("minus_half", [TK])
        sq_acc = sb("sq_acc", [SEQ])
        c_in = sb("c_in", [KD * 2])
        c_act = sb("c_act", [KD * 2])
        modA = sb("modA", [2, 2 * KD])
        modG = sb("modG", [2, KD])
        modc0 = sb("modc0", [4 * KD])
        modc1 = sb("modc1", [6 * KD])
        gains = sb("gains", [3, KD])
        var = sb("var", [len(EVENTS), TK])
        rstd = sb("rstd", [len(EVENTS), TK])
        row_scale = sb("row_scale", [1 + GQA_HEADS, TX])
        top = sb("top", [32])
        minus_top = sb("minus_top", [32])
        psum_row = sb("psum_row", [32])
        inv_row = sb("inv_row", [32])
        ident = tab[:, TAB["ident"]:TAB["ident"] + P]

        mix0 = ExitStack()
        with ExitStack() as a:
            mod_head = sb("mod_head", [16, CHUNK], on=a)
        gq = sb("gq", [GQA_HEADS, SEQ], on=mix0)
        kg = sb("kg", [GQA_KV, KEYS], on=mix0)
        kr_even = sb("kr_even", [KEYS], on=mix0)
        kr_odd = sb("kr_odd", [KEYS], on=mix0)
        vg = sb("vg", [TK, GQA_KV * HD], on=mix0)
        with ExitStack() as a:
            cq_hi = sb("cq_hi", [KQ, SEQ], F32R, a)
            cq_lo = sb("cq_lo", [KQ, SEQ], F32R, a)
            ckv_hi = sb("ckv_hi", [KKV, KEYS], F32R, a)
            ckv_lo = sb("ckv_lo", [KKV, KEYS], F32R, a)
        probs_t = sb("probs_t", [2, TK, SEQ], on=mix0)
        sb("gap_a", [1024], on=mix0)
        with ExitStack() as a:
            hc_hi = sb("hc_hi", [KD, CTX], F32R, a)
            hc_lo = sb("hc_lo", [KD, CTX], F32R, a)
            with ExitStack() as b:
                ctx_x = sb("ctx_x", [KD, CTX], on=b)
            ckv_raw = sb("ckv_raw", [KKV, KEYS], on=a)
        qn = sb("qn", [MLA_HEADS, SEQ], on=mix0)
        qr = sb("qr", [2, SEQ], on=mix0)
        kn = sb("kn", [MLA_HEADS, KEYS], on=mix0)
        with ExitStack() as a:
            sq = [sb(f"sq{i}", [KEYS], on=a) for i in range(2)]
            kr_raw = sb("kr_raw", [KEYS], on=a)
            kg_raw = sb("kg_raw", [GQA_KV, KEYS], on=a)
        vm = sb("vm", [TK, MLA_HEADS * P], on=mix0)
        sb("gap_b", [768], on=mix0)
        with ExitStack() as a:
            knx = sb("knx", [SEQ], on=a)
            q_raw = sb("q_raw", [2, SEQ], on=a)
        probs = sb("probs", [3, KEYS], on=mix0)
        with ExitStack() as a:
            tmp = sb("tmp", [3, SEQ], on=a)
        mod_acc0 = sb("mod_acc0", [2, 2, BLOCK], on=mix0)
        mix0.close()

        cs = sb("cs", [2, TX, SEQ])
        cs_small = sb("cs_small", [2 * P])
        sq_b = [sb(f"sq_b{i}", [SEQ]) for i in range(2)]
        tmp_b = sb("tmp_b", [3, SEQ])
        mod_acc1 = sb("mod_acc1", [3, 2, BLOCK])
        with ExitStack() as a:
            hid_hi = sb("hid_hi", [KD, SEQ], F32R, a)
            hid_lo = sb("hid_lo", [KD, SEQ], F32R, a)
            relu = sb("relu", [2, SEQ], on=a)
            relu2 = sb("relu2", [2, SEQ], on=a)
        part = sb("part", [KCH, SEQ])
        product_of_tap = sb("product_of_tap", [PRODUCTS, SEQ])
        f_t = sb("f_t", [GROUPS, SEQ])
        f_mid = sb("f_mid", [TX, GROUPS, 2 * P])
        gate = sb("gate", [2, SEQ])
        u = sb("u", [KCH, SEQ + 2 * PAD])
        conv = sb("conv", [KCH, SEQ])
        cent = sb("cent", [KCH, SEQ])

        c_landed, vec_landed, tab_landed = sem("c_landed"), sem("vec_landed"), sem("tab_landed")
        ident_landed = sem("ident_landed")
        x_landed, ctx_landed, dft_landed = sem("x_landed"), sem("ctx_landed"), sem("dft_landed")
        head_landed = [sem(f"head_landed{b}") for b in range(4)]
        staged = [sem(f"staged{s}") for s in range(STAGES)]
        out_written = sem("out_written")
        consts_set, pads_set = sem("consts_set"), sem("pads_set")
        chunk_done = sem("chunk_done")
        w_high = sem("w_high")
        filled = [sem(f"filled{b}") for b in range(8)]
        drained = [sem(f"drained{b}") for b in range(8)]
        values_half = sem("values_half")
        silu_done = sem("silu_done")
        sq_ready = sem("sq_ready")
        sq_summed = sem("sq_summed")
        mod_summed = sem("mod_summed")
        var_ready, rstd_ready = sem("var_ready"), sem("rstd_ready")
        scale_spread = sem("scale_spread")
        t_ready, hh_ready, h_ready = sem("t_ready"), sem("hh_ready"), sem("h_ready")
        knx_ready, rotated, rot_used = sem("knx_ready"), sem("rotated"), sem("rot_used")
        cq_ready, ckv_scaled, ckvh_ready, ckv_ready = (sem("cq_ready"), sem("ckv_scaled"), sem("ckvh_ready"),
                                                       sem("ckv_ready"))
        scored, top_ready, exp_done, probs_ready = sem("scored"), sem("top_ready"), sem("exp_done"), sem("probs_ready")
        turned, turned_copied, oh_ready = sem("turned"), sem("turned_copied"), sem("oh_ready")
        hidh_ready, hid_ready = sem("hidh_ready"), sem("hid_ready")
        fh_ready, conv_step, cent_ready, y_ready, s_ready, sh_ready, mix_ready = (
            sem("fh_ready"), sem("conv_step"), sem("cent_ready"), sem("y_ready"), sem("s_ready"), sem("sh_ready"),
            sem("mix_ready"))
        tap_ready, tap_added = sem("tap_ready"), sem("tap_added")
        y_tile = sem("y_tile")
        dve_step = sem("dve_step")

        dve_taps = plan_taps([TAPS - n for n in POOL_TAPS], 5)
        pool_taps = plan_taps(POOL_TAPS, 5)

        block = life.enter_context(nc.Block())

        def v(name, n=0, w=1):
            return vec[:, VEC[name] + n:VEC[name] + n + w]

        def bank_of(key):
            return ps[:, AT[key][0], :]

        def staged_value(n, at=0):
            return 16 * (n // STAGES + 1) + at * 16

        def mlp_offsets(l):
            if l:
                return list(range(MLP_W)), []
            return [0, *(2 * s - 1 for s in range(1, 13)), 25, 26, 27], [2 * q + 2 for q in range(MLP_M)]

        @block.sync
        def _(sp):
            sp.dma_start(c_in[:], c_cols).then_inc(c_landed, 16)
            sp.dma_start(x[:], x_t.rearrange("k p t -> p k t")).then_inc(x_landed, 16)
            sp.dma_start(ident, tables[:, TAB["ident"]:TAB["ident"] + P]).then_inc(ident_landed, 16)
            sp.dma_start(vec[:], vectors).then_inc(vec_landed, 16)
            for b in range(4):
                sp.dma_start(mod_head[:, 4 * b:4 * b + 4, :],
                             mod0_head[4 * b:4 * b + 4].rearrange("c p n -> p c n")).then_inc(head_landed[b], 16)
            sp.dma_start(ctx_x[:], ctx_t.rearrange("k p t -> p k t")).then_inc(ctx_landed, 16)

            def load(n, src, later=0):
                if n >= STAGES:
                    sp.wait_ge(chunk_done, n - STAGES + 1 + later)
                sp.dma_start(stage[:, n % STAGES, :], src).then_inc(staged[n % STAGES], 16)

            for w in range(NW_IN):
                load(w, w_mix0[w])
                if w == 1:
                    for lo_c, hi_c in ((0, TAB["ident"]), (TAB["ident"] + P, NTAB)):
                        sp.dma_start(tab[:, lo_c:hi_c], tables[:, lo_c:hi_c]).then_inc(tab_landed, 16)
            for m in range(NM0):
                load(NW_IN + m, mod0[m])
            for j in range(KD):
                load(N_WOUT + j, w_mix0[NW_IN + j])
            bank, use = AT[("wo", 0)]
            sp.wait_ge(drained[bank], use)
            sp.dma_start(cs[:], dft).then_inc(dft_landed, 16)
            sp.dma_start(cs_small[:], dft_small).then_inc(dft_landed, 16)
            for l, (n0, weights) in enumerate(((N_MLP0, w_mlp0), (N_MLP1, w_mlp1))):
                w_at, m_at = mlp_offsets(l)
                per = len(w_at) + len(m_at)
                with sp.Fori(0, FFG) as i:
                    for o in range(per):
                        src = (weights[bass.ds(i * MLP_W + w_at.index(o), 1)] if o in w_at
                               else mod1[bass.ds(i * MLP_M + m_at.index(o), 1)])
                        load(n0 + o, src.rearrange("a p n -> (a p) n"), i * per)
                if l == 0:
                    for c in range(NFI + KD):
                        load(N_FC + c, w_fc[c])
            for k in range(KD):
                sp.wait_ge(y_tile, k + 1)
                sp.dma_start(out[k], x[:, k, :]).then_inc(out_written, 16)
            sp.wait_ge(out_written, 16 * KD)

        @block.gpsimd
        def _(pool):
            pool.memset(ones[:], 1.0).then_inc(consts_set, 1)
            pool.memset(meanw[:], -1.0 / CH).then_inc(consts_set, 1)
            pool.memset(minus_half[:], -0.5).then_inc(consts_set, 1)
            pool.wait_ge(consts_set, 3)

            def inverse_root(e):
                n = EVENTS[e][2]
                pool.wait_ge(var_ready, e + 1)
                pool.tensor_tensor(rstd[:, e, 0:n], var[:, e, 0:n], minus_half[:, 0:n], ALU.pow).then_inc(rstd_ready, 1)

            def add_square(e, j):
                q, width = SQ0[e] + j, (CTX if EVENTS[e][4] == "c" else SEQ)
                buf = (sq if e < EV["x1"] else sq_b)[q % 2][:, 0:width]
                if j == 0 and e:
                    pool.wait_ge(var_ready, e)
                if j:
                    pool.wait_ge(sq_summed, q)
                pool.wait_ge(sq_ready, q + 1)
                if j == 0:
                    ins = pool.tensor_copy(sq_acc[:, 0:width], buf)
                else:
                    ins = pool.tensor_tensor(sq_acc[:, 0:width], sq_acc[:, 0:width], buf, ALU.add)
                ins.then_inc(sq_summed, 1)

            def mean_square(e):
                if EVENTS[e][1] > 2:
                    for j in range(EVENTS[e][1] - 1):
                        add_square(e, j)
                inverse_root(e)

            def halves(acc, chunk, later=0):
                pool.wait_ge(chunk_done, chunk + 1 + later)
                pool.tensor_tensor(acc[:, 0, :], acc[:, 0, :], acc[:, 1, :], ALU.add).then_inc(mod_summed, 1)

            mean_square(EV["x0"])
            mean_square(EV["ctx0"])
            pool.wait_ge(drained[3], 1)
            pool.wait_ge(rstd_ready, EV["ctx0"] + 1)
            pool.memset(kr_even[ROPE:P, :], 0.0).then_inc(pads_set, 1)
            pool.memset(kr_odd[0:ROPE, :], 0.0).then_inc(pads_set, 1)
            pool.wait_ge(pads_set, 2)
            for e in range(EV["ckv"], EV["ln"]):
                if e == EV["x1"]:
                    for b in range(KD):
                        halves(mod_acc0[:, b % 2], NW_IN + 4 * b + 3)
                if e < EV["x2"]:
                    mean_square(e)
                else:
                    at = [N_MLP0 + mlp_offsets(0)[1][4 * b + 3] for b in range(3)]
                    per = MLP_W + MLP_M
                    with pool.Fori(0, FFG - 1) as i:
                        for b in range(3):
                            halves(mod_acc1[:, b], at[b], per * i)
                    for b in range(3):
                        halves(mod_acc1[:, b], at[b], per * (FFG - 1))
                    mean_square(e)
                    pool.memset(u[:, :, 0:PAD], 0.0).then_inc(pads_set, 1)
                    pool.memset(u[:, :, PAD + SEQ:SEQ + 2 * PAD], 0.0).then_inc(pads_set, 1)
                    pool.wait_ge(pads_set, 4)
            ready, added, last = 0, 0, {}
            for i, n in sum(pool_taps, []):
                ready += 1
                if n:
                    pool.wait_ge(tap_ready, ready)
                    if n > 1:
                        pool.wait_ge(tap_added, last[i])
                    pool.tensor_tensor(part[:, i, :], part[:, i, :], product_of_tap[:, added % PRODUCTS, :],
                                       ALU.add).then_inc(tap_added, 1)
                    added += 1
                    last[i] = added
            for e in range(EV["ln"], len(EVENTS)):
                mean_square(e)

        @block.scalar
        def _(act):
            def full(key, later=0):
                bank, use = AT[key]
                act.wait_ge(filled[bank], use + later)
                return ps[:, bank, :]

            def free(ins, key):
                ins.then_inc(drained[AT[key][0]], 1)

            def split_high(n, w, slot_key, staged_later=0, key_later=0):
                act.wait_ge(staged[n % STAGES], 16 * (n // STAGES + 1) + staged_later)
                if slot_key is not None:
                    full(slot_key, key_later)
                act.activation(w_hi[:, w % SLOTS, :], stage[:, n % STAGES, :], ACT.Copy).then_inc(w_high, 1)

            def square(q, in_ap):
                buf = (sq if q < SQ0[EV["x1"]] else sq_b)[q % 2]
                if q >= 2:
                    act.wait_ge(sq_summed, q - 1)
                return act.activation(buf[:, 0:in_ap.shape[1]], in_ap, ACT.Square)

            def modulated_high(a, shift, hi, width, t):
                for k in range(KD):
                    act.wait_ge(t_ready, a * KD + k + 1)
                    act.activation(hi[:, k, :], t[:, (a * KD + k) % 3, 0:width], ACT.Identity,
                                   bias=shift[:, k:k + 1]).then_inc(hh_ready, 1)

            def square_x(event, k, key):
                bank, use = AT[key]
                act.wait_ge(drained[bank], use)
                square(SQ0[EV[event]] + k, x[:, k, :]).then_inc(sq_ready, 1)

            act.wait_ge(c_landed, 16)
            act.activation(c_act[:], c_in[:], ACT.Silu).then_inc(silu_done, 1)
            act.wait_ge(x_landed, 16)
            for k in range(KD):
                square(SQ0[EV["x0"]] + k, x[:, k, :]).then_inc(sq_ready, 1)
            for b in range(4):
                act.activation(mod_acc0[0:2, b // 2, b % 2, :], full(("row", b))[0:2, :],
                               ACT.Copy).then_inc(drained[b], 1)
            split_high(0, 0, None)
            split_high(1, 1, None)
            modulated_high(0, modA[:, 0, :], h_hi, SEQ, tmp)
            act.wait_ge(ctx_landed, 16)
            for k in range(KD):
                square(SQ0[EV["ctx0"]] + k, ctx_x[:, k, :]).then_inc(sq_ready, 1)
            modulated_high(1, modA[:, 1, :], hc_hi, CTX, tmp)

            for t, name in enumerate(PROJ):
                if t == VALUES[1]:
                    act.wait_ge(values_half, 1)
                    split_high(t + 1, t + 1, None)
                elif t == VALUES[1] + 1:
                    split_high(t + 1, t + 1, ("vg", TK // 2 - 1))
                elif t >= 1:
                    split_high(t + 1, t + 1, ("px", t - 1))
                if t == 5:
                    for i in range(KKV):
                        act.wait_ge(ckv_scaled, i + 1)
                        act.activation(ckv_hi[:, i, :], ckv_raw[:, i, :], ACT.Copy).then_inc(ckvh_ready, 1)
                if t == VALUES[0]:
                    continue
                if t == VALUES[1]:
                    for n in range(TK // 2):
                        first = (TC + 2 * n) % TK
                        free(act.activation(vg[:, first:first + 2, :],
                                            full(("vg", n)).rearrange("p (t c) -> p t c", t=2), ACT.Copy), ("vg", n))
                    continue
                px = full(("px", t))
                if t < BOTH:
                    pc = full(("pc", t))[:, 0:CTX]
                if name in ("ckv0", "ckv1", "kg0", "kg1"):
                    i = int(name[-1])
                    raw = (ckv_raw if name[0] == "c" else kg_raw)[:, i, :]
                    q = SQ0[EV["ckv"]] + i if name[0] == "c" else SQ0[EV[name]]
                    act.activation(raw[:, CTX:KEYS], px, ACT.Copy)
                    act.wait_ge(sq_summed, q - 1)
                    free(act.activation(sq[q % 2][:, CTX:KEYS], px, ACT.Square), ("px", t))
                    free(act.activation(raw[:, 0:CTX], pc, ACT.Copy), ("pc", t))
                    act.wait_ge(drained[AT[("pc", t)][0]], AT[("pc", t)][1])
                    act.activation(sq[q % 2][:, 0:CTX], raw[:, 0:CTX], ACT.Square).then_inc(sq_ready, 1)
                elif name == "kr":
                    free(act.activation(kr_raw[:, CTX:KEYS], px, ACT.Copy), ("px", t))
                    free(act.activation(kr_raw[:, 0:CTX], pc, ACT.Copy), ("pc", t))
                elif name[:2] == "cq":
                    i = int(name[2])
                    act.activation(cq_hi[:, i, :], px, ACT.Copy, scale=v("qg", i))
                    square(SQ0[EV["cq"]] + i, px).then_inc(sq_ready, 1)
                else:
                    i = int(name[2])
                    square(SQ0[EV[name]], px).then_inc(sq_ready, 1)
                    if i >= 2:
                        act.wait_ge(rot_used, ROTS.index(name) - 1)
                    free(act.activation(q_raw[:, i % 2, :], px, ACT.Copy, scale=v("gqg")), ("px", t))

            split_high(UQ0 + 1, UQ0 + 1, ("px", NPROJ - 1))
            for i in range(2):
                free(act.activation(qn[:, i, :], full(("uq", 0, i)), ACT.Copy), ("uq", 0, i))
            split_high(UQR, UQR, ("uq", 0, 1))
            for i in range(2):
                free(act.activation(qn[:, 2 + i, :], full(("uq", 1, i)), ACT.Copy), ("uq", 1, i))
            split_high(UKK, UKK, ("uq", 1, 1))
            for i in range(2):
                act.wait_ge(rot_used, ROTS.index(f"qr{i}") - 1)
                free(act.activation(q_raw[:, i, :], full(("uq", 2, i)), ACT.Copy), ("uq", 2, i))
            split_high(UKV, UKV, ("uq", 2, 1))
            for n in range(2):
                for h in (2 * n, 2 * n + 1):
                    free(act.activation(kn[:, h, CTX:KEYS], full(("kx", h)), ACT.Copy), ("kx", h))
                free(act.activation(kn[:, 2 * n:2 * n + 2, 0:CTX],
                                    full(("kc", n)).rearrange("p (h t) -> p h t", t=CTX), ACT.Copy), ("kc", n))
            for t in range(TK):
                free(act.activation(vm[:, t, :], full(("v", t)), ACT.Copy), ("v", t))

            for s in range(4 * HEADS + 4):
                if s >= 7 and s % 4 == 3:
                    h = (s - 7) // 4
                    act.activation(h_hi[:, h, :], full(("pv", h)), ACT.Copy).then_inc(oh_ready, 1)
                if 2 <= s < 4 * HEADS + 2:
                    n = s - 2
                    h, qt = n // 4, n % 4
                    act.wait_ge(turned, n + 1)
                    act.activation(probs_t[:, h % 2, :, qt * P:qt * P + P].rearrange("p (a b) c -> p a b c", a=2),
                                   ps[:, 4:6, 0:3 * P].rearrange("p a (b c) -> p a b c", c=P),
                                   ACT.Copy).then_inc(turned_copied, 1)
                if s < 4 * HEADS:
                    h, qt = s // 4, s % 4
                    pair = 2 * (s % 2)
                    act.wait_ge(top_ready, s + 1)
                    if s >= 3:
                        act.wait_ge(turned, s - 2)
                    head_scale = row_scale[:, max(h - MLA_HEADS + 1, 0), qt:qt + 1]
                    act.activation(probs[:, s % 3, :].rearrange("p (a b) -> p a b", a=2), ps[:, pair:pair + 2, 0:384],
                                   ACT.Exp, bias=minus_top[:, s:s + 1], scale=head_scale,
                                   accum_out=psum_row[:, s:s + 1]).then_inc(exp_done, 1)

            split_high(N_WOUT, W_WOUT, ("v", TK - 1))
            split_high(N_WOUT + 1, W_WOUT + 1, ("v", TK - 1))
            for j in range(KD):
                n, w = (N_WOUT + j + 2, W_WOUT + j + 2) if j < KD - 2 else (N_MLP0 + j - KD + 2, W_MLP0 + j - KD + 2)
                split_high(n, w, ("wo", j))
                if j >= 1:
                    square_x("x1", j - 1, ("wo", j - 1))
            square_x("x1", KD - 1, ("wo", KD - 1))
            modulated_high(2, modc0[:, KD:2 * KD], h_hi, SEQ, tmp_b)

            def mlp(l, i, last):
                n0, w0 = (N_MLP0, W_MLP0) if l == 0 else (N_MLP1, W_MLP1)
                w_at, m_at = mlp_offsets(l)
                per = len(w_at) + len(m_at)
                for s in range(MLP_W):
                    o = w_at[s + 2] if s + 2 < MLP_W else per + s + 2 - MLP_W
                    if not (last and l == 1 and s + 2 >= MLP_W):
                        split_high(n0 + o, w0 + s + 2, ("mlp", l, s), 16 * per // STAGES * i, PER[l][s % 4] * i)
                    if s < KD:
                        key = ("mlp", l, s)
                        p = full(key, PER[l][s % 4] * i)
                        if s >= 2:
                            act.wait_ge(hid_ready, l * FFG * KD + s - 1 + KD * i)
                        free(act.activation(relu[:, s % 2, :], p, ACT.Relu), key)
                        act.wait_ge(drained[AT[key][0]], AT[key][1] + PER[l][s % 4] * i)
                        act.activation(hid_hi[:, s, :], relu[:, s % 2, :], ACT.Square).then_inc(hidh_ready, 1)
                    elif last and s > KD:
                        bank, use = AT[("mlp", l, s - 1)]
                        act.wait_ge(drained[bank], use + PER[l][bank] * i)
                        square(SQ0[EV["x2" if l == 0 else "x4"]] + s - KD - 1, x[:, s - KD - 1, :]).then_inc(sq_ready, 1)
                if last:
                    bank, use = AT[("mlp", l, MLP_W - 1)]
                    act.wait_ge(drained[bank], use + PER[l][bank] * i)
                    square(SQ0[EV["x2" if l == 0 else "x4"]] + KD - 1, x[:, KD - 1, :]).then_inc(sq_ready, 1)

            with act.Fori(0, FFG - 1) as i:
                mlp(0, i, False)
            mlp(0, FFG - 1, True)

            modulated_high(3, modc1[:, 0:KD], h_hi, SEQ, tmp_b)
            adds = [0]

            def tap_products(c):
                for i, n in pool_taps[c]:
                    w = v("convw", i * TAPS + TAPS - POOL_TAPS[i] + n)
                    src = u[:, i, TAPS - POOL_TAPS[i] + n:TAPS - POOL_TAPS[i] + n + SEQ]
                    if n == 0:
                        bank, use = AT[("fi", FI.index(f"a{i}"))]
                        act.wait_ge(drained[bank], use)
                        act.wait_ge(pads_set, 4)
                        dst = part[:, i, :]
                    else:
                        if adds[0] >= PRODUCTS:
                            act.wait_ge(tap_added, adds[0] - PRODUCTS + 1)
                        dst = product_of_tap[:, adds[0] % PRODUCTS, :]
                        adds[0] += 1
                    act.activation(dst, src, ACT.Copy, scale=w).then_inc(tap_ready, 1)

            for c, name in enumerate(FI):
                split_high(N_FC + c + 2, W_FC + c + 2, ("fi", c))
                key = ("fi", c)
                i = int(name[1])
                if name[0] == "g":
                    if i >= 2:
                        bank, use = AT[("fi", FI.index(f"a{i - 2}"))]
                        act.wait_ge(drained[bank], use)
                    free(act.activation(gate[:, i % 2, :], full(key), ACT.Sigmoid), key)
                elif name[0] == "f":
                    free(act.activation(f_t[:, i, :], full(key), ACT.Copy), key)
                    if i >= 1:
                        for b in range(2):
                            free(act.activation(f_mid[:, 2 * b:2 * b + 2, i - 1, :],
                                                full(("f1", i - 1, b)).rearrange("p (t c) -> p t c", t=2),
                                                ACT.Copy), ("f1", i - 1, b))
                tap_products(c)
            tap_products(NFI)
            for b in range(2):
                free(act.activation(f_mid[:, 2 * b:2 * b + 2, GROUPS - 1, :],
                                    full(("f1", GROUPS - 1, b)).rearrange("p (t c) -> p t c", t=2),
                                    ACT.Copy), ("f1", GROUPS - 1, b))
            for g in range(GROUPS):
                act.activation(h_hi[:, g, :], full(("f2", g)), ACT.Copy,
                               scale=float((SEQ * P) ** -0.5)).then_inc(fh_ready, 1)
                if g == 1:
                    for i in range(KCH):
                        act.wait_ge(cent_ready, i + 1)
                        square(SQ0[EV["ln"]] + i, cent[:, i, :]).then_inc(sq_ready, 1)
            for i in range(KCH + 1):
                if i < KCH:
                    act.wait_ge(y_ready, i + 1)
                    act.activation(conv[:, i, :], cent[:, i, :], ACT.Silu, bias=v("lnb", i),
                                   scale=v("lng", i)).then_inc(s_ready, 1)
                if i >= 1:
                    act.wait_ge(s_ready, i)
                    act.activation(h_hi[:, KCH + i - 1, :], conv[:, i - 1, :], ACT.Copy).then_inc(sh_ready, 1)
            for j in range(KD):
                n, w = (N_FCOUT + j + 2, W_FCOUT + j + 2) if j < KD - 2 else (N_MLP1 + j - KD + 2, W_MLP1 + j - KD + 2)
                split_high(n, w, ("fo", j))
                if j >= 1:
                    square_x("x3", j - 1, ("fo", j - 1))
            square_x("x3", KD - 1, ("fo", KD - 1))
            modulated_high(4, modc1[:, 3 * KD:4 * KD], h_hi, SEQ, tmp_b)
            with act.Fori(0, FFG - 1) as i:
                mlp(1, i, False)
            mlp(1, FFG - 1, True)

        @block.vector
        def _(dve):
            own = [0]

            def tick(ins):
                ins.then_inc(dve_step, 1)
                own[0] += 1
                return own[0]

            def own_wait(count, later=0):
                dve.wait_ge(dve_step, count + later)

            def full(key, later=0):
                bank, use = AT[key]
                dve.wait_ge(filled[bank], use + later)
                return ps[:, bank, :]

            def free(ins, key):
                ins.then_inc(drained[AT[key][0]], 1)

            def split_low(n, w, w_later=0, n_later=0):
                dve.wait_ge(w_high, w + 1 + w_later)
                dve.tensor_tensor(w_lo[:, w % SLOTS, :], stage[:, n % STAGES, :],
                                  w_hi[:, w % SLOTS, :].bitcast(F32), ALU.subtract).then_inc(chunk_done, 1)

            def mod_chunk(n, block_acc, q, staged_later=0, n_before=None, n_later=0):
                dve.wait_ge(staged[n % STAGES], 16 * (n // STAGES + 1) + staged_later)
                if q:
                    dve.wait_ge(chunk_done, n_before + 1 + n_later)
                for k2 in range(2):
                    k = 2 * q + k2
                    src = stage[:, n % STAGES, k2 * BLOCK:(k2 + 1) * BLOCK]
                    acc = block_acc[:, k2, :]
                    if q == 0:
                        ins = dve.tensor_scalar(acc, src, c_act[:, 2 * k:2 * k + 1], None, ALU.mult)
                    else:
                        ins = dve.scalar_tensor_tensor(out=acc, in0=src, scalar=c_act[:, 2 * k:2 * k + 1], in1=acc,
                                                       op0=ALU.mult, op1=ALU.add)
                ins.then_inc(chunk_done, 1)

            def variance(e):
                n, width = EVENTS[e][2], EVENTS[e][3]
                dve.wait_ge(sq_summed, SQ0[e + 1])
                dve.tensor_scalar(var[:, e, 0:n], ps[:, 7, 0:n], 1.0 / width, EPS, ALU.mult, ALU.add) \
                    .then_inc(var_ready, 1)

            def modulated(a, e, src, gain, shift, hi, lo, width, bank, t):
                dve.wait_ge(scale_spread, BC[e] + 1)
                for k in range(KD + 1):
                    if k < KD:
                        if a * KD + k - 2 > 0:
                            dve.wait_ge(h_ready, a * KD + k - 2)
                        ins = dve.scalar_tensor_tensor(out=t[:, (a * KD + k) % 3, 0:width], in0=src[:, k, :],
                                                       scalar=gain[:, k:k + 1], in1=ps[:, bank, 0:width],
                                                       op0=ALU.mult, op1=ALU.mult).then_inc(t_ready, 1)
                    if k >= 1:
                        dve.wait_ge(hh_ready, a * KD + k)
                        dve.scalar_tensor_tensor(out=lo[:, k - 1, :], in0=t[:, (a * KD + k - 1) % 3, 0:width],
                                                 scalar=shift[:, k - 1:k], in1=hi[:, k - 1, :].bitcast(F32),
                                                 op0=ALU.add, op1=ALU.subtract).then_inc(h_ready, 1)

            def add_product(key, k, g, later=0):
                p = full(key, later)
                free(dve.scalar_tensor_tensor(out=x[:, k, :], in0=p, scalar=g, in1=x[:, k, :], op0=ALU.mult,
                                              op1=ALU.add), key)

            def rope(name, src, x_ready, dsts):
                r = ROTS.index(name)
                c, s = ("cosm", "sinm") if name[1] == "r" else ("cosg", "sing")
                x_ready()
                if r:
                    dve.wait_ge(rot_used, r)
                else:
                    dve.wait_ge(h_ready, 2 * KD)
                dve.tensor_tensor(tmp[:, 0, :], src, tab[:, TAB[c]:TAB[c] + SEQ], ALU.mult)
                dve.wait_ge(rotated, r + 1)
                done = tick(dve.tensor_tensor(tmp[:, 1, :], ps[:, 4, :], tab[:, TAB[s]:TAB[s] + SEQ], ALU.mult))
                own_wait(done)
                for dst, lo_p, hi_p in dsts:
                    ins = dve.tensor_tensor(dst, tmp[lo_p:hi_p, 0, :], tmp[lo_p:hi_p, 1, :], ALU.add)
                ins.then_inc(rot_used, 1)

            def drained_key(key):
                bank, use = AT[key]
                return lambda: dve.wait_ge(drained[bank], use)

            dve.wait_ge(consts_set, 3)
            variance(EV["x0"])
            dve.wait_ge(vec_landed, 16)
            cols = full("mod columns x")[:, 0:4 * KD].rearrange("p (j s) -> p s j", s=2)
            for s in range(2):
                ins = dve.tensor_tensor(modA[:, s, :], cols[:, s, :], v("modb", 0, 2 * KD), ALU.add)
            free(ins, "mod columns x")
            drained_key("mod columns x")()
            for s in range(2):
                done = tick(dve.scalar_tensor_tensor(out=modG[:, s, :], in0=modA[:, s, KD:2 * KD], scalar=1.0,
                                                     in1=v("n1", 0, KD), op0=ALU.add, op1=ALU.mult))
            own_wait(done)
            split_low(0, 0)
            split_low(1, 1)
            modulated(0, EV["x0"], x, modG[:, 0, :], modA[:, 0, :], h_hi, h_lo, SEQ, 5, tmp)
            variance(EV["ctx0"])
            modulated(1, EV["ctx0"], ctx_x, modG[:, 1, :], modA[:, 1, :], hc_hi, hc_lo, CTX, 6, tmp)

            def kr_rope():
                dve.wait_ge(tab_landed, 32)
                dve.wait_ge(pads_set, 2)
                drained_key(("pc", 2))()
                dve.tensor_copy(kr_even[0:ROPE, 0:CTX], kr_raw[0:ROPE, 0:CTX])
                dve.tensor_copy(kr_odd[ROPE:P, 0:CTX], kr_raw[ROPE:P, 0:CTX])
                rope("kr", kr_raw[:, CTX:KEYS], drained_key(("pc", 2)),
                     [(kr_even[0:ROPE, CTX:KEYS], 0, ROPE), (kr_odd[ROPE:P, CTX:KEYS], ROPE, P)])

            def scale_ckv():
                dve.wait_ge(scale_spread, BC[EV["ckv"]] + 1)
                for i in range(KKV):
                    for bank, lo_t, hi_t in ((6, 0, CTX), (5, CTX, KEYS)):
                        ins = dve.scalar_tensor_tensor(out=ckv_raw[:, i, lo_t:hi_t], in0=ckv_raw[:, i, lo_t:hi_t],
                                                       scalar=v("kvg", i), in1=ps[:, bank, 0:hi_t - lo_t],
                                                       op0=ALU.mult, op1=ALU.mult)
                    ins.then_inc(ckv_scaled, 1)

            def low_ckv():
                for i in range(KKV):
                    dve.wait_ge(ckvh_ready, i + 1)
                    dve.tensor_tensor(ckv_lo[:, i, :], ckv_raw[:, i, :], ckv_hi[:, i, :].bitcast(F32),
                                      ALU.subtract).then_inc(ckv_ready, 1)

            def scale_kg(i):
                dve.wait_ge(scale_spread, BC[EV[f"kg{i}"]] + 1)
                dve.scalar_tensor_tensor(out=kg[:, i, 0:CTX], in0=kg_raw[:, i, 0:CTX], scalar=v("gkg"),
                                         in1=ps[:, 6, 0:CTX], op0=ALU.mult, op1=ALU.mult)
                dve.scalar_tensor_tensor(out=knx[:], in0=kg_raw[:, i, CTX:KEYS], scalar=v("gkg"), in1=ps[:, 5, :],
                                         op0=ALU.mult, op1=ALU.mult).then_inc(knx_ready, 1)

            def row_scales(e, r, scale):
                dve.wait_ge(rstd_ready, e + 1)
                tick(dve.tensor_scalar(row_scale[:, r, :], rstd[:, e, 0:TX], scale, None, ALU.mult))

            def gq_steps(i):
                variance(EV[f"gq{i}"])
                rope(f"gq{i}", q_raw[:, i % 2, :], drained_key(("px", PROJ.index(f"gq{i}"))), [(gq[:, i, :], 0, P)])
                row_scales(EV[f"gq{i}"], 1 + i, GQA_SCALE)

            for t, name in enumerate(PROJ):
                if t == 3:
                    variance(EV["ckv"])
                if t == 4:
                    scale_ckv()
                    kr_rope()
                if t == 5:
                    variance(EV["kg0"])
                    low_ckv()
                if t == 6:
                    scale_kg(0)
                    variance(EV["kg1"])
                if t == 7:
                    rope("kg0", knx[:], lambda: dve.wait_ge(knx_ready, 1), [(kg[:, 0, CTX:KEYS], 0, P)])
                    scale_kg(1)
                if t == 8:
                    rope("kg1", knx[:], lambda: dve.wait_ge(knx_ready, 2), [(kg[:, 1, CTX:KEYS], 0, P)])
                if t == 12:
                    variance(EV["cq"])
                    row_scales(EV["cq"], 0, MLA_SCALE)
                if t >= 13:
                    gq_steps(t - 13)
                if t >= 1:
                    split_low(t + 1, t + 1)
                if name[:2] == "cq":
                    i = int(name[2])
                    px = full(("px", t))
                    dve.wait_ge(sq_ready, SQ0[EV["cq"]] + i + 1)
                    free(dve.scalar_tensor_tensor(out=cq_lo[:, i, :], in0=px, scalar=v("qg", i),
                                                  in1=cq_hi[:, i, :].bitcast(F32), op0=ALU.mult, op1=ALU.subtract),
                         ("px", t))
            gq_steps(2)
            split_low(UQ0 + 1, UQ0 + 1)
            gq_steps(3)
            for w in (UQR, UKK, UKV):
                split_low(w, w)
            for i in range(2):
                rope(f"qr{i}", q_raw[:, i, :], drained_key(("uq", 2, i)), [(qr[:, i, :], 0, P)])

            for s in range(4 * HEADS + 4):
                if 1 <= s < 4 * HEADS + 1:
                    n = s - 1
                    dve.wait_ge(exp_done, n + 1)
                    done = tick(dve.reciprocal(inv_row[:, n:n + 1], psum_row[:, n:n + 1]))
                    own_wait(done)
                    dve.tensor_scalar(probs[:, n % 3, :], probs[:, n % 3, :], inv_row[:, n:n + 1], None,
                                      ALU.mult).then_inc(probs_ready, 1)
                if s < 4 * HEADS:
                    h, qt, pair = s // 4, s % 4, 2 * (s % 2)
                    dve.wait_ge(scored, s + 1)
                    done = tick(dve.tensor_reduce(top[:, s:s + 1], ps[:, pair:pair + 2, 0:384], AX.XY, ALU.max))
                    own_wait(done)
                    dve.tensor_scalar(minus_top[:, s:s + 1], top[:, s:s + 1],
                                      row_scale[:, max(h - MLA_HEADS + 1, 0), qt:qt + 1], -1.0, ALU.mult,
                                      ALU.mult).then_inc(top_ready, 1)
                    b, q = s // 4, s % 4
                    mod_chunk(NW_IN + s, mod_acc0[:, b % 2], q, n_before=NW_IN + s - 1)
                if s >= 6 and s % 4 == 2:
                    b = (s - 6) // 4
                    p = full(("mc0", b))
                    free(dve.tensor_tensor(modc0[:, 4 * b:4 * b + 4], p[:, 0:4], v("modb", 2 * KD + 4 * b, 4),
                                           ALU.add), ("mc0", b))
                if s >= 7 and s % 4 == 3:
                    h = (s - 7) // 4
                    dve.wait_ge(oh_ready, h + 1)
                    free(dve.tensor_tensor(h_lo[:, h, :], full(("pv", h)), h_hi[:, h, :].bitcast(F32), ALU.subtract),
                         ("pv", h))

            split_low(N_WOUT, W_WOUT)
            split_low(N_WOUT + 1, W_WOUT + 1)
            for j in range(KD):
                n, w = (N_WOUT + j + 2, W_WOUT + j + 2) if j < KD - 2 else (N_MLP0 + j - KD + 2, W_MLP0 + j - KD + 2)
                split_low(n, w)
                add_product(("wo", j), j, modc0[:, j:j + 1])

            def gain(r, scales, norm):
                return tick(dve.scalar_tensor_tensor(out=gains[:, r, :], in0=scales, scalar=1.0, in1=norm, op0=ALU.add,
                                                     op1=ALU.mult))

            def norm_x(r, event, scales, norm, shift):
                done = gain(r, scales, norm)
                variance(EV[event])
                own_wait(done)
                modulated(2 + r, EV[event], x, gains[:, r, :], shift, h_hi, h_lo, SEQ, 5, tmp_b)

            norm_x(0, "x1", modc0[:, 2 * KD:3 * KD], v("n2", 0, KD), modc0[:, KD:2 * KD])

            def mlp(l, i, last, gate2):
                n0, w0 = (N_MLP0, W_MLP0) if l == 0 else (N_MLP1, W_MLP1)
                w_at, m_at = mlp_offsets(l)
                per = len(w_at) + len(m_at)
                first = own[0]
                steps = KD * i
                for s in range(MLP_W):
                    if s < len(m_at):
                        b, q = s // 4, s % 4
                        mod_chunk(n0 + m_at[s], mod_acc1[:, b], q, 16 * per // STAGES * i, n0 + m_at[s - 1], per * i)
                    o = w_at[s + 2] if s + 2 < MLP_W else per + s + 2 - MLP_W
                    behind = last and s >= MLP_W - 2
                    if not behind:
                        split_low(n0 + o, w0 + s + 2, MLP_W * i)
                    if l == 0 and s in (6, 10, 14):
                        b = (s - 6) // 4
                        p = full(("mc1", b), PER[0][6] * i)
                        cols = bass.ds((3 * i + b) * 4, 4)
                        free(dve.tensor_tensor(modc1[:, cols], p[:, 0:4],
                                               vec[:, bass.ds(VEC["modb"] + 6 * KD + (3 * i + b) * 4, 4)],
                                               ALU.add), ("mc1", b))
                    key = ("mlp", l, s)
                    if s < KD:
                        bank, use = AT[key]
                        dve.wait_ge(drained[bank], use + PER[l][bank] * i)
                        own[0] += 1
                        dve.tensor_tensor(relu2[:, s % 2, :], relu[:, s % 2, :], relu[:, s % 2, :],
                                          ALU.mult).then_inc(dve_step, 1)
                        dve.wait_ge(hidh_ready, (l * FFG + 0) * KD + s + 1 + KD * i)
                        own_wait(first + s + 1, steps)
                        dve.tensor_tensor(hid_lo[:, s, :], relu2[:, s % 2, :], hid_hi[:, s, :].bitcast(F32),
                                          ALU.subtract).then_inc(hid_ready, 1)
                    else:
                        add_product(key, s - KD, gate2[:, s - KD:s - KD + 1], PER[l][s % 4] * i)
                    if behind and l == 0:
                        split_low(n0 + o, w0 + s + 2, MLP_W * i)
                own[0] = first

            with dve.Fori(0, FFG - 1) as i:
                mlp(0, i, False, modc0[:, 3 * KD:4 * KD])
            mlp(0, FFG - 1, True, modc0[:, 3 * KD:4 * KD])
            own[0] += FFG * KD

            norm_x(1, "x2", modc1[:, KD:2 * KD], v("n1", KD, KD), modc1[:, 0:KD])

            steps, last = [0], {}

            def convolve(taps):
                for i, k in taps:
                    w = v("convw", i * TAPS + k)
                    if k == 0:
                        bank, use = AT[("fi", FI.index(f"a{i}"))]
                        dve.wait_ge(drained[bank], use)
                        ins = dve.tensor_scalar(conv[:, i, :], u[:, i, 0:SEQ], w, v("convb", i), ALU.mult, ALU.add)
                    else:
                        dve.wait_ge(conv_step, last[i])
                        ins = dve.scalar_tensor_tensor(out=conv[:, i, :], in0=u[:, i, k:k + SEQ], scalar=w,
                                                       in1=conv[:, i, :], op0=ALU.mult, op1=ALU.add)
                    ins.then_inc(conv_step, 1)
                    steps[0] += 1
                    last[i] = steps[0]

            dve.wait_ge(pads_set, 4)
            for c, name in enumerate(FI):
                split_low(N_FC + c + 2, W_FC + c + 2)
                i = int(name[1])
                if name[0] == "a":
                    p = full(("fi", c))
                    bank, use = AT[("fi", c - 1)]
                    dve.wait_ge(drained[bank], use)
                    free(dve.tensor_tensor(u[:, i, PAD:PAD + SEQ], p, gate[:, i % 2, :], ALU.mult), ("fi", c))
                convolve(dve_taps[c])
            convolve(dve_taps[NFI])
            dve.wait_ge(tap_added, sum(POOL_TAPS) - KCH)
            for i in range(KCH):
                dve.wait_ge(conv_step, last[i])
                dve.tensor_tensor(conv[:, i, :], conv[:, i, :], part[:, i, :], ALU.add).then_inc(conv_step, 1)

            def low_fourier(g):
                dve.wait_ge(fh_ready, g + 1)
                free(dve.scalar_tensor_tensor(out=h_lo[:, g, :], in0=full(("f2", g)), scalar=float((SEQ * P) ** -0.5),
                                              in1=h_hi[:, g, :].bitcast(F32), op0=ALU.mult, op1=ALU.subtract),
                     ("f2", g))

            low_fourier(0)
            low_fourier(1)
            mean = full("mean")
            for i in range(KCH):
                dve.tensor_tensor(cent[:, i, :], conv[:, i, :], mean, ALU.add).then_inc(cent_ready, 1)
            variance(EV["ln"])
            low_fourier(2)
            low_fourier(3)
            dve.wait_ge(scale_spread, BC[EV["ln"]] + 1)
            for i in range(KCH):
                dve.tensor_tensor(cent[:, i, :], cent[:, i, :], ps[:, 5, :], ALU.mult).then_inc(y_ready, 1)
            for i in range(KCH):
                dve.wait_ge(sh_ready, i + 1)
                dve.tensor_tensor(h_lo[:, KCH + i, :], conv[:, i, :], h_hi[:, KCH + i, :].bitcast(F32),
                                  ALU.subtract).then_inc(mix_ready, 1)
            for j in range(KD):
                n, w = (N_FCOUT + j + 2, W_FCOUT + j + 2) if j < KD - 2 else (N_MLP1 + j - KD + 2, W_MLP1 + j - KD + 2)
                split_low(n, w)
                add_product(("fo", j), j, modc1[:, 2 * KD + j:2 * KD + j + 1])
            norm_x(2, "x3", modc1[:, 4 * KD:5 * KD], v("n2", KD, KD), modc1[:, 3 * KD:4 * KD])
            with dve.Fori(0, FFG - 1) as i:
                mlp(1, i, False, modc1[:, 5 * KD:6 * KD])
            mlp(1, FFG - 1, True, modc1[:, 5 * KD:6 * KD])

            variance(EV["x4"])
            dve.wait_ge(scale_spread, BC[EV["x4"]] + 1)
            for k in range(KD):
                dve.scalar_tensor_tensor(out=x[:, k, :], in0=x[:, k, :], scalar=v("nf", k), in1=ps[:, 5, :],
                                         op0=ALU.mult, op1=ALU.mult).then_inc(y_tile, 1)

        @block.tensor
        def _(pe):
            def acquire(key, later=0):
                bank, use = AT[key]
                if use > 1:
                    pe.wait_ge(drained[bank], use - 1 + later)
                return ps[:, bank, :]

            def fill(ins, key):
                ins.then_inc(filled[AT[key][0]], 1)

            def product(outp, left, right, first, last, **how):
                (lh, ll), (rh, rl) = left, right
                pe.matmul(outp, lh, rh, start=first, stop=False, **how)
                pe.matmul(outp, lh, rl, start=False, stop=False, **how)
                return pe.matmul(outp, ll, rh, start=False, stop=last, **how)

            def weights(w, lo_c, hi_c):
                return w_hi[:, w % SLOTS, lo_c:hi_c], w_lo[:, w % SLOTS, lo_c:hi_c]

            def tile_product(key, w, n, hi, lo, ready=None, later=0, n_later=0):
                outp = acquire(key, later)[:, 0:hi.shape[2]]
                pe.wait_ge(chunk_done, n + 1 + n_later)
                for k in range(KD):
                    if ready:
                        ready(k)
                    ins = product(outp, weights(w, k * P, k * P + P), (hi[:, k, :], lo[:, k, :]), k == 0, k == KD - 1)
                fill(ins, key)

            def sum_squares(e, j):
                n = EVENTS[e][1]
                if n > 2 and j < n - 1:
                    return
                q = SQ0[e] + j
                if j == (n - 1 if n > 2 else 0) and e > 0:
                    pe.wait_ge(var_ready, e)
                parts = [(sq if e < EV["x1"] else sq_b)[q % 2]]
                if n > 2:
                    pe.wait_ge(sq_summed, q)
                    parts = [sq_acc, *parts]
                for i, buf in enumerate(parts):
                    if i == len(parts) - 1:
                        pe.wait_ge(sq_ready, q + 1)
                    for t in range(EVENTS[e][2]):
                        ins = pe.matmul(ps[:, 7, t:t + 1], buf[:, t * P:t * P + P], ones[:, 0:1],
                                        start=(t == 0 and i == 0 and (n > 2 or j == 0)),
                                        stop=(j == n - 1 and i == len(parts) - 1), skip_group_check=True)
                ins.then_inc(sq_summed, 1)

            def spread(e):
                pe.wait_ge(rstd_ready, e + 1)
                for t, (bank, col) in enumerate(event_tiles(e)):
                    ins = pe.matmul(ps[:, bank, col:col + P], rstd[:, e, t:t + 1].to_broadcast([P, P]), ident,
                                    start=True, stop=True)
                ins.then_inc(scale_spread, 1)

            def rotate(name, src):
                r = ROTS.index(name)
                if r:
                    pe.wait_ge(rot_used, r)
                m = TAB["rotm" if name[1] == "r" else "rotg"]
                pe.matmul(ps[:, 4, :], tab[:, m:m + P], src, start=True, stop=True).then_inc(rotated, 1)

            def mod_columns(key, acc, later=0):
                outp = acquire(key, later)
                for j in range(4):
                    ins = pe.matmul(outp[:, j:j + 1], acc[:, 0, j * P:j * P + P], ones[:, 0:1], start=(j == 0),
                                    stop=True, skip_group_check=True)
                fill(ins, key)

            pe.wait_ge(consts_set, 3)
            for j in range(KD):
                sum_squares(EV["x0"], j)
            pe.wait_ge(ident_landed, 16)
            spread(EV["x0"])
            pe.wait_ge(silu_done, 1)
            for b in range(4):
                pe.wait_ge(head_landed[b], 16)
                for k in range(KD):
                    ins = pe.matmul(ps[0:2, b, :], c_act[:, 2 * k:2 * k + 2],
                                    mod_head[:, 4 * b + k // 2, (k % 2) * BLOCK:(k % 2 + 1) * BLOCK],
                                    start=(k == 0), stop=(k == KD - 1))
                fill(ins, ("row", b))
            for j in range(2 * KD):
                if j % 4 == 0:
                    pe.wait_ge(drained[j // 4], 1)
                ins = pe.transpose(ps[:, 4, 2 * j:2 * j + 2],
                                   mod_acc0[0:2, j // 8, j // 4 % 2, j % 4 * P:j % 4 * P + P], ident[0:2, 0:2])
            fill(ins, "mod columns x")

            def kept(key):
                bank, use = AT[key]
                pe.wait_ge(drained[bank], use)

            def between(t):
                if t in (1, 2):
                    sum_squares(EV["ckv"], t - 1)
                if t == 3:
                    spread_after(EV["ckv"], t_ready, 2 * KD)
                    pe.wait_ge(tab_landed, 32)
                    kept(("pc", 2))
                    rotate("kr", kr_raw[:, CTX:KEYS])
                if t == 4:
                    sum_squares(EV["kg0"], 0)
                if t == 5:
                    spread_after(EV["kg0"], ckv_scaled, KKV)
                    sum_squares(EV["kg1"], 0)
                if t == 6:
                    pe.wait_ge(knx_ready, 1)
                    rotate("kg0", knx[:])
                    spread_after(EV["kg1"], knx_ready, 1)
                if t == 7:
                    pe.wait_ge(knx_ready, 2)
                    rotate("kg1", knx[:])
                if 8 <= t < 12:
                    sum_squares(EV["cq"], t - 8)
                if 12 <= t < 16:
                    i = t - 12
                    sum_squares(EV[f"gq{i}"], 0)
                    kept(("px", 11 + i))
                    rotate(f"gq{i}", q_raw[:, i % 2, :])

            def spread_after(e, used, count):
                pe.wait_ge(used, count)
                spread(e)

            for t, name in enumerate(PROJ):
                if t in VALUES:
                    half = VALUES.index(t)
                    pe.wait_ge(chunk_done, t + 1)
                    for n in range(TK // 2):
                        outp = bank_of(("vg", n)) if half else acquire(("vg", n))
                        hi, lo, first = (h_hi, h_lo, 2 * n) if 2 * n < TX else (hc_hi, hc_lo, 2 * n - TX)
                        for tt in range(2):
                            cols = slice((first + tt) * P, (first + tt) * P + P)
                            for k in range(KD // 2):
                                ins = product(outp[:, tt * 2 * P:(tt + 1) * 2 * P],
                                              (hi[:, half * KD // 2 + k, cols], lo[:, half * KD // 2 + k, cols]),
                                              weights(t, k * 2 * P, (k + 1) * 2 * P),
                                              half == 0 and tt == 0 and k == 0, half == 1 and k == KD // 2 - 1,
                                              skip_group_check=True)
                        if half:
                            fill(ins, ("vg", n))
                    if half == 0:
                        ins.then_inc(values_half, 1)
                elif t == 0:
                    tile_product(("px", t), t, t, h_hi, h_lo, lambda k: pe.wait_ge(h_ready, k + 1))
                elif t == 1:
                    tile_product(("px", t), t, t, h_hi, h_lo)
                    for j in range(KD):
                        sum_squares(EV["ctx0"], j)
                    spread(EV["ctx0"])
                    tile_product(("pc", 0), 0, 0, hc_hi, hc_lo, lambda k: pe.wait_ge(h_ready, KD + k + 1))
                    tile_product(("pc", t), t, t, hc_hi, hc_lo)
                else:
                    tile_product(("px", t), t, t, h_hi, h_lo)
                    if t < BOTH:
                        tile_product(("pc", t), t, t, hc_hi, hc_lo)
                between(t)

            pe.wait_ge(drained[AT[("px", 10)][0]], AT[("px", 10)][1])
            for n in range(3):
                pe.wait_ge(chunk_done, UQ0 + n + 1)
                for i in range(2):
                    outp = acquire(("uq", n, i))
                    for k in range(KQ):
                        c = (i * KQ + k) * P
                        ins = product(outp, weights(UQ0 + n, c, c + P), (cq_hi[:, k, :], cq_lo[:, k, :]), k == 0,
                                      k == KQ - 1)
                    fill(ins, ("uq", n, i))
                if n == 0:
                    between(15)
            pe.wait_ge(ckv_ready, KKV)
            pe.wait_ge(knx_ready, 2)
            pe.wait_ge(chunk_done, UKK + 1)
            for n in range(2):
                ctx_bank = acquire(("kc", n))
                for h in (2 * n, 2 * n + 1):
                    outp = acquire(("kx", h))
                    for k in range(KKV):
                        c = (h * KKV + k) * P
                        ins = product(outp, weights(UKK, c, c + P), (ckv_hi[:, k, CTX:KEYS], ckv_lo[:, k, CTX:KEYS]),
                                      k == 0, k == KKV - 1)
                    fill(ins, ("kx", h))
                for h in (2 * n, 2 * n + 1):
                    for k in range(KKV):
                        c = (h * KKV + k) * P
                        ins = product(ctx_bank[:, h % 2 * CTX:h % 2 * CTX + CTX], weights(UKK, c, c + P),
                                      (ckv_hi[:, k, 0:CTX], ckv_lo[:, k, 0:CTX]), k == 0, k == KKV - 1)
                fill(ins, ("kc", n))
                kept(("uq", 2, n))
                rotate(f"qr{n}", q_raw[:, n, :])
            pe.wait_ge(chunk_done, UKV + 1)
            for t in range(TK):
                outp = acquire(("v", t))
                cols = slice(t * P, t * P + P)
                for k in range(KKV):
                    ins = product(outp, (ckv_hi[:, k, cols], ckv_lo[:, k, cols]),
                                  weights(UKV, k * BLOCK, (k + 1) * BLOCK), k == 0, k == KKV - 1)
                fill(ins, ("v", t))

            kept(("v", TK - 1))
            pe.wait_ge(rot_used, len(ROTS))
            for s in range(4 * HEADS + 3):
                if s < 4 * HEADS:
                    h, qt, pair = s // 4, s % 4, 2 * (s % 2)
                    q_cols = slice(qt * P, qt * P + P)
                    if s >= 2:
                        pe.wait_ge(exp_done, s - 1)
                    for half in range(2):
                        keys = slice(half * 384, half * 384 + 384)
                        outp = ps[:, pair + half, 0:384]
                        if h < MLA_HEADS:
                            pe.matmul(outp, qn[:, h, q_cols], kn[:, h, keys], start=True, stop=False)
                            ins = pe.matmul(outp, qr[:, h // 2, q_cols], (kr_odd if h % 2 else kr_even)[:, keys],
                                            start=False, stop=True)
                        else:
                            g = h - MLA_HEADS
                            ins = pe.matmul(outp, gq[:, g, q_cols], kg[:, g // 2, keys], start=True, stop=True)
                    ins.then_inc(scored, 1)
                if 2 <= s < 4 * HEADS + 2:
                    n = s - 2
                    pe.wait_ge(probs_ready, n + 1)
                    if n:
                        pe.wait_ge(turned_copied, n)
                    for kt in range(TK):
                        ins = pe.transpose(ps[:, 4 + kt // 3, kt % 3 * P:kt % 3 * P + P],
                                           probs[:, n % 3, kt * P:kt * P + P], ident)
                    ins.then_inc(turned, 1)
                if s >= 5 and s % 4 == 1:
                    b = (s - 5) // 4
                    pe.wait_ge(mod_summed, b + 1)
                    mod_columns(("mc0", b), mod_acc0[:, b % 2])
                if s >= 6 and s % 4 == 2:
                    h = (s - 6) // 4
                    outp = acquire(("pv", h))
                    pe.wait_ge(turned_copied, 4 * h + 4)
                    for kt in range(TK):
                        g = (h - MLA_HEADS) // 2
                        val = vm[:, kt, h * P:h * P + P] if h < MLA_HEADS else vg[:, kt, g * P:g * P + P]
                        ins = pe.matmul(outp, val, probs_t[:, h % 2, kt, :], start=(kt == 0), stop=(kt == TK - 1))
                    fill(ins, ("pv", h))

            pe.wait_ge(exp_done, 4 * HEADS)
            for j in range(KD):
                tile_product(("wo", j), W_WOUT + j, N_WOUT + j, h_hi, h_lo,
                             (lambda k: kept(("pv", k))) if j == 0 else None)
                if j == 2:
                    pe.wait_ge(drained[7], AT[("mc0", 7)][1])
                if j >= 2:
                    sum_squares(EV["x1"], j - 2)
            sum_squares(EV["x1"], KD - 2)
            sum_squares(EV["x1"], KD - 1)
            spread_after(EV["x1"], turned_copied, 4 * HEADS)

            def mlp(l, i, last):
                n0, w0 = (N_MLP0, W_MLP0) if l == 0 else (N_MLP1, W_MLP1)
                w_at, m_at = mlp_offsets(l)
                per = len(w_at) + len(m_at)
                e = EV["x2" if l == 0 else "x4"]
                normed = (2 if l == 0 else 4) * KD
                for s in range(MLP_W):
                    key = ("mlp", l, s)
                    ready = None
                    if s == 0:
                        def ready(k):
                            pe.wait_ge(h_ready, normed + k + 1)
                    if s == KD:
                        def ready(k):
                            pe.wait_ge(hid_ready, l * FFG * KD + k + 1 + KD * i)
                    hi, lo = (h_hi, h_lo) if s < KD else (hid_hi, hid_lo)
                    tile_product(key, w0 + s, n0 + w_at[s], hi, lo, ready, PER[l][s % 4] * i, per * i)
                    if l == 0 and s in (5, 9, 13):
                        b = (s - 5) // 4
                        pe.wait_ge(mod_summed, KD + b + 1 + 3 * i)
                        mod_columns(("mc1", b), mod_acc1[:, b], PER[0][6] * i)
                    if last and s >= KD + 2:
                        sum_squares(e, s - KD - 2)
                if last:
                    sum_squares(e, KD - 2)
                    sum_squares(e, KD - 1)

            with pe.Fori(0, FFG - 1) as i:
                mlp(0, i, False)
            mlp(0, FFG - 1, True)
            spread(EV["x2"])

            def channel_dft(g):
                kept(("fi", FI.index(f"f{g}")))
                for b in range(2):
                    outp = acquire(("f1", g, b))
                    for t in (2 * b, 2 * b + 1):
                        ins = pe.matmul(outp[:, t % 2 * 2 * P:(t % 2 + 1) * 2 * P], f_t[:, g, t * P:t * P + P],
                                        cs_small[:], start=True, stop=True)
                    fill(ins, ("f1", g, b))

            for c in range(NFI):
                tile_product(("fi", c), W_FC + c, N_FC + c, h_hi, h_lo,
                             (lambda k: pe.wait_ge(h_ready, 3 * KD + k + 1)) if c == 0 else None)
                if c == 8:
                    pe.wait_ge(dft_landed, 32)
                if c >= 9:
                    channel_dft(c - 9)
            channel_dft(GROUPS - 1)

            def token_dft(g):
                outp = acquire(("f2", g))
                kept(("f1", g, 0))
                kept(("f1", g, 1))
                for part in range(2):
                    for t in range(TX):
                        ins = pe.matmul(outp, f_mid[:, t, g, part * P:part * P + P], cs[:, part, t, :],
                                        start=(part == 0 and t == 0), stop=(part == 1 and t == TX - 1))
                fill(ins, ("f2", g))

            token_dft(0)
            token_dft(1)
            outp = acquire("mean")
            taps = KCH * TAPS - sum(POOL_TAPS)
            for i in range(KCH):
                pe.wait_ge(conv_step, taps + i + 1)
                ins = pe.matmul(outp, meanw[:], conv[:, i, :], start=(i == 0), stop=(i == KCH - 1))
            fill(ins, "mean")
            token_dft(2)
            for i in range(KCH):
                sum_squares(EV["ln"], i)
            token_dft(3)
            spread(EV["ln"])

            for half in range(2):
                for j in range(2):
                    outp = bank_of(("fo", j)) if half else acquire(("fo", j))
                    pe.wait_ge(chunk_done, N_FCOUT + j + 1)
                    for k in range(half * GROUPS, half * GROUPS + GROUPS):
                        if j == 0 and k < GROUPS:
                            kept(("f2", k))
                        elif j == 0:
                            pe.wait_ge(mix_ready, k - GROUPS + 1)
                        ins = product(outp, weights(W_FCOUT + j, k * P, k * P + P), (h_hi[:, k, :], h_lo[:, k, :]),
                                      k == 0, k == KD - 1)
                    if half:
                        fill(ins, ("fo", j))
            for j in range(2, KD):
                tile_product(("fo", j), W_FCOUT + j, N_FCOUT + j, h_hi, h_lo)
                if j >= 2:
                    sum_squares(EV["x3"], j - 2)
            sum_squares(EV["x3"], KD - 2)
            sum_squares(EV["x3"], KD - 1)
            spread_after(EV["x3"], y_ready, KCH)
            with pe.Fori(0, FFG - 1) as i:
                mlp(1, i, False)
            mlp(1, FFG - 1, True)
            spread(EV["x4"])


def rope_tables():
    tok = np.arange(SEQ)
    pos = (tok // GRID_W, tok % GRID_W)
    made = []
    for block in (HD // 2, ROPE // 2):
        half = block // 2
        freqs = np.float32(10000.0) ** (-np.arange(half, dtype=np.float32) / np.float32(half))
        cos, sin, rot = np.zeros((P, SEQ), np.float32), np.zeros((P, SEQ), np.float32), np.zeros((P, P), np.float32)
        for d in range(P):
            angle = pos[d // block % 2].astype(np.float32) * freqs[d % half]
            cos[d], sin[d] = np.cos(angle), np.sin(angle)
            if d % block < half:
                rot[d + half, d] = -1.0
            else:
                rot[d - half, d] = 1.0
        made.append((cos, sin, rot))
    (cg, sg, rg), (cm, sm, rm) = made
    return np.concatenate([cg, sg, cm, sm, np.eye(P, dtype=np.float32), rg, rm], axis=1)


def dft_tables():
    def table(n, f):
        k = np.outer(np.arange(n), np.arange(n)) % n
        return f(2 * np.pi * k / n).astype(np.float32)
    big = np.stack([table(SEQ, np.cos), -table(SEQ, np.sin)]).reshape(2, TX, P, SEQ).transpose(2, 0, 1, 3)
    return np.ascontiguousarray(big), np.concatenate([table(P, np.cos), table(P, np.sin)], axis=1)


def columns(a):
    return a.reshape(-1, P).T


def tiles(w):
    k, m = w.shape[0] // P, w.shape[1] // P
    return w.reshape(k, P, m, P).transpose(2, 1, 0, 3).reshape(m, P, k * P)


def mod_blocks(w):
    b = w.shape[1] // BLOCK
    return w.reshape(4, 2, P, b, BLOCK).transpose(3, 0, 2, 1, 4).reshape(b * 4, P, CHUNK)


def lay_out(i):
    w_in, uq, ukv = i["attn_w_in"][0], i["mla_w_uq"][0], i["mla_w_ukv"][0]
    at = np.cumsum([0, Q_RANK, GQA_HEADS * HD, KV_RANK, ROPE, GQA_KV * HD, GQA_KV * HD])
    cq, gq, ckv, kr, kg, vg = (w_in[:, a:b] for a, b in zip(at[:-1], at[1:]))
    v_chunks = vg.reshape(2, KD // 2, P, GQA_KV * HD).transpose(0, 2, 1, 3).reshape(2, P, CHUNK)
    uq = uq.reshape(Q_RANK, MLA_HEADS, NOPE + ROPE)
    uq = np.concatenate([uq[:, :, :NOPE].reshape(Q_RANK, -1), uq[:, :, NOPE:].reshape(Q_RANK, -1)], axis=1)
    ukv = ukv.reshape(KV_RANK, MLA_HEADS, 2 * P)
    uq_chunks = tiles(uq).reshape(3, 2, P, KQ * P).transpose(0, 2, 1, 3).reshape(3, P, CHUNK)
    k_chunk = tiles(ukv[:, :, :NOPE].reshape(KV_RANK, -1)).transpose(1, 0, 2).reshape(1, P, CHUNK)
    v_chunk = ukv[:, :, NOPE:].reshape(KKV, P, MLA_HEADS * P).transpose(1, 0, 2).reshape(1, P, CHUNK)
    fc = i["fc_w_in"][0]
    order = np.concatenate([np.concatenate([np.arange(P) + GATE_AT + g * P, np.arange(P) + CH + g * P])
                            for g in range(KCH)] + [np.arange(CH)])
    vectors = [columns(i["norm1_g"]), columns(i["norm2_g"]), columns(i["final_g"]), columns(i["mod_b"]),
               columns(i["mla_q_norm_g"]), columns(i["mla_kv_norm_g"]), columns(i["gqa_q_norm_g"]),
               columns(i["gqa_k_norm_g"]), columns(i["conv_b"]), columns(i["conv_ln_g"]), columns(i["conv_ln_b"]),
               i["conv_w"][0].reshape(TAPS, KCH, P).transpose(2, 1, 0).reshape(P, -1)]
    mod = [mod_blocks(w) for w in i["mod_w"]]

    def mlp_chunks(l):
        up = tiles(i["mlp_w1"][l])
        down = [tiles(i["mlp_w2"][l][g * D:(g + 1) * D]) for g in range(FFG)]
        return np.concatenate([part for g in range(FFG) for part in (up[g * KD:(g + 1) * KD], down[g])])

    dft, dft_small = dft_tables()
    return [
        np.stack([i["c"][0], i["c_ctx"]]).reshape(2, KD, P).transpose(2, 1, 0).reshape(P, 2 * KD),
        np.concatenate(vectors, axis=1), rope_tables(), dft, dft_small,
        i["x"][0].T.reshape(KD, P, SEQ), i["ctx"][0].T.reshape(KD, P, CTX),
        mod[0][:16], mod[0][16:], mod[1],
        np.concatenate([tiles(np.concatenate([ckv, kr, kr, kg], axis=1)), v_chunks,
                        tiles(np.concatenate([cq, gq], axis=1)), uq_chunks, k_chunk, v_chunk, tiles(i["attn_w_out"][0])]),
        mlp_chunks(0), np.concatenate([tiles(fc[:, order]), tiles(i["fc_w_out"][0])]), mlp_chunks(1),
    ]


def kernel(**inputs):
    import concourse.bacc as bacc
    from concourse.bass_utils import run_bass_kernel_spmd

    nc = bacc.Bacc("TRN2", target_bir_lowering=False, num_devices=1)
    names = ["c_cols", "vectors", "tables", "dft", "dft_small", "x_t", "ctx_t", "mod0_head", "mod0", "mod1", "w_mix0",
             "w_mlp0", "w_fc", "w_mlp1"]
    arrays, args = {}, []
    for name, a in zip(names, lay_out({k: np.asarray(a) for k, a in inputs.items()})):
        arrays[name] = np.ascontiguousarray(a)
        args.append(nc.dram_tensor(name, arrays[name].shape, F32, kind="ExternalInput").ap())
    args.append(nc.dram_tensor("y_t", (KD, P, SEQ), F32, kind="ExternalOutput").ap())
    dit_block_kernel(nc, *args)
    r = run_bass_kernel_spmd(nc, [arrays], core_ids=[0])
    return np.ascontiguousarray(r.results[0]["y_t"].reshape(D, SEQ).T)[None]
```

```python
from contextlib import ExitStack

import numpy as np

import concourse.bass as bass
from concourse import mybir

ACT = mybir.ActivationFunctionType
ALU = mybir.AluOpType
AX = mybir.AxisListType
F32 = mybir.dt.float32
F32R = mybir.dt.float32r

P = 128
D = 1024
KD = D // P
SEQ, CTX = 512, 256
KEYS = CTX + SEQ
TX, TC = SEQ // P, CTX // P
TK = TX + TC
FF = 4 * D
GRID_W = 64
EPS = 1e-6
MLA_HEADS, NOPE, ROPE = 4, 128, 64
GQA_HEADS, GQA_KV, HD = 4, 2, 128
Q_RANK, KV_RANK = D // 2, D // 4
KQ, KKV = Q_RANK // P, KV_RANK // P
MLA_SCALE = float(NOPE + ROPE) ** -0.5
GQA_SCALE = float(HD) ** -0.5
HEADS = MLA_HEADS + GQA_HEADS
GROUPS, CH, TAPS = 4, 512, 31
KCH = CH // P
GATE_AT = 2 * CH
PAD = TAPS // 2
POOL_TAPS = (14, 14, 14, 13)
PRODUCTS = 4

CHUNK = 1024
BLOCK = 512
FFG = 4
STAGES = 4
SLOTS = 2

VEC = {}
_at = 0
for _name, _n in (("n1", 2 * KD), ("n2", 2 * KD), ("nf", KD), ("modb", 2 * 6 * KD), ("qg", KQ), ("kvg", KKV),
                  ("gqg", 1), ("gkg", 1), ("convb", KCH), ("lng", KCH), ("lnb", KCH), ("convw", KCH * TAPS)):
    VEC[_name] = _at
    _at += _n
NVEC = _at
TAB = {"cosg": 0, "sing": 512, "cosm": 1024, "sinm": 1536, "ident": 2048, "rotg": 2176, "rotm": 2304}
NTAB = 2432

PROJ = ["ckv0", "ckv1", "kr", "kg0", "kg1", "v0", "v1", "cq0", "cq1", "cq2", "cq3", "gq0", "gq1", "gq2", "gq3"]
NPROJ = len(PROJ)
BOTH = 7
VALUES = (5, 6)
VALUE_BANKS = (3, 0, 2)
UQ0, UQ1, UQR, UKK, UKV = range(NPROJ, NPROJ + 5)
NW_IN = NPROJ + 5
NM0 = 32
N_WOUT = NW_IN + NM0
N_MLP0 = N_WOUT + KD
MLP_W, MLP_M = 16, 12
N_FC = N_MLP0 + FFG * (MLP_W + MLP_M)
NFI = 12
N_FCOUT = N_FC + NFI
N_MLP1 = N_FCOUT + KD
W_WOUT, W_MLP0 = NW_IN, NW_IN + KD
W_FC = W_MLP0 + FFG * MLP_W
W_FCOUT = W_FC + NFI
W_MLP1 = W_FCOUT + KD

FI = ["g0", "a0", "g1", "a1", "g2", "a2", "g3", "a3", "f0", "f1", "f2", "f3"]
ROTS = ["kr", "kg0", "kg1", "gq0", "gq1", "gq2", "gq3", "qr0", "qr1"]
OUT_STEP = {4 * h + 9: h for h in range(HEADS - 1)} | {4 * HEADS + 3: HEADS - 1}
EVENTS = [("x0", KD, TX, D, "x"), ("ctx0", KD, TC, D, "c"), ("ckv", KKV, TK, KV_RANK, "xc"),
          ("kg0", 1, TK, HD, "xc"), ("kg1", 1, TK, HD, "xc"), ("cq", KQ, TX, Q_RANK, ""),
          ("gq0", 1, TX, HD, ""), ("gq1", 1, TX, HD, ""), ("gq2", 1, TX, HD, ""), ("gq3", 1, TX, HD, ""),
          ("x1", KD, TX, D, "x"), ("x2", KD, TX, D, "x"), ("ln", KCH, TX, CH, "x"), ("x3", KD, TX, D, "x"),
          ("x4", KD, TX, D, "x")]
EV = {e[0]: i for i, e in enumerate(EVENTS)}
SQ0 = [sum(e[1] for e in EVENTS[:i]) for i in range(len(EVENTS) + 1)]
BC = [sum(bool(e[4]) for e in EVENTS[:i]) for i in range(len(EVENTS) + 1)]


def event_tiles(e):
    if EVENTS[e][4] == "x" or EVENTS[e][2] == TX:
        return [(5, t * P) for t in range(TX)]
    if EVENTS[e][4] == "c":
        return [(6, t * P) for t in range(TC)]
    return [(6, t * P) for t in range(TC)] + [(5, t * P) for t in range(TX)]


POOL_LOWS = (1, 3, 4, 6)


def lows_before(g):
    pooled = sum(g // KD + (g % KD > k) for k in POOL_LOWS)
    return pooled, g - pooled


AHEAD = 3

ROW_BLOCKS = (0, 2, 3)


class Ledger:

    def __init__(self):
        self.uses, self.at = [0] * 8, {}

    def use(self, key, bank):
        self.uses[bank] += 1
        self.at[key] = (bank, self.uses[bank])


def plan_taps(quota, rate):
    done, order, last = [0] * KCH, [], None
    for c in range(NFI + 1):
        here = []
        while sum(done) < sum(quota) and (len(here) < rate or c == NFI):
            open_tiles = [i for i in range(KCH) if c >= 2 * i + 2 and done[i] < quota[i]]
            if not open_tiles:
                break
            last = max(open_tiles, key=lambda i: (i != last, quota[i] - done[i]))
            here.append((last, done[last]))
            done[last] += 1
        order.append(here)
    return order


def plan_banks():
    led = Ledger()
    for b in ROW_BLOCKS:
        led.use(("row", b), b)
    led.use("mod columns x", 4)
    for t in range(NPROJ):
        if t not in VALUES:
            led.use(("px", t), t % 2)
            if t < BOTH:
                led.use(("pc", t), 2 + t % 2)
        elif t == VALUES[0]:
            for n, b in enumerate(VALUE_BANKS):
                led.use(("vg", n), b)
    for n, (a, b) in enumerate(((2, 3), (0, 1), (2, 3))):
        led.use(("uq", n, 0), a)
        led.use(("uq", n, 1), b)
    for n, (a, b, c) in enumerate(((0, 1, 5), (2, 3, 6))):
        led.use(("kx", 2 * n), a)
        led.use(("kx", 2 * n + 1), b)
        led.use(("kc", n), c)
    for t, b in enumerate((0, 1, 2, 3, 5, 6)):
        led.use(("v", t), b)
    for h in range(HEADS):
        led.use(("pv", h), 6)
    for b in range(8):
        led.use(("mc0", b), 7)
    for j in range(KD):
        led.use(("wo", j), j % 4)
    per = {}

    def mlp(l):
        base = list(led.uses)
        for s in range(MLP_W):
            led.use(("mlp", l, s), s % 4)
        if l == 0:
            for b in range(3):
                led.use(("mc1", b), 6)
        per[l] = [a - b for a, b in zip(led.uses, base)]
        led.uses = [b + FFG * p for b, p in zip(base, per[l])]

    mlp(0)
    for c in range(NFI):
        led.use(("fi", c), c % 4)
    for g in range(GROUPS):
        led.use(("f1", g, 0), 4)
        led.use(("f1", g, 1), 5)
    for g in range(GROUPS):
        led.use(("f2", g), (6, 2, 3, 6)[g])
    led.use("mean", 4)
    for j in range(KD):
        led.use(("fo", j), j % 4)
    mlp(1)
    return led.at, per


def dit_block_kernel(nc, c_cols, vectors, tables, dft, dft_small, x_t, ctx_t, mod0_head, mod0, mod1, w_mix0, w_mlp0,
                     w_fc, w_mlp1, out):
    AT, PER = plan_banks()
    with ExitStack() as life:
        def sb(name, shape, dt=F32, on=life):
            return on.enter_context(nc.sbuf_tensor(name, [P, *shape], dt))

        def sem(name):
            return life.enter_context(nc.semaphore(name))

        ps = life.enter_context(nc.psum_tensor("ps", [P, 8, 512], F32))

        vec = sb("vec", [NVEC])
        tab = sb("tab", [NTAB])
        x = sb("x", [KD, SEQ])
        stage = sb("stage", [STAGES, CHUNK])
        w_hi = sb("w_hi", [SLOTS, CHUNK], F32R)
        w_lo = sb("w_lo", [SLOTS, CHUNK], F32R)
        h_hi = sb("h_hi", [KD, SEQ], F32R)
        h_lo = sb("h_lo", [KD, SEQ], F32R)
        ones = sb("ones", [P])
        meanw = sb("meanw", [P])
        minus_half = sb("minus_half", [TK])
        c_in = sb("c_in", [KD * 2])
        c_act = sb("c_act", [KD * 2])
        modA = sb("modA", [2, 2 * KD])
        modG = sb("modG", [2, KD])
        modc0 = sb("modc0", [4 * KD])
        modc1 = sb("modc1", [6 * KD])
        gains = sb("gains", [3, KD])
        var = sb("var", [len(EVENTS), TK])
        rstd = sb("rstd", [len(EVENTS), TK])
        row_scale = sb("row_scale", [1 + GQA_HEADS, TX])
        top = sb("top", [32])
        minus_top = sb("minus_top", [32])
        psum_row = sb("psum_row", [32])
        inv_row = sb("inv_row", [32])
        ident = tab[:, TAB["ident"]:TAB["ident"] + P]

        mix0 = ExitStack()
        with ExitStack() as a:
            mod_head = sb("mod_head", [16, CHUNK], on=a)
        gq = sb("gq", [GQA_HEADS, SEQ], on=mix0)
        kg = sb("kg", [GQA_KV, KEYS], on=mix0)
        kr_hi = sb("kr_hi", [KEYS], F32R, mix0)
        kr_lo = sb("kr_lo", [KEYS], F32R, mix0)
        vg = sb("vg", [TK, GQA_KV * HD], on=mix0)
        with ExitStack() as a:
            cq_hi = sb("cq_hi", [KQ, SEQ], F32R, a)
            cq_lo = sb("cq_lo", [KQ, SEQ], F32R, a)
            ckv_hi = sb("ckv_hi", [KKV, KEYS], F32R, a)
            ckv_lo = sb("ckv_lo", [KKV, KEYS], F32R, a)
        probs_t = sb("probs_t", [2, TK, SEQ], on=mix0)
        mod_acc0 = [sb("mod_acc0_even", [2, BLOCK], on=mix0)]
        with ExitStack() as a:
            hc_hi = sb("hc_hi", [KD, CTX], F32R, a)
            hc_lo = sb("hc_lo", [KD, CTX], F32R, a)
            with ExitStack() as b:
                ctx_x = sb("ctx_x", [KD, CTX], on=b)
            ckv_raw = sb("ckv_raw", [KKV, KEYS], on=a)
        qn_hi = sb("qn_hi", [MLA_HEADS, SEQ], F32R, mix0)
        q_rope = sb("q_rope", [MLA_HEADS, SEQ], F32R, mix0)
        kn_hi = sb("kn_hi", [MLA_HEADS, KEYS], F32R, mix0)
        qn_lo, kn_lo = h_hi[:, KD - MLA_HEADS:KD, :], h_lo[:, KD - MLA_HEADS:KD, :]
        with ExitStack() as a:
            sq = [sb(f"sq{i}", [KEYS], on=a) for i in range(2)]
            kr_raw = sb("kr_raw", [KEYS], on=a)
            kg_raw = sb("kg_raw", [GQA_KV, KEYS], on=a)
        vm = sb("vm", [TK, MLA_HEADS * P], on=mix0)
        sq_acc_a = sb("sq_acc_a", [KEYS], on=mix0)
        with ExitStack() as a:
            knx = sb("knx", [SEQ], on=a)
            q_raw = sb("q_raw", [2, SEQ], on=a)
            tmp = sb("tmp", [3, SEQ], on=a)
        probs = sb("probs", [3, KEYS], on=mix0)
        mod_acc0.append(sb("mod_acc0_odd", [2, BLOCK], on=mix0))
        kc_lo = sb("kc_lo", [MLA_HEADS, CTX], F32R, mix0)
        mix0.close()

        cs = sb("cs", [2, TX, SEQ])
        cs_small = sb("cs_small", [2 * P])
        sq_b = [sb(f"sq_b{i}", [SEQ]) for i in range(2)]
        tmp_b = sb("tmp_b", [3, SEQ])
        sq_acc_b = sb("sq_acc_b", [SEQ])
        mod_acc1 = sb("mod_acc1", [3, 2, BLOCK])
        with ExitStack() as a:
            hid_hi = sb("hid_hi", [KD, SEQ], F32R, a)
            hid_lo = sb("hid_lo", [KD, SEQ], F32R, a)
            relu = sb("relu", [2, SEQ], on=a)
            relu2 = sb("relu2", [2, SEQ], on=a)
        part = sb("part", [KCH, SEQ])
        product_of_tap = sb("product_of_tap", [PRODUCTS, SEQ])
        f_t = sb("f_t", [GROUPS, SEQ])
        f_mid = sb("f_mid", [TX, GROUPS, 2 * P])
        gate = sb("gate", [2, SEQ])
        u = sb("u", [KCH, SEQ + 2 * PAD])
        conv = sb("conv", [KCH, SEQ])
        cent = sb("cent", [KCH, SEQ])

        c_landed, vec_landed, tab_landed = sem("c_landed"), sem("vec_landed"), sem("tab_landed")
        ident_landed = sem("ident_landed")
        x_landed, ctx_landed, dft_landed = sem("x_landed"), sem("ctx_landed"), sem("dft_landed")
        head_landed = [sem(f"head_landed{b}") for b in range(2 + 8)]
        head_summed = sem("head_summed")
        staged = [sem(f"staged{s}") for s in range(STAGES)]
        out_written = sem("out_written")
        consts_set, pads_set = sem("consts_set"), sem("pads_set")
        chunk_done = sem("chunk_done")
        w_high = sem("w_high")
        filled = [sem(f"filled{b}") for b in range(8)]
        drained = [sem(f"drained{b}") for b in range(8)]
        values_half = sem("values_half")
        sum_ready = sem("sum_ready")
        h_pooled = sem("h_pooled")
        silu_done = sem("silu_done")
        sq_ready = sem("sq_ready")
        sq_summed = sem("sq_summed")
        mod_summed = sem("mod_summed")
        var_ready, rstd_ready = sem("var_ready"), sem("rstd_ready")
        scale_spread = sem("scale_spread")
        latent_high = sem("latent_high")
        rope_high, rope_split = sem("rope_high"), sem("rope_split")
        t_ready, hh_ready, h_ready = sem("t_ready"), sem("hh_ready"), sem("h_ready")
        knx_ready, rotated, rot_used = sem("knx_ready"), sem("rotated"), sem("rot_used")
        cq_ready, ckv_scaled, ckvh_ready, ckv_ready = (sem("cq_ready"), sem("ckv_scaled"), sem("ckvh_ready"),
                                                       sem("ckv_ready"))
        scored, top_ready, exp_done, probs_ready = sem("scored"), sem("top_ready"), sem("exp_done"), sem("probs_ready")
        turned, turned_copied, oh_ready = sem("turned"), sem("turned_copied"), sem("oh_ready")
        hidh_ready, hid_ready = sem("hidh_ready"), sem("hid_ready")
        fh_ready, conv_step, cent_ready, y_ready, s_ready, sh_ready, mix_ready = (
            sem("fh_ready"), sem("conv_step"), sem("cent_ready"), sem("y_ready"), sem("s_ready"), sem("sh_ready"),
            sem("mix_ready"))
        tap_ready, tap_added = sem("tap_ready"), sem("tap_added")
        y_tile = sem("y_tile")
        dve_step = sem("dve_step")

        dve_taps = plan_taps([TAPS - n for n in POOL_TAPS], 6)
        pool_taps = plan_taps(POOL_TAPS, 5)

        block = life.enter_context(nc.Block())

        def v(name, n=0, w=1):
            return vec[:, VEC[name] + n:VEC[name] + n + w]

        def bank_of(key):
            return ps[:, AT[key][0], :]

        def staged_value(n, at=0):
            return 16 * (n // STAGES + 1) + at * 16

        def mlp_offsets(l):
            if l:
                return list(range(MLP_W)), []
            return [0, *(2 * s - 1 for s in range(1, 13)), 25, 26, 27], [2 * q + 2 for q in range(MLP_M)]

        def mod_row(b):
            return probs[0:2, 2, 0:BLOCK] if b == 3 else mod_acc0[1][0:2, b // 2, :]

        def scores(pair):
            return ps[:, pair:pair + 2, :].rearrange("p a b -> p (a b)")[:, 0:KEYS]

        def low_ready(engine, a, k):
            pooled, own = lows_before(a * KD + k + 1)
            if k in POOL_LOWS:
                engine.wait_ge(h_pooled, pooled)
            else:
                engine.wait_ge(h_ready, own)

        def full_sum(a, n):
            return q_raw[:, n % 2, :] if a < 2 else product_of_tap[:, n % 2, :]

        @block.sync
        def _(sp):
            sp.dma_start(c_in[:], c_cols).then_inc(c_landed, 16)
            for b in range(4):
                n = 4 if b < 2 else 1
                for c in range(4 * b, 4 * b + 4, n):
                    sp.dma_start(mod_head[:, c:c + n, :], mod0_head[c:c + n].rearrange("c p n -> p c n")) \
                        .then_inc(head_landed[b if b < 2 else c - 6], 16)
                if b == 1:
                    sp.dma_start(x[:], x_t.rearrange("k p t -> p k t")).then_inc(x_landed, 16)
                    sp.dma_start(ident, tables[:, TAB["ident"]:TAB["ident"] + P]).then_inc(ident_landed, 16)
                    sp.dma_start(vec[:], vectors).then_inc(vec_landed, 16)

            def load(n, src, later=0):
                if n >= STAGES:
                    sp.wait_ge(chunk_done, n - STAGES + 1 + later)
                sp.dma_start(stage[:, n % STAGES, :], src).then_inc(staged[n % STAGES], 16)

            for w in range(NW_IN):
                load(w, w_mix0[w])
                if w == 1:
                    sp.dma_start(ctx_x[:], ctx_t.rearrange("k p t -> p k t")).then_inc(ctx_landed, 16)
                    for lo_c, hi_c in ((0, TAB["ident"]), (TAB["ident"] + P, NTAB)):
                        sp.dma_start(tab[:, lo_c:hi_c], tables[:, lo_c:hi_c]).then_inc(tab_landed, 16)
            for m in range(NM0):
                load(NW_IN + m, mod0[m])
            for j in range(KD):
                load(N_WOUT + j, w_mix0[NW_IN + j])
            bank, use = AT[("wo", 0)]
            sp.wait_ge(drained[bank], use)
            sp.dma_start(cs[:], dft).then_inc(dft_landed, 16)
            sp.dma_start(cs_small[:], dft_small).then_inc(dft_landed, 16)
            for l, (n0, weights) in enumerate(((N_MLP0, w_mlp0), (N_MLP1, w_mlp1))):
                w_at, m_at = mlp_offsets(l)
                per = len(w_at) + len(m_at)
                with sp.Fori(0, FFG) as i:
                    for o in range(per):
                        src = (weights[bass.ds(i * MLP_W + w_at.index(o), 1)] if o in w_at
                               else mod1[bass.ds(i * MLP_M + m_at.index(o), 1)])
                        load(n0 + o, src.rearrange("a p n -> (a p) n"), i * per)
                if l == 0:
                    for c in range(NFI + KD):
                        load(N_FC + c, w_fc[c])
            for k in range(KD):
                sp.wait_ge(y_tile, k + 1)
                sp.dma_start(out[k], x[:, k, :]).then_inc(out_written, 16)
            sp.wait_ge(out_written, 16 * KD)

        @block.gpsimd
        def _(pool):
            pool.memset(ones[:], 1.0).then_inc(consts_set, 1)
            pool.memset(meanw[:], -1.0 / CH).then_inc(consts_set, 1)
            pool.memset(minus_half[:], -0.5).then_inc(consts_set, 1)
            pool.wait_ge(consts_set, 3)

            def inverse_root(e):
                n = EVENTS[e][2]
                pool.wait_ge(var_ready, e + 1)
                pool.tensor_tensor(rstd[:, e, 0:n], var[:, e, 0:n], minus_half[:, 0:n], ALU.pow).then_inc(rstd_ready, 1)

            def add_square(e, j):
                q, width = SQ0[e] + j, (CTX if EVENTS[e][4] == "c" else SEQ)
                buf = (sq if e < EV["x1"] else sq_b)[q % 2][:, 0:width]
                sq_acc = sq_acc_a if e < EV["x1"] else sq_acc_b
                if j == 0 and e:
                    pool.wait_ge(var_ready, e)
                if j:
                    pool.wait_ge(sq_summed, q)
                pool.wait_ge(sq_ready, q + 1)
                if j == 0:
                    ins = pool.tensor_copy(sq_acc[:, 0:width], buf)
                else:
                    ins = pool.tensor_tensor(sq_acc[:, 0:width], sq_acc[:, 0:width], buf, ALU.add)
                ins.then_inc(sq_summed, 1)

            def mean_square(e):
                if EVENTS[e][1] > 2:
                    for j in range(EVENTS[e][1] - 1):
                        add_square(e, j)
                inverse_root(e)

            def halves(acc, chunk, later=0):
                pool.wait_ge(chunk_done, chunk + 1 + later)
                pool.tensor_tensor(acc[:, 0, :], acc[:, 0, :], acc[:, 1, :], ALU.add).then_inc(mod_summed, 1)

            def low(a, k, hi, lo, width):
                n = lows_before(a * KD + k)[0]
                pool.wait_ge(hh_ready, a * KD + k + 1)
                pool.wait_ge(sum_ready, n + 1)
                pool.tensor_tensor(lo[:, k, :], full_sum(a, n)[:, 0:width], hi[:, k, :].bitcast(F32),
                                   ALU.subtract).then_inc(h_pooled, 1)

            mean_square(EV["x0"])
            for k in range(KD):
                if k in POOL_LOWS:
                    low(0, k, h_hi, h_lo, SEQ)
                if k < KD - 1:
                    add_square(EV["ctx0"], k)
            inverse_root(EV["ctx0"])
            for k in POOL_LOWS:
                low(1, k, hc_hi, hc_lo, CTX)
            for e in range(EV["ckv"], EV["ln"]):
                if e == EV["x1"]:
                    for b in range(KD):
                        halves(mod_acc0[b % 2], NW_IN + 4 * b + 3)
                if e == EV["cq"]:
                    pool.wait_ge(knx_ready, GQA_KV)
                if e < EV["x2"]:
                    mean_square(e)
                    if e == EV["x1"]:
                        for k in POOL_LOWS:
                            low(2, k, h_hi, h_lo, SEQ)
                else:
                    at = [N_MLP0 + mlp_offsets(0)[1][4 * b + 3] for b in range(3)]
                    per = MLP_W + MLP_M
                    with pool.Fori(0, FFG - 1) as i:
                        for b in range(3):
                            halves(mod_acc1[:, b], at[b], per * i)
                    for b in range(3):
                        halves(mod_acc1[:, b], at[b], per * (FFG - 1))
                    mean_square(e)
                    for k in POOL_LOWS:
                        low(3, k, h_hi, h_lo, SEQ)
                    pool.memset(u[:, :, 0:PAD], 0.0).then_inc(pads_set, 1)
                    pool.memset(u[:, :, PAD + SEQ:SEQ + 2 * PAD], 0.0).then_inc(pads_set, 1)
                    pool.wait_ge(pads_set, 2)
            ready, added, last = 0, 0, {}
            for i, n in sum(pool_taps, []):
                ready += 1
                if n:
                    pool.wait_ge(tap_ready, ready)
                    if n > 1:
                        pool.wait_ge(tap_added, last[i])
                    pool.tensor_tensor(part[:, i, :], part[:, i, :], product_of_tap[:, added % PRODUCTS, :],
                                       ALU.add).then_inc(tap_added, 1)
                    added += 1
                    last[i] = added
            for e in range(EV["ln"], len(EVENTS)):
                mean_square(e)
                if e == EV["x3"]:
                    for k in POOL_LOWS:
                        low(4, k, h_hi, h_lo, SEQ)

        @block.scalar
        def _(act):
            def full(key, later=0):
                bank, use = AT[key]
                act.wait_ge(filled[bank], use + later)
                return ps[:, bank, :]

            def free(ins, key):
                ins.then_inc(drained[AT[key][0]], 1)

            def split_high(n, w, slot_key, staged_later=0, key_later=0):
                act.wait_ge(staged[n % STAGES], 16 * (n // STAGES + 1) + staged_later)
                if slot_key is not None:
                    full(slot_key, key_later)
                act.activation(w_hi[:, w % SLOTS, :], stage[:, n % STAGES, :], ACT.Copy).then_inc(w_high, 1)

            def square(q, in_ap):
                buf = (sq if q < SQ0[EV["x1"]] else sq_b)[q % 2]
                if q >= 2:
                    act.wait_ge(sq_summed, q - 1)
                return act.activation(buf[:, 0:in_ap.shape[1]], in_ap, ACT.Square)

            def modulated_high(a, shift, hi, width, t, beside=None):
                for k in range(KD):
                    act.wait_ge(t_ready, a * KD + k + 1)
                    act.activation(hi[:, k, :], t[:, (a * KD + k) % 3, 0:width], ACT.Identity,
                                   bias=shift[:, k:k + 1]).then_inc(hh_ready, 1)
                    if k in POOL_LOWS:
                        n = lows_before(a * KD + k)[0]
                        if n >= 2:
                            act.wait_ge(h_pooled, n - 1)
                        act.activation(full_sum(a, n)[:, 0:width], t[:, (a * KD + k) % 3, 0:width], ACT.Identity,
                                       bias=shift[:, k:k + 1]).then_inc(sum_ready, 1)
                    if beside:
                        beside(k)

            def square_x(event, k, key):
                bank, use = AT[key]
                act.wait_ge(drained[bank], use)
                square(SQ0[EV[event]] + k, x[:, k, :]).then_inc(sq_ready, 1)

            act.wait_ge(c_landed, 16)
            act.activation(c_act[:], c_in[:], ACT.Silu).then_inc(silu_done, 1)
            for b in ROW_BLOCKS:
                if b == 2:
                    act.wait_ge(x_landed, 16)
                    for k in range(KD):
                        square(SQ0[EV["x0"]] + k, x[:, k, :]).then_inc(sq_ready, 1)
                if b == 3:
                    split_high(0, 0, None)
                act.activation(mod_row(b), full(("row", b))[0:2, :],
                               ACT.Copy).then_inc(drained[b], 1)
            split_high(1, 1, None)

            def square_ctx(k):
                act.wait_ge(ctx_landed, 16)
                square(SQ0[EV["ctx0"]] + k, ctx_x[:, k, :]).then_inc(sq_ready, 1)

            modulated_high(0, modA[:, 0, :], h_hi, SEQ, tmp, square_ctx)
            modulated_high(1, modA[:, 1, :], hc_hi, CTX, tmp)

            def rope_highs(name, *pairs):
                act.wait_ge(rot_used, ROTS.index(name) + 1)
                for dst, src in zip(pairs[::2], pairs[1::2]):
                    ins = act.activation(dst, src, ACT.Copy)
                ins.then_inc(rope_high, 1)

            for t, name in enumerate(PROJ):
                if t == VALUES[1]:
                    act.wait_ge(values_half, 1)
                    split_high(t + 1, t + 1, None)
                elif t == VALUES[1] + 1:
                    split_high(t + 1, t + 1, ("vg", TK // 2 - 1))
                elif t >= 1:
                    split_high(t + 1, t + 1, ("px", t - 1))
                if t == 5:
                    rope_highs("kr", kr_hi[:, CTX:KEYS], tmp[:, 2, :])
                    for i in range(KKV):
                        act.wait_ge(ckv_scaled, i + 1)
                        act.activation(ckv_hi[:, i, :], ckv_raw[:, i, :], ACT.Copy).then_inc(ckvh_ready, 1)
                if t == VALUES[0]:
                    continue
                if t == VALUES[1]:
                    for n in range(TK // 2):
                        first = (TC + 2 * n) % TK
                        free(act.activation(vg[:, first:first + 2, :],
                                            full(("vg", n)).rearrange("p (t c) -> p t c", t=2), ACT.Copy), ("vg", n))
                    continue
                px = full(("px", t))
                if t < BOTH:
                    pc = full(("pc", t))[:, 0:CTX]
                if name in ("ckv0", "ckv1", "kg0", "kg1"):
                    i = int(name[-1])
                    raw = (ckv_raw if name[0] == "c" else kg_raw)[:, i, :]
                    q = SQ0[EV["ckv"]] + i if name[0] == "c" else SQ0[EV[name]]
                    act.activation(raw[:, CTX:KEYS], px, ACT.Copy)
                    act.wait_ge(sq_summed, q - 1)
                    free(act.activation(sq[q % 2][:, CTX:KEYS], px, ACT.Square), ("px", t))
                    free(act.activation(raw[:, 0:CTX], pc, ACT.Copy), ("pc", t))
                    act.wait_ge(drained[AT[("pc", t)][0]], AT[("pc", t)][1])
                    act.activation(sq[q % 2][:, 0:CTX], raw[:, 0:CTX], ACT.Square).then_inc(sq_ready, 1)
                elif name == "kr":
                    free(act.activation(kr_raw[:, CTX:KEYS], px, ACT.Copy), ("px", t))
                    act.activation(kr_hi[:, 0:CTX], pc, ACT.Copy)
                    free(act.activation(kr_raw[:, 0:CTX], pc, ACT.Copy), ("pc", t))
                elif name[:2] == "cq":
                    i = int(name[2])
                    act.activation(cq_hi[:, i, :], px, ACT.Copy, scale=v("qg", i))
                    square(SQ0[EV["cq"]] + i, px).then_inc(sq_ready, 1)
                else:
                    i = int(name[2])
                    square(SQ0[EV[name]], px).then_inc(sq_ready, 1)
                    if i >= 2:
                        act.wait_ge(rot_used, ROTS.index(name) - 1)
                    free(act.activation(q_raw[:, i % 2, :], px, ACT.Copy, scale=v("gqg")), ("px", t))

            split_high(UQ0 + 1, UQ0 + 1, ("px", NPROJ - 1))
            for i in range(2):
                act.activation(qn_hi[:, i, :], full(("uq", 0, i)), ACT.Copy).then_inc(latent_high, 1)
            split_high(UQR, UQR, ("uq", 0, 1))
            for i in range(2):
                act.activation(qn_hi[:, 2 + i, :], full(("uq", 1, i)), ACT.Copy).then_inc(latent_high, 1)
            split_high(UKK, UKK, ("uq", 1, 1))
            for i in range(2):
                act.wait_ge(rot_used, ROTS.index(f"qr{i}") - 1)
                free(act.activation(q_raw[:, i, :], full(("uq", 2, i)), ACT.Copy), ("uq", 2, i))
            split_high(UKV, UKV, ("uq", 2, 1))
            for n in range(2):
                for h in (2 * n, 2 * n + 1):
                    act.activation(kn_hi[:, h, CTX:KEYS], full(("kx", h)), ACT.Copy).then_inc(latent_high, 1)
                act.activation(kn_hi[:, 2 * n:2 * n + 2, 0:CTX],
                               full(("kc", n)).rearrange("p (h t) -> p h t", t=CTX), ACT.Copy).then_inc(latent_high, 1)
                rope_highs(f"qr{n}", q_rope[0:ROPE, 2 * n, :], tmp[0:ROPE, 2, :],
                           q_rope[ROPE:P, 2 * n + 1, :], tmp[ROPE:P, 2, :])
            for t in range(TK):
                free(act.activation(vm[:, t, :], full(("v", t)), ACT.Copy), ("v", t))

            for s in range(4 * HEADS + 4):
                if s == 4 * HEADS + 3:
                    split_high(N_WOUT, W_WOUT, ("v", TK - 1))
                    split_high(N_WOUT + 1, W_WOUT + 1, ("v", TK - 1))
                if s in OUT_STEP:
                    h = OUT_STEP[s]
                    act.activation(h_hi[:, h, :], full(("pv", h)), ACT.Copy).then_inc(oh_ready, 1)
                if 2 <= s < 4 * HEADS + 2:
                    n = s - 2
                    h, qt = n // 4, n % 4
                    act.wait_ge(turned, n + 1)
                    act.activation(probs_t[:, h % 2, :, qt * P:qt * P + P].rearrange("p (a b) c -> p a b c", a=2),
                                   ps[:, 4:6, 0:3 * P].rearrange("p a (b c) -> p a b c", c=P),
                                   ACT.Copy).then_inc(turned_copied, 1)
                if s < 4 * HEADS:
                    h, qt = s // 4, s % 4
                    pair = 2 * (s % 2)
                    act.wait_ge(top_ready, s + 1)
                    if s >= 3:
                        act.wait_ge(turned, s - 2)
                    head_scale = row_scale[:, max(h - MLA_HEADS + 1, 0), qt:qt + 1]
                    act.activation(probs[:, s % 3, :], scores(pair),
                                   ACT.Exp, bias=minus_top[:, s:s + 1], scale=head_scale,
                                   accum_out=psum_row[:, s:s + 1]).then_inc(exp_done, 1)

            for j in range(KD):
                n, w = (N_WOUT + j + 2, W_WOUT + j + 2) if j < KD - 2 else (N_MLP0 + j - KD + 2, W_MLP0 + j - KD + 2)
                if j < KD - 1:
                    split_high(n, w, ("wo", j))
                if j >= 1:
                    square_x("x1", j - 1, ("wo", j - 1))
            square_x("x1", KD - 1, ("wo", KD - 1))
            split_high(n, w, ("wo", KD - 1))
            modulated_high(2, modc0[:, KD:2 * KD], h_hi, SEQ, tmp_b)

            def mlp(l, i, last):
                n0, w0 = (N_MLP0, W_MLP0) if l == 0 else (N_MLP1, W_MLP1)
                w_at, m_at = mlp_offsets(l)
                per = len(w_at) + len(m_at)
                for s in range(MLP_W):
                    o = w_at[s + 2] if s + 2 < MLP_W else per + s + 2 - MLP_W
                    if not last or s + 2 < MLP_W:
                        split_high(n0 + o, w0 + s + 2, ("mlp", l, s), 16 * per // STAGES * i, PER[l][s % 4] * i)
                    if s < KD:
                        key = ("mlp", l, s)
                        p = full(key, PER[l][s % 4] * i)
                        if s >= 2:
                            act.wait_ge(hid_ready, l * FFG * KD + s - 1 + KD * i)
                        free(act.activation(relu[:, s % 2, :], p, ACT.Relu), key)
                        act.wait_ge(drained[AT[key][0]], AT[key][1] + PER[l][s % 4] * i)
                        act.activation(hid_hi[:, s, :], relu[:, s % 2, :], ACT.Square).then_inc(hidh_ready, 1)
                    elif last and s > KD:
                        bank, use = AT[("mlp", l, s - 1)]
                        act.wait_ge(drained[bank], use + PER[l][bank] * i)
                        square(SQ0[EV["x2" if l == 0 else "x4"]] + s - KD - 1, x[:, s - KD - 1, :]).then_inc(sq_ready, 1)
                        if l == 0 and s == MLP_W - 2:
                            split_high(n0 + o, w0 + s + 2, ("mlp", l, s), 16 * per // STAGES * i, PER[l][s % 4] * i)
                if last:
                    bank, use = AT[("mlp", l, MLP_W - 1)]
                    act.wait_ge(drained[bank], use + PER[l][bank] * i)
                    square(SQ0[EV["x2" if l == 0 else "x4"]] + KD - 1, x[:, KD - 1, :]).then_inc(sq_ready, 1)
                    if l == 0:
                        split_high(n0 + o, w0 + s + 2, ("mlp", l, s), 16 * per // STAGES * i, PER[l][s % 4] * i)

            with act.Fori(0, FFG - 1) as i:
                mlp(0, i, False)
            mlp(0, FFG - 1, True)

            modulated_high(3, modc1[:, 0:KD], h_hi, SEQ, tmp_b)
            adds = [0]

            def tap_products(c):
                for i, n in pool_taps[c]:
                    w = v("convw", i * TAPS + TAPS - POOL_TAPS[i] + n)
                    src = u[:, i, TAPS - POOL_TAPS[i] + n:TAPS - POOL_TAPS[i] + n + SEQ]
                    if n == 0:
                        bank, use = AT[("fi", FI.index(f"a{i}"))]
                        act.wait_ge(drained[bank], use)
                        act.wait_ge(pads_set, 2)
                        dst = part[:, i, :]
                    else:
                        if adds[0] >= PRODUCTS:
                            act.wait_ge(tap_added, adds[0] - PRODUCTS + 1)
                        dst = product_of_tap[:, adds[0] % PRODUCTS, :]
                        adds[0] += 1
                    act.activation(dst, src, ACT.Copy, scale=w).then_inc(tap_ready, 1)

            for c, name in enumerate(FI):
                split_high(N_FC + c + 2, W_FC + c + 2, ("fi", c))
                key = ("fi", c)
                i = int(name[1])
                if name[0] == "g":
                    if i >= 2:
                        bank, use = AT[("fi", FI.index(f"a{i - 2}"))]
                        act.wait_ge(drained[bank], use)
                    free(act.activation(gate[:, i % 2, :], full(key), ACT.Sigmoid), key)
                elif name[0] == "f":
                    free(act.activation(f_t[:, i, :], full(key), ACT.Copy), key)
                    if i >= 1:
                        for b in range(2):
                            free(act.activation(f_mid[:, 2 * b:2 * b + 2, i - 1, :],
                                                full(("f1", i - 1, b)).rearrange("p (t c) -> p t c", t=2),
                                                ACT.Copy), ("f1", i - 1, b))
                tap_products(c)
            tap_products(NFI)
            for b in range(2):
                free(act.activation(f_mid[:, 2 * b:2 * b + 2, GROUPS - 1, :],
                                    full(("f1", GROUPS - 1, b)).rearrange("p (t c) -> p t c", t=2),
                                    ACT.Copy), ("f1", GROUPS - 1, b))
            for g in range(GROUPS):
                act.activation(h_hi[:, g, :], full(("f2", g)), ACT.Copy,
                               scale=float((SEQ * P) ** -0.5)).then_inc(fh_ready, 1)
                if g == 1:
                    for i in range(KCH):
                        act.wait_ge(cent_ready, i + 1)
                        square(SQ0[EV["ln"]] + i, cent[:, i, :]).then_inc(sq_ready, 1)
            for i in range(KCH + 1):
                if i < KCH:
                    act.wait_ge(y_ready, i + 1)
                    act.activation(conv[:, i, :], cent[:, i, :], ACT.Silu, bias=v("lnb", i),
                                   scale=v("lng", i)).then_inc(s_ready, 1)
                if i >= 1:
                    act.wait_ge(s_ready, i)
                    act.activation(h_hi[:, KCH + i - 1, :], conv[:, i - 1, :], ACT.Copy).then_inc(sh_ready, 1)
            for j in range(KD):
                n, w = (N_FCOUT + j + 2, W_FCOUT + j + 2) if j < KD - 2 else (N_MLP1 + j - KD + 2, W_MLP1 + j - KD + 2)
                if j < KD - 1:
                    split_high(n, w, ("fo", j))
                if j >= 1:
                    square_x("x3", j - 1, ("fo", j - 1))
            square_x("x3", KD - 1, ("fo", KD - 1))
            split_high(n, w, ("fo", KD - 1))
            modulated_high(4, modc1[:, 3 * KD:4 * KD], h_hi, SEQ, tmp_b)
            with act.Fori(0, FFG - 1) as i:
                mlp(1, i, False)
            mlp(1, FFG - 1, True)

        @block.vector
        def _(dve):
            own = [0]

            def tick(ins):
                ins.then_inc(dve_step, 1)
                own[0] += 1
                return own[0]

            def own_wait(count, later=0):
                dve.wait_ge(dve_step, count + later)

            def full(key, later=0):
                bank, use = AT[key]
                dve.wait_ge(filled[bank], use + later)
                return ps[:, bank, :]

            def free(ins, key):
                ins.then_inc(drained[AT[key][0]], 1)

            def split_low(n, w, w_later=0, n_later=0):
                dve.wait_ge(w_high, w + 1 + w_later)
                dve.tensor_tensor(w_lo[:, w % SLOTS, :], stage[:, n % STAGES, :],
                                  w_hi[:, w % SLOTS, :].bitcast(F32), ALU.subtract).then_inc(chunk_done, 1)

            def mod_chunk(n, block_acc, q, staged_later=0, n_before=None, n_later=0):
                dve.wait_ge(staged[n % STAGES], 16 * (n // STAGES + 1) + staged_later)
                if q:
                    dve.wait_ge(chunk_done, n_before + 1 + n_later)
                for k2 in range(2):
                    k = 2 * q + k2
                    src = stage[:, n % STAGES, k2 * BLOCK:(k2 + 1) * BLOCK]
                    acc = block_acc[:, k2, :]
                    if q == 0:
                        ins = dve.tensor_scalar(acc, src, c_act[:, 2 * k:2 * k + 1], None, ALU.mult)
                    else:
                        ins = dve.scalar_tensor_tensor(out=acc, in0=src, scalar=c_act[:, 2 * k:2 * k + 1], in1=acc,
                                                       op0=ALU.mult, op1=ALU.add)
                ins.then_inc(chunk_done, 1)

            def variance(e):
                n, width = EVENTS[e][2], EVENTS[e][3]
                dve.wait_ge(sq_summed, SQ0[e + 1])
                dve.tensor_scalar(var[:, e, 0:n], ps[:, 7, 0:n], 1.0 / width, EPS, ALU.mult, ALU.add) \
                    .then_inc(var_ready, 1)

            def modulated(a, e, src, gain, shift, hi, lo, width, bank, t):
                dve.wait_ge(scale_spread, BC[e] + 1)
                for k in range(KD + 1):
                    if k < KD:
                        g = a * KD + k
                        if g >= 3 and (g - 3) % KD in POOL_LOWS:
                            dve.wait_ge(sum_ready, lows_before(g - 2)[0])
                        elif g >= 3:
                            dve.wait_ge(h_ready, lows_before(g - 2)[1])
                        ins = dve.scalar_tensor_tensor(out=t[:, g % 3, 0:width], in0=src[:, k, :],
                                                       scalar=gain[:, k:k + 1], in1=ps[:, bank, 0:width],
                                                       op0=ALU.mult, op1=ALU.mult).then_inc(t_ready, 1)
                    if k >= 1 and k - 1 not in POOL_LOWS:
                        dve.wait_ge(hh_ready, a * KD + k)
                        dve.scalar_tensor_tensor(out=lo[:, k - 1, :], in0=t[:, (a * KD + k - 1) % 3, 0:width],
                                                 scalar=shift[:, k - 1:k], in1=hi[:, k - 1, :].bitcast(F32),
                                                 op0=ALU.add, op1=ALU.subtract).then_inc(h_ready, 1)

            def add_product(key, k, g, later=0):
                p = full(key, later)
                free(dve.scalar_tensor_tensor(out=x[:, k, :], in0=p, scalar=g, in1=x[:, k, :], op0=ALU.mult,
                                              op1=ALU.add), key)

            def rope(name, src, x_ready, dsts):
                r = ROTS.index(name)
                c, s = ("cosm", "sinm") if name[1] == "r" else ("cosg", "sing")
                x_ready()
                if r:
                    dve.wait_ge(rot_used, r)
                else:
                    low_ready(dve, 1, KD - 1)
                dve.tensor_tensor(tmp[:, 0, :], src, tab[:, TAB[c]:TAB[c] + SEQ], ALU.mult)
                dve.wait_ge(rotated, r + 1)
                done = tick(dve.tensor_tensor(tmp[:, 1, :], ps[:, 4, :], tab[:, TAB[s]:TAB[s] + SEQ], ALU.mult))
                own_wait(done)
                for dst, lo_p, hi_p in dsts:
                    ins = dve.tensor_tensor(dst, tmp[lo_p:hi_p, 0, :], tmp[lo_p:hi_p, 1, :], ALU.add)
                ins.then_inc(rot_used, 1)

            def drained_key(key):
                bank, use = AT[key]
                return lambda: dve.wait_ge(drained[bank], use)

            dve.wait_ge(silu_done, 1)
            dve.wait_ge(head_landed[1], 16)
            for k in range(KD):
                w = mod_head[:, 4 + k // 2, k % 2 * BLOCK:(k % 2 + 1) * BLOCK]
                for s in range(2):
                    scale = c_act[:, 2 * k + s:2 * k + s + 1]
                    if k == 0:
                        ins = dve.tensor_scalar(probs[:, s, 0:BLOCK], w, scale, None, ALU.mult)
                    else:
                        dve.wait_ge(head_summed, 2 * k + s - 1)
                        ins = dve.scalar_tensor_tensor(out=probs[:, s, 0:BLOCK], in0=w, scalar=scale, in1=probs[:, s, 0:BLOCK],
                                                       op0=ALU.mult, op1=ALU.add)
                    ins.then_inc(head_summed, 1)
            variance(EV["x0"])
            split_low(0, 0)
            dve.wait_ge(vec_landed, 16)
            cols = full("mod columns x")[:, 0:4 * KD].rearrange("p (j s) -> p s j", s=2)
            for s in range(2):
                ins = dve.tensor_tensor(modA[:, s, :], cols[:, s, :], v("modb", 0, 2 * KD), ALU.add)
            free(ins, "mod columns x")
            drained_key("mod columns x")()
            for s in range(2):
                done = tick(dve.scalar_tensor_tensor(out=modG[:, s, :], in0=modA[:, s, KD:2 * KD], scalar=1.0,
                                                     in1=v("n1", 0, KD), op0=ALU.add, op1=ALU.mult))
            own_wait(done)
            modulated(0, EV["x0"], x, modG[:, 0, :], modA[:, 0, :], h_hi, h_lo, SEQ, 5, tmp)
            variance(EV["ctx0"])
            split_low(1, 1)
            modulated(1, EV["ctx0"], ctx_x, modG[:, 1, :], modA[:, 1, :], hc_hi, hc_lo, CTX, 6, tmp)

            def kr_rope():
                dve.wait_ge(tab_landed, 32)
                drained_key(("pc", 2))()
                rope("kr", kr_raw[:, CTX:KEYS], drained_key(("pc", 2)), [(tmp[:, 2, :], 0, P)])

            def kr_low():
                dve.wait_ge(rope_high, 1)
                dve.tensor_tensor(kr_lo[:, CTX:KEYS], tmp[:, 2, :], kr_hi[:, CTX:KEYS].bitcast(F32), ALU.subtract)
                dve.tensor_tensor(kr_lo[:, 0:CTX], kr_raw[:, 0:CTX], kr_hi[:, 0:CTX].bitcast(F32),
                                  ALU.subtract).then_inc(rope_split, 1)

            def q_rope_low(n):
                dve.wait_ge(rope_high, n + 2)
                for h, rows, others in ((2 * n, slice(0, ROPE), slice(ROPE, P)),
                                        (2 * n + 1, slice(ROPE, P), slice(0, ROPE))):
                    ins = dve.tensor_tensor(q_rope[others, h, :], tmp[rows, 2, :], q_rope[rows, h, :].bitcast(F32),
                                            ALU.subtract)
                ins.then_inc(rope_split, 1)

            highs = [0]

            def latent_low(key, dst, hi, form=lambda p: p):
                highs[0] += 1
                dve.wait_ge(latent_high, highs[0])
                free(dve.tensor_tensor(dst, form(full(key)), hi.bitcast(F32), ALU.subtract), key)

            def scale_ckv():
                dve.wait_ge(scale_spread, BC[EV["ckv"]] + 1)
                for i in range(KKV):
                    for bank, lo_t, hi_t in ((6, 0, CTX), (5, CTX, KEYS)):
                        ins = dve.scalar_tensor_tensor(out=ckv_raw[:, i, lo_t:hi_t], in0=ckv_raw[:, i, lo_t:hi_t],
                                                       scalar=v("kvg", i), in1=ps[:, bank, 0:hi_t - lo_t],
                                                       op0=ALU.mult, op1=ALU.mult)
                    ins.then_inc(ckv_scaled, 1)

            def low_ckv():
                for i in range(KKV):
                    dve.wait_ge(ckvh_ready, i + 1)
                    dve.tensor_tensor(ckv_lo[:, i, :], ckv_raw[:, i, :], ckv_hi[:, i, :].bitcast(F32),
                                      ALU.subtract).then_inc(ckv_ready, 1)

            def scale_kg(i):
                dve.wait_ge(scale_spread, BC[EV[f"kg{i}"]] + 1)
                dve.scalar_tensor_tensor(out=kg[:, i, 0:CTX], in0=kg_raw[:, i, 0:CTX], scalar=v("gkg"),
                                         in1=ps[:, 6, 0:CTX], op0=ALU.mult, op1=ALU.mult)
                dve.scalar_tensor_tensor(out=knx[:], in0=kg_raw[:, i, CTX:KEYS], scalar=v("gkg"), in1=ps[:, 5, :],
                                         op0=ALU.mult, op1=ALU.mult).then_inc(knx_ready, 1)

            def row_scales(e, r, scale):
                dve.wait_ge(rstd_ready, e + 1)
                tick(dve.tensor_scalar(row_scale[:, r, :], rstd[:, e, 0:TX], scale, None, ALU.mult))

            def gq_steps(i):
                variance(EV[f"gq{i}"])
                rope(f"gq{i}", q_raw[:, i % 2, :], drained_key(("px", PROJ.index(f"gq{i}"))), [(gq[:, i, :], 0, P)])
                row_scales(EV[f"gq{i}"], 1 + i, GQA_SCALE)

            for t, name in enumerate(PROJ):
                if t == 3:
                    variance(EV["ckv"])
                if t == 4:
                    scale_ckv()
                    kr_rope()
                if t == 5:
                    variance(EV["kg0"])
                    low_ckv()
                if t == 6:
                    kr_low()
                    scale_kg(0)
                    variance(EV["kg1"])
                if t == 7:
                    rope("kg0", knx[:], lambda: dve.wait_ge(knx_ready, 1), [(kg[:, 0, CTX:KEYS], 0, P)])
                    scale_kg(1)
                if t == 8:
                    rope("kg1", knx[:], lambda: dve.wait_ge(knx_ready, 2), [(kg[:, 1, CTX:KEYS], 0, P)])
                if t == 12:
                    variance(EV["cq"])
                    row_scales(EV["cq"], 0, MLA_SCALE)
                if t >= 13:
                    gq_steps(t - 13)
                if t >= 1:
                    split_low(t + 1, t + 1)
                if name[:2] == "cq":
                    i = int(name[2])
                    px = full(("px", t))
                    dve.wait_ge(sq_ready, SQ0[EV["cq"]] + i + 1)
                    free(dve.scalar_tensor_tensor(out=cq_lo[:, i, :], in0=px, scalar=v("qg", i),
                                                  in1=cq_hi[:, i, :].bitcast(F32), op0=ALU.mult, op1=ALU.subtract),
                         ("px", t))
            gq_steps(2)
            split_low(UQ0 + 1, UQ0 + 1)
            gq_steps(3)
            for n, w in enumerate((UQR, UKK)):
                split_low(w, w)
                for i in range(2):
                    latent_low(("uq", n, i), qn_lo[:, 2 * n + i, :], qn_hi[:, 2 * n + i, :])
            split_low(UKV, UKV)
            for n in range(2):
                for h in (2 * n, 2 * n + 1):
                    latent_low(("kx", h), kn_lo[:, h, :], kn_hi[:, h, CTX:KEYS])
                latent_low(("kc", n), kc_lo[:, 2 * n:2 * n + 2, :], kn_hi[:, 2 * n:2 * n + 2, 0:CTX],
                           lambda p: p.rearrange("p (h t) -> p h t", t=CTX))
                dve.wait_ge(rope_split, n + 1)
                rope(f"qr{n}", q_raw[:, n, :], drained_key(("uq", 2, n)), [(tmp[:, 2, :], 0, P)])
                q_rope_low(n)

            for s in range(4 * HEADS + 4):
                if 1 <= s < 4 * HEADS + 1:
                    n = s - 1
                    dve.wait_ge(exp_done, n + 1)
                    done = tick(dve.reciprocal(inv_row[:, n:n + 1], psum_row[:, n:n + 1]))
                    own_wait(done)
                    dve.tensor_scalar(probs[:, n % 3, :], probs[:, n % 3, :], inv_row[:, n:n + 1], None,
                                      ALU.mult).then_inc(probs_ready, 1)
                if s < 4 * HEADS:
                    h, qt, pair = s // 4, s % 4, 2 * (s % 2)
                    dve.wait_ge(scored, s + 1)
                    done = tick(dve.tensor_reduce(top[:, s:s + 1], scores(pair), AX.X, ALU.max))
                    own_wait(done)
                    dve.tensor_scalar(minus_top[:, s:s + 1], top[:, s:s + 1],
                                      row_scale[:, max(h - MLA_HEADS + 1, 0), qt:qt + 1], -1.0, ALU.mult,
                                      ALU.mult).then_inc(top_ready, 1)
                    b, q = s // 4, s % 4
                    mod_chunk(NW_IN + s, mod_acc0[b % 2], q, n_before=NW_IN + s - 1)
                if s >= 6 and s % 4 == 2:
                    b = (s - 6) // 4
                    p = full(("mc0", b))
                    free(dve.tensor_tensor(modc0[:, 4 * b:4 * b + 4], p[:, 0:4], v("modb", 2 * KD + 4 * b, 4),
                                           ALU.add), ("mc0", b))
                if s == 4 * HEADS + 3:
                    split_low(N_WOUT, W_WOUT)
                    split_low(N_WOUT + 1, W_WOUT + 1)
                if s in OUT_STEP:
                    h = OUT_STEP[s]
                    dve.wait_ge(oh_ready, h + 1)
                    free(dve.tensor_tensor(h_lo[:, h, :], full(("pv", h)), h_hi[:, h, :].bitcast(F32), ALU.subtract),
                         ("pv", h))

            for j in range(KD):
                n, w = (N_WOUT + j + 2, W_WOUT + j + 2) if j < KD - 2 else (N_MLP0 + j - KD + 2, W_MLP0 + j - KD + 2)
                if j < KD - 2:
                    split_low(n, w)
                add_product(("wo", j), j, modc0[:, j:j + 1])
                if j == KD - 2:
                    split_low(n, w)

            def gain(r, scales, norm):
                return tick(dve.scalar_tensor_tensor(out=gains[:, r, :], in0=scales, scalar=1.0, in1=norm, op0=ALU.add,
                                                     op1=ALU.mult))

            def norm_x(r, event, scales, norm, shift, n, w):
                done = gain(r, scales, norm)
                variance(EV[event])
                if event == "x2":
                    mod1_sums(0, FFG - 1)
                split_low(n, w)
                if event == "x2":
                    mod1_sums(1, FFG - 1)
                own_wait(done)
                modulated(2 + r, EV[event], x, gains[:, r, :], shift, h_hi, h_lo, SEQ, 5, tmp_b)

            def mod1_sums(b, i):
                p = full(("mc1", b), PER[0][6] * i)
                cols = bass.ds((3 * i + b) * 4, 4)
                free(dve.tensor_tensor(modc1[:, cols], p[:, 0:4],
                                       vec[:, bass.ds(VEC["modb"] + 6 * KD + (3 * i + b) * 4, 4)], ALU.add),
                     ("mc1", b))

            norm_x(0, "x1", modc0[:, 2 * KD:3 * KD], v("n2", 0, KD), modc0[:, KD:2 * KD], N_MLP0 + 1, W_MLP0 + 1)

            def mlp(l, i, last, gate2):
                n0, w0 = (N_MLP0, W_MLP0) if l == 0 else (N_MLP1, W_MLP1)
                w_at, m_at = mlp_offsets(l)
                per = len(w_at) + len(m_at)
                first = own[0]
                steps = KD * i
                for s in range(MLP_W):
                    if s < len(m_at):
                        b, q = s // 4, s % 4
                        mod_chunk(n0 + m_at[s], mod_acc1[:, b], q, 16 * per // STAGES * i, n0 + m_at[s - 1], per * i)
                    o = w_at[s + 2] if s + 2 < MLP_W else per + s + 2 - MLP_W
                    behind = last and s >= MLP_W - 2
                    if not behind:
                        split_low(n0 + o, w0 + s + 2, MLP_W * i)
                    if l == 0 and s in (6, 10, 14) and not last:
                        mod1_sums((s - 6) // 4, i)
                    key = ("mlp", l, s)
                    if s < KD:
                        bank, use = AT[key]
                        dve.wait_ge(drained[bank], use + PER[l][bank] * i)
                        own[0] += 1
                        dve.tensor_tensor(relu2[:, s % 2, :], relu[:, s % 2, :], relu[:, s % 2, :],
                                          ALU.mult).then_inc(dve_step, 1)
                        dve.wait_ge(hidh_ready, l * FFG * KD + s + 1 + KD * i)
                        own_wait(first + s + 1, steps)
                        dve.tensor_tensor(hid_lo[:, s, :], relu2[:, s % 2, :], hid_hi[:, s, :].bitcast(F32),
                                          ALU.subtract).then_inc(hid_ready, 1)
                    else:
                        add_product(key, s - KD, gate2[:, s - KD:s - KD + 1], PER[l][s % 4] * i)
                    if behind and l == 0 and s < MLP_W - 1:
                        split_low(n0 + o, w0 + s + 2, MLP_W * i)
                own[0] = first

            with dve.Fori(0, FFG - 1) as i:
                mlp(0, i, False, modc0[:, 3 * KD:4 * KD])
            mlp(0, FFG - 1, True, modc0[:, 3 * KD:4 * KD])
            own[0] += FFG * KD

            norm_x(1, "x2", modc1[:, KD:2 * KD], v("n1", KD, KD), modc1[:, 0:KD], N_FC + 1, W_FC + 1)
            mod1_sums(2, FFG - 1)

            steps, last = [0], {}

            def convolve(taps):
                for i, k in taps:
                    w = v("convw", i * TAPS + k)
                    if k == 0:
                        bank, use = AT[("fi", FI.index(f"a{i}"))]
                        dve.wait_ge(drained[bank], use)
                        ins = dve.tensor_scalar(conv[:, i, :], u[:, i, 0:SEQ], w, v("convb", i), ALU.mult, ALU.add)
                    else:
                        dve.wait_ge(conv_step, last[i])
                        ins = dve.scalar_tensor_tensor(out=conv[:, i, :], in0=u[:, i, k:k + SEQ], scalar=w,
                                                       in1=conv[:, i, :], op0=ALU.mult, op1=ALU.add)
                    ins.then_inc(conv_step, 1)
                    steps[0] += 1
                    last[i] = steps[0]

            dve.wait_ge(pads_set, 2)
            for c, name in enumerate(FI):
                split_low(N_FC + c + 2, W_FC + c + 2)
                i = int(name[1])
                if name[0] == "a":
                    p = full(("fi", c))
                    bank, use = AT[("fi", c - 1)]
                    dve.wait_ge(drained[bank], use)
                    free(dve.tensor_tensor(u[:, i, PAD:PAD + SEQ], p, gate[:, i % 2, :], ALU.mult), ("fi", c))
                convolve(dve_taps[c])
            convolve(dve_taps[NFI])
            dve.wait_ge(tap_added, sum(POOL_TAPS) - KCH)
            for i in range(KCH):
                dve.wait_ge(conv_step, last[i])
                dve.tensor_tensor(conv[:, i, :], conv[:, i, :], part[:, i, :], ALU.add).then_inc(conv_step, 1)

            def low_fourier(g):
                dve.wait_ge(fh_ready, g + 1)
                free(dve.scalar_tensor_tensor(out=h_lo[:, g, :], in0=full(("f2", g)), scalar=float((SEQ * P) ** -0.5),
                                              in1=h_hi[:, g, :].bitcast(F32), op0=ALU.mult, op1=ALU.subtract),
                     ("f2", g))

            low_fourier(0)
            low_fourier(1)
            mean = full("mean")
            for i in range(KCH):
                dve.tensor_tensor(cent[:, i, :], conv[:, i, :], mean, ALU.add).then_inc(cent_ready, 1)
            variance(EV["ln"])
            low_fourier(2)
            low_fourier(3)
            dve.wait_ge(scale_spread, BC[EV["ln"]] + 1)
            for i in range(KCH):
                dve.tensor_tensor(cent[:, i, :], cent[:, i, :], ps[:, 5, :], ALU.mult).then_inc(y_ready, 1)
            for i in range(KCH):
                dve.wait_ge(sh_ready, i + 1)
                dve.tensor_tensor(h_lo[:, KCH + i, :], conv[:, i, :], h_hi[:, KCH + i, :].bitcast(F32),
                                  ALU.subtract).then_inc(mix_ready, 1)
            for j in range(KD):
                n, w = (N_FCOUT + j + 2, W_FCOUT + j + 2) if j < KD - 2 else (N_MLP1 + j - KD + 2, W_MLP1 + j - KD + 2)
                if j < KD - 2:
                    split_low(n, w)
                add_product(("fo", j), j, modc1[:, 2 * KD + j:2 * KD + j + 1])
                if j == KD - 2:
                    split_low(n, w)
            norm_x(2, "x3", modc1[:, 4 * KD:5 * KD], v("n2", KD, KD), modc1[:, 3 * KD:4 * KD], N_MLP1 + 1,
                   W_MLP1 + 1)
            with dve.Fori(0, FFG - 1) as i:
                mlp(1, i, False, modc1[:, 5 * KD:6 * KD])
            mlp(1, FFG - 1, True, modc1[:, 5 * KD:6 * KD])

            variance(EV["x4"])
            dve.wait_ge(scale_spread, BC[EV["x4"]] + 1)
            for k in range(KD):
                dve.scalar_tensor_tensor(out=x[:, k, :], in0=x[:, k, :], scalar=v("nf", k), in1=ps[:, 5, :],
                                         op0=ALU.mult, op1=ALU.mult).then_inc(y_tile, 1)

        @block.tensor
        def _(pe):
            def acquire(key, later=0):
                bank, use = AT[key]
                if use > 1:
                    pe.wait_ge(drained[bank], use - 1 + later)
                return ps[:, bank, :]

            def fill(ins, key):
                ins.then_inc(filled[AT[key][0]], 1)

            def product(outp, left, right, first, last, **how):
                (lh, ll), (rh, rl) = left, right
                pe.matmul(outp, lh, rh, start=first, stop=False, **how)
                pe.matmul(outp, lh, rl, start=False, stop=False, **how)
                return pe.matmul(outp, ll, rh, start=False, stop=last, **how)

            def weights(w, lo_c, hi_c):
                return w_hi[:, w % SLOTS, lo_c:hi_c], w_lo[:, w % SLOTS, lo_c:hi_c]

            def tile_product(key, w, n, hi, lo, ready=None, later=0, n_later=0):
                outp = acquire(key, later)[:, 0:hi.shape[2]]
                pe.wait_ge(chunk_done, n + 1 + n_later)
                for k in range(KD):
                    if ready:
                        ready(k)
                    ins = product(outp, weights(w, k * P, k * P + P), (hi[:, k, :], lo[:, k, :]), k == 0, k == KD - 1)
                fill(ins, key)

            def first_tiles(keys, w, n, a):
                outps = [acquire(key) for key in keys]

                def step(c, k):
                    left, out_k = weights(w + c, k * P, k * P + P), outps[c]
                    if c == 0:
                        pe.wait_ge(hh_ready, a * KD + k + 1)
                    pe.matmul(out_k, left[0], h_hi[:, k, :], start=(k == 0), stop=False)
                    pe.matmul(out_k, left[1], h_hi[:, k, :], start=False, stop=False)
                    if c == 0:
                        low_ready(pe, a, k)
                    ins = pe.matmul(out_k, left[0], h_lo[:, k, :], start=False, stop=(k == KD - 1))
                    if k == KD - 1:
                        fill(ins, keys[c])

                pe.wait_ge(chunk_done, n + 1)
                for k in range(KD):
                    step(0, k)
                    if k == 0:
                        pe.wait_ge(chunk_done, n + 2)
                    if k < AHEAD:
                        step(1, k)
                for k in range(AHEAD, KD):
                    step(1, k)

            def sum_squares(e, j):
                n = EVENTS[e][1]
                if n > 2 and j < n - 1:
                    return
                q = SQ0[e] + j
                if j == (n - 1 if n > 2 else 0) and e > 0:
                    pe.wait_ge(var_ready, e)
                parts = [(sq if e < EV["x1"] else sq_b)[q % 2]]
                if n > 2:
                    pe.wait_ge(sq_summed, q)
                    parts = [sq_acc_a if e < EV["x1"] else sq_acc_b, *parts]
                for i, buf in enumerate(parts):
                    if i == len(parts) - 1:
                        pe.wait_ge(sq_ready, q + 1)
                    for t in range(EVENTS[e][2]):
                        ins = pe.matmul(ps[:, 7, t:t + 1], buf[:, t * P:t * P + P], ones[:, 0:1],
                                        start=(t == 0 and i == 0 and (n > 2 or j == 0)),
                                        stop=(j == n - 1 and i == len(parts) - 1), skip_group_check=True)
                ins.then_inc(sq_summed, 1)

            def spread(e):
                pe.wait_ge(rstd_ready, e + 1)
                for t, (bank, col) in enumerate(event_tiles(e)):
                    ins = pe.matmul(ps[:, bank, col:col + P], rstd[:, e, t:t + 1].to_broadcast([P, P]), ident,
                                    start=True, stop=True)
                ins.then_inc(scale_spread, 1)

            def rotate(name, src):
                r = ROTS.index(name)
                if r:
                    pe.wait_ge(rot_used, r)
                m = TAB["rotm" if name[1] == "r" else "rotg"]
                pe.matmul(ps[:, 4, :], tab[:, m:m + P], src, start=True, stop=True).then_inc(rotated, 1)

            def mod_columns(key, acc, later=0):
                outp = acquire(key, later)
                for j in range(4):
                    ins = pe.matmul(outp[:, j:j + 1], acc[:, 0, j * P:j * P + P], ones[:, 0:1], start=(j == 0),
                                    stop=True, skip_group_check=True)
                fill(ins, key)

            pe.wait_ge(consts_set, 3)
            pe.wait_ge(silu_done, 1)

            def columns_of(b):
                pe.wait_ge(drained[b], 1)
                for j in range(4 * b, 4 * b + 4):
                    ins = pe.transpose(ps[:, 4, 2 * j:2 * j + 2],
                                       mod_row(b)[:, j % 4 * P:j % 4 * P + P], ident[0:2, 0:2])
                return ins

            for b in ROW_BLOCKS:
                for k in range(KD):
                    if b == 3 and k == 4:
                        for j in range(KD):
                            sum_squares(EV["x0"], j)
                    if b == 0 and k == 0:
                        pe.wait_ge(head_landed[b], 16)
                    if b >= 2 and k % 2 == 0:
                        pe.wait_ge(head_landed[2 + 4 * (b - 2) + k // 2], 16)
                    ins = pe.matmul(ps[0:2, b, :], c_act[:, 2 * k:2 * k + 2],
                                    mod_head[:, 4 * b + k // 2, (k % 2) * BLOCK:(k % 2 + 1) * BLOCK],
                                    start=(k == 0), stop=(k == KD - 1))
                fill(ins, ("row", b))
            pe.wait_ge(ident_landed, 16)
            columns_of(0)
            pe.wait_ge(head_summed, 2 * KD)
            for j in range(4):
                for s in range(2):
                    pe.matmul(ps[:, 4, 8 + 2 * j + s:9 + 2 * j + s], probs[:, s, j * P:j * P + P], ones[:, 0:1],
                              start=True, stop=True)
            columns_of(2)
            spread(EV["x0"])
            fill(columns_of(3), "mod columns x")

            def kept(key):
                bank, use = AT[key]
                pe.wait_ge(drained[bank], use)

            def between(t):
                if t in (1, 2):
                    sum_squares(EV["ckv"], t - 1)
                if t == 3:
                    spread_after(EV["ckv"], t_ready, 2 * KD)
                    pe.wait_ge(tab_landed, 32)
                    kept(("pc", 2))
                    rotate("kr", kr_raw[:, CTX:KEYS])
                if t == 4:
                    sum_squares(EV["kg0"], 0)
                if t == 5:
                    spread_after(EV["kg0"], ckv_scaled, KKV)
                    sum_squares(EV["kg1"], 0)
                if t == 6:
                    pe.wait_ge(knx_ready, 1)
                    rotate("kg0", knx[:])
                    spread_after(EV["kg1"], knx_ready, 1)
                if t == 7:
                    pe.wait_ge(knx_ready, 2)
                    rotate("kg1", knx[:])
                if 8 <= t < 12:
                    sum_squares(EV["cq"], t - 8)
                if 12 <= t < 16:
                    i = t - 12
                    sum_squares(EV[f"gq{i}"], 0)
                    kept(("px", 11 + i))
                    rotate(f"gq{i}", q_raw[:, i % 2, :])

            def spread_after(e, used, count):
                pe.wait_ge(used, count)
                spread(e)

            for t, name in enumerate(PROJ):
                if t in VALUES:
                    half = VALUES.index(t)
                    pe.wait_ge(chunk_done, t + 1)
                    for n in range(TK // 2):
                        outp = bank_of(("vg", n)) if half else acquire(("vg", n))
                        hi, lo, first = (h_hi, h_lo, 2 * n) if 2 * n < TX else (hc_hi, hc_lo, 2 * n - TX)
                        for tt in range(2):
                            cols = slice((first + tt) * P, (first + tt) * P + P)
                            for k in range(KD // 2):
                                ins = product(outp[:, tt * 2 * P:(tt + 1) * 2 * P],
                                              (hi[:, half * KD // 2 + k, cols], lo[:, half * KD // 2 + k, cols]),
                                              weights(t, k * 2 * P, (k + 1) * 2 * P),
                                              half == 0 and tt == 0 and k == 0, half == 1 and k == KD // 2 - 1,
                                              skip_group_check=True)
                        if half:
                            fill(ins, ("vg", n))
                    if half == 0:
                        ins.then_inc(values_half, 1)
                elif t == 0:
                    tile_product(("px", t), t, t, h_hi, h_lo, lambda k: low_ready(pe, 0, k))
                    for j in range(KD):
                        sum_squares(EV["ctx0"], j)
                elif t == 1:
                    tile_product(("px", t), t, t, h_hi, h_lo, lambda k: spread(EV["ctx0"]) if k == KD // 2 else None)
                    outps = [acquire(("pc", c)) for c in range(2)]
                    for k in range(KD):
                        low_ready(pe, 1, k)
                        for c in range(2):
                            ins = product(outps[c][:, 0:CTX], weights(c, k * P, k * P + P),
                                          (hc_hi[:, k, :], hc_lo[:, k, :]), k == 0, k == KD - 1)
                            if k == KD - 1:
                                fill(ins, ("pc", c))
                else:
                    tile_product(("px", t), t, t, h_hi, h_lo)
                    if t < BOTH:
                        tile_product(("pc", t), t, t, hc_hi, hc_lo)
                between(t)

            pe.wait_ge(drained[AT[("px", 10)][0]], AT[("px", 10)][1])
            for n in range(3):
                pe.wait_ge(chunk_done, UQ0 + n + 1)
                for i in range(2):
                    outp = acquire(("uq", n, i))
                    for k in range(KQ):
                        c = (i * KQ + k) * P
                        ins = product(outp, weights(UQ0 + n, c, c + P), (cq_hi[:, k, :], cq_lo[:, k, :]), k == 0,
                                      k == KQ - 1)
                    fill(ins, ("uq", n, i))
                if n == 0:
                    between(15)
            pe.wait_ge(ckv_ready, KKV)
            pe.wait_ge(knx_ready, 2)
            pe.wait_ge(chunk_done, UKK + 1)
            for n in range(2):
                ctx_bank = acquire(("kc", n))
                for h in (2 * n, 2 * n + 1):
                    outp = acquire(("kx", h))
                    for k in range(KKV):
                        c = (h * KKV + k) * P
                        ins = product(outp, weights(UKK, c, c + P), (ckv_hi[:, k, CTX:KEYS], ckv_lo[:, k, CTX:KEYS]),
                                      k == 0, k == KKV - 1)
                    fill(ins, ("kx", h))
                for h in (2 * n, 2 * n + 1):
                    for k in range(KKV):
                        c = (h * KKV + k) * P
                        ins = product(ctx_bank[:, h % 2 * CTX:h % 2 * CTX + CTX], weights(UKK, c, c + P),
                                      (ckv_hi[:, k, 0:CTX], ckv_lo[:, k, 0:CTX]), k == 0, k == KKV - 1)
                fill(ins, ("kc", n))
                kept(("uq", 2, n))
                rotate(f"qr{n}", q_raw[:, n, :])
            pe.wait_ge(chunk_done, UKV + 1)
            for t in range(TK):
                outp = acquire(("v", t))
                cols = slice(t * P, t * P + P)
                for k in range(KKV):
                    ins = product(outp, (ckv_hi[:, k, cols], ckv_lo[:, k, cols]),
                                  weights(UKV, k * BLOCK, (k + 1) * BLOCK), k == 0, k == KKV - 1)
                fill(ins, ("v", t))

            kept(("v", TK - 1))
            pe.wait_ge(rope_split, 3)
            for s in range(4 * HEADS + 3):
                if s < 4 * HEADS:
                    h, qt, pair = s // 4, s % 4, 2 * (s % 2)
                    q_cols = slice(qt * P, qt * P + P)
                    if s >= 2:
                        pe.wait_ge(exp_done, s - 1)
                    for bank, keys in ((pair, slice(CTX, KEYS)), (pair + 1, slice(0, CTX))):
                        outp = ps[:, bank, 0:keys.stop - keys.start]
                        if h < MLA_HEADS:
                            k_low = kn_lo[:, h, :] if bank == pair else kc_lo[:, h, :]
                            product(outp, (qn_hi[:, h, q_cols], qn_lo[:, h, q_cols]), (kn_hi[:, h, keys], k_low), True,
                                    False)
                            pe.matmul(outp, q_rope[:, h, q_cols], kr_hi[:, keys], start=False, stop=False)
                            ins = pe.matmul(outp, q_rope[:, h, q_cols], kr_lo[:, keys], start=False, stop=True)
                        else:
                            g = h - MLA_HEADS
                            ins = pe.matmul(outp, gq[:, g, q_cols], kg[:, g // 2, keys], start=True, stop=True)
                    ins.then_inc(scored, 1)
                if 2 <= s < 4 * HEADS + 2:
                    n = s - 2
                    pe.wait_ge(probs_ready, n + 1)
                    if n:
                        pe.wait_ge(turned_copied, n)
                    for kt in range(TK):
                        ins = pe.transpose(ps[:, 4 + kt // 3, kt % 3 * P:kt % 3 * P + P],
                                           probs[:, n % 3, kt * P:kt * P + P], ident)
                    ins.then_inc(turned, 1)
                if s >= 5 and s % 4 == 1:
                    b = (s - 5) // 4
                    pe.wait_ge(mod_summed, b + 1)
                    mod_columns(("mc0", b), mod_acc0[b % 2])
                h, third = (s - 6) // 4, (s - 6) % 4
                if s >= 6 and third < 3 and h < HEADS and (h < HEADS - 1 or third == 0):
                    outp = bank_of(("pv", h)) if third else acquire(("pv", h))
                    if third == 0:
                        pe.wait_ge(turned_copied, 4 * h + 4)
                    for kt in range(TK // 3 * third, TK // 3 * (third + 1) if h < HEADS - 1 else TK):
                        g = (h - MLA_HEADS) // 2
                        at = (kt + TC) % TK
                        val = vm[:, at, h * P:h * P + P] if h < MLA_HEADS else vg[:, at, g * P:g * P + P]
                        ins = pe.matmul(outp, val, probs_t[:, h % 2, kt, :], start=(kt == 0), stop=(kt == TK - 1))
                    if third == 2 or h == HEADS - 1:
                        fill(ins, ("pv", h))

            pe.wait_ge(exp_done, 4 * HEADS)
            for j in range(KD):
                tile_product(("wo", j), W_WOUT + j, N_WOUT + j, h_hi, h_lo,
                             (lambda k: kept(("pv", k))) if j == 0 else None)
                if j == 2:
                    pe.wait_ge(drained[7], AT[("mc0", 7)][1])
                if j >= 2:
                    sum_squares(EV["x1"], j - 2)
            sum_squares(EV["x1"], KD - 2)
            sum_squares(EV["x1"], KD - 1)
            spread_after(EV["x1"], turned_copied, 4 * HEADS)

            def mod1_columns(b, i):
                pe.wait_ge(mod_summed, KD + b + 1 + 3 * i)
                mod_columns(("mc1", b), mod_acc1[:, b], PER[0][6] * i)

            def mlp(l, i, first=False, last=False):
                n0, w0 = (N_MLP0, W_MLP0) if l == 0 else (N_MLP1, W_MLP1)
                w_at, m_at = mlp_offsets(l)
                per = len(w_at) + len(m_at)
                e = EV["x2" if l == 0 else "x4"]
                if first:
                    first_tiles([("mlp", l, 0), ("mlp", l, 1)], w0, n0, 2 if l == 0 else 4)
                for s in range(2 if first else 0, MLP_W):
                    key = ("mlp", l, s)
                    ready = None
                    if s == KD:
                        def ready(k):
                            pe.wait_ge(hid_ready, l * FFG * KD + k + 1 + KD * i)
                    hi, lo = (h_hi, h_lo) if s < KD else (hid_hi, hid_lo)
                    tile_product(key, w0 + s, n0 + w_at[s], hi, lo, ready, PER[l][s % 4] * i, per * i)
                    if l == 0 and s in (5, 9, 13) and not last:
                        mod1_columns((s - 5) // 4, i)
                    if last and s >= KD + 2:
                        sum_squares(e, s - KD - 2)
                if last:
                    sum_squares(e, KD - 2)
                    sum_squares(e, KD - 1)

            mlp(0, 0, first=True)
            with pe.Fori(1, FFG - 1) as i:
                mlp(0, i)
            mlp(0, FFG - 1, last=True)
            mod1_columns(0, FFG - 1)
            spread(EV["x2"])
            mod1_columns(1, FFG - 1)
            mod1_columns(2, FFG - 1)

            def channel_dft(g):
                kept(("fi", FI.index(f"f{g}")))
                for b in range(2):
                    outp = acquire(("f1", g, b))
                    for t in (2 * b, 2 * b + 1):
                        ins = pe.matmul(outp[:, t % 2 * 2 * P:(t % 2 + 1) * 2 * P], f_t[:, g, t * P:t * P + P],
                                        cs_small[:], start=True, stop=True)
                    fill(ins, ("f1", g, b))

            first_tiles([("fi", 0), ("fi", 1)], W_FC, N_FC, 3)
            for c in range(2, NFI):
                tile_product(("fi", c), W_FC + c, N_FC + c, h_hi, h_lo)
                if c == 8:
                    pe.wait_ge(dft_landed, 32)
                if c >= 9:
                    channel_dft(c - 9)
            channel_dft(GROUPS - 1)

            def token_dft(g):
                outp = acquire(("f2", g))
                kept(("f1", g, 0))
                kept(("f1", g, 1))
                for part in range(2):
                    for t in range(TX):
                        ins = pe.matmul(outp, f_mid[:, t, g, part * P:part * P + P], cs[:, part, t, :],
                                        start=(part == 0 and t == 0), stop=(part == 1 and t == TX - 1))
                fill(ins, ("f2", g))

            token_dft(0)
            token_dft(1)
            outp = acquire("mean")
            taps = KCH * TAPS - sum(POOL_TAPS)
            for i in range(KCH):
                pe.wait_ge(conv_step, taps + i + 1)
                ins = pe.matmul(outp, meanw[:], conv[:, i, :], start=(i == 0), stop=(i == KCH - 1))
            fill(ins, "mean")
            token_dft(2)
            for i in range(KCH):
                sum_squares(EV["ln"], i)
            token_dft(3)
            spread(EV["ln"])

            for half in range(2):
                for j in range(2):
                    outp = bank_of(("fo", j)) if half else acquire(("fo", j))
                    pe.wait_ge(chunk_done, N_FCOUT + j + 1)
                    for k in range(half * GROUPS, half * GROUPS + GROUPS):
                        if j == 0 and k < GROUPS:
                            kept(("f2", k))
                        elif j == 0:
                            pe.wait_ge(mix_ready, k - GROUPS + 1)
                        ins = product(outp, weights(W_FCOUT + j, k * P, k * P + P), (h_hi[:, k, :], h_lo[:, k, :]),
                                      k == 0, k == KD - 1)
                    if half:
                        fill(ins, ("fo", j))
            for j in range(2, KD):
                tile_product(("fo", j), W_FCOUT + j, N_FCOUT + j, h_hi, h_lo)
                if j >= 2:
                    sum_squares(EV["x3"], j - 2)
            sum_squares(EV["x3"], KD - 2)
            sum_squares(EV["x3"], KD - 1)
            spread_after(EV["x3"], y_ready, KCH)
            mlp(1, 0, first=True)
            with pe.Fori(1, FFG - 1) as i:
                mlp(1, i)
            mlp(1, FFG - 1, last=True)
            spread(EV["x4"])


def rope_tables():
    tok = np.arange(SEQ)
    pos = (tok // GRID_W, tok % GRID_W)
    made = []
    for block in (HD // 2, ROPE // 2):
        half = block // 2
        freqs = np.float32(10000.0) ** (-np.arange(half, dtype=np.float32) / np.float32(half))
        cos, sin, rot = np.zeros((P, SEQ), np.float32), np.zeros((P, SEQ), np.float32), np.zeros((P, P), np.float32)
        for d in range(P):
            angle = pos[d // block % 2].astype(np.float32) * freqs[d % half]
            cos[d], sin[d] = np.cos(angle), np.sin(angle)
            if d % block < half:
                rot[d + half, d] = -1.0
            else:
                rot[d - half, d] = 1.0
        made.append((cos, sin, rot))
    (cg, sg, rg), (cm, sm, rm) = made
    return np.concatenate([cg, sg, cm, sm, np.eye(P, dtype=np.float32), rg, rm], axis=1)


def dft_tables():
    def table(n, f):
        k = np.outer(np.arange(n), np.arange(n)) % n
        return f(2 * np.pi * k / n).astype(np.float32)
    big = np.stack([table(SEQ, np.cos), -table(SEQ, np.sin)]).reshape(2, TX, P, SEQ).transpose(2, 0, 1, 3)
    return np.ascontiguousarray(big), np.concatenate([table(P, np.cos), table(P, np.sin)], axis=1)


def columns(a):
    return a.reshape(-1, P).T


def tiles(w):
    k, m = w.shape[0] // P, w.shape[1] // P
    return w.reshape(k, P, m, P).transpose(2, 1, 0, 3).reshape(m, P, k * P)


def mod_blocks(w):
    b = w.shape[1] // BLOCK
    return w.reshape(4, 2, P, b, BLOCK).transpose(3, 0, 2, 1, 4).reshape(b * 4, P, CHUNK)


def lay_out(i):
    w_in, uq, ukv = i["attn_w_in"][0], i["mla_w_uq"][0], i["mla_w_ukv"][0]
    at = np.cumsum([0, Q_RANK, GQA_HEADS * HD, KV_RANK, ROPE, GQA_KV * HD, GQA_KV * HD])
    cq, gq, ckv, kr, kg, vg = (w_in[:, a:b] for a, b in zip(at[:-1], at[1:]))
    v_chunks = vg.reshape(2, KD // 2, P, GQA_KV * HD).transpose(0, 2, 1, 3).reshape(2, P, CHUNK)
    uq = uq.reshape(Q_RANK, MLA_HEADS, NOPE + ROPE)
    uq = np.concatenate([uq[:, :, :NOPE].reshape(Q_RANK, -1), uq[:, :, NOPE:].reshape(Q_RANK, -1)], axis=1)
    ukv = ukv.reshape(KV_RANK, MLA_HEADS, 2 * P)
    uq_chunks = tiles(uq).reshape(3, 2, P, KQ * P).transpose(0, 2, 1, 3).reshape(3, P, CHUNK)
    k_chunk = tiles(ukv[:, :, :NOPE].reshape(KV_RANK, -1)).transpose(1, 0, 2).reshape(1, P, CHUNK)
    v_chunk = ukv[:, :, NOPE:].reshape(KKV, P, MLA_HEADS * P).transpose(1, 0, 2).reshape(1, P, CHUNK)
    fc = i["fc_w_in"][0]
    order = np.concatenate([np.concatenate([np.arange(P) + GATE_AT + g * P, np.arange(P) + CH + g * P])
                            for g in range(KCH)] + [np.arange(CH)])
    vectors = [columns(i["norm1_g"]), columns(i["norm2_g"]), columns(i["final_g"]), columns(i["mod_b"]),
               columns(i["mla_q_norm_g"]), columns(i["mla_kv_norm_g"]), columns(i["gqa_q_norm_g"]),
               columns(i["gqa_k_norm_g"]), columns(i["conv_b"]), columns(i["conv_ln_g"]), columns(i["conv_ln_b"]),
               i["conv_w"][0].reshape(TAPS, KCH, P).transpose(2, 1, 0).reshape(P, -1)]
    mod = [mod_blocks(w) for w in i["mod_w"]]

    def mlp_chunks(l):
        up = tiles(i["mlp_w1"][l])
        down = [tiles(i["mlp_w2"][l][g * D:(g + 1) * D]) for g in range(FFG)]
        return np.concatenate([part for g in range(FFG) for part in (up[g * KD:(g + 1) * KD], down[g])])

    dft, dft_small = dft_tables()
    return [
        np.stack([i["c"][0], i["c_ctx"]]).reshape(2, KD, P).transpose(2, 1, 0).reshape(P, 2 * KD),
        np.concatenate(vectors, axis=1), rope_tables(), dft, dft_small,
        i["x"][0].T.reshape(KD, P, SEQ), i["ctx"][0].T.reshape(KD, P, CTX),
        mod[0][:16], mod[0][16:], mod[1],
        np.concatenate([tiles(np.concatenate([ckv, kr, kr, kg], axis=1)), v_chunks,
                        tiles(np.concatenate([cq, gq], axis=1)), uq_chunks, k_chunk, v_chunk, tiles(i["attn_w_out"][0])]),
        mlp_chunks(0), np.concatenate([tiles(fc[:, order]), tiles(i["fc_w_out"][0])]), mlp_chunks(1),
    ]


def kernel(**inputs):
    import concourse.bacc as bacc
    from concourse.bass_utils import run_bass_kernel_spmd

    nc = bacc.Bacc("TRN2", target_bir_lowering=False, num_devices=1)
    names = ["c_cols", "vectors", "tables", "dft", "dft_small", "x_t", "ctx_t", "mod0_head", "mod0", "mod1", "w_mix0",
             "w_mlp0", "w_fc", "w_mlp1"]
    arrays, args = {}, []
    for name, a in zip(names, lay_out({k: np.asarray(a) for k, a in inputs.items()})):
        arrays[name] = np.ascontiguousarray(a)
        args.append(nc.dram_tensor(name, arrays[name].shape, F32, kind="ExternalInput").ap())
    args.append(nc.dram_tensor("y_t", (KD, P, SEQ), F32, kind="ExternalOutput").ap())
    dit_block_kernel(nc, *args)
    r = run_bass_kernel_spmd(nc, [arrays], core_ids=[0])
    return np.ascontiguousarray(r.results[0]["y_t"].reshape(D, SEQ).T)[None]
```
